# Optimizing a Trainium2 kernel written in Bass

```python
import jax, jax.numpy as jnp
from jax import lax
import numpy as np
import math

D_MODEL = 1024
BATCH = 1
SEQ = 1024
DEPTH = 1

DN_HEADS = 8
DN_HEAD_DIM = 64
DN_WIDTH = DN_HEADS * DN_HEAD_DIM
DN_CONV = 3
DN_CHUNK = 64
ATT_GROUPS = ((128, 1), (512, 4), (2048, 16))
N_GROUPS = 3
ATT_HEADS_PER_GROUP = 8
ATT_HEAD_DIM = 64
ATT_HEADS = N_GROUPS * ATT_HEADS_PER_GROUP
ATT_WIDTH = ATT_HEADS * ATT_HEAD_DIM
ATT_OUT_WIDTH = ATT_HEADS_PER_GROUP * ATT_HEAD_DIM
ATT_BLOCK = 64
ALIBI_MAX = 8.0
D_FF = 2816
FFN_CONV = 3
IN_PROJ_SIZES = (3 * DN_WIDTH, DN_WIDTH, 2 * DN_HEADS, 2 * DN_HEADS,
                 ATT_WIDTH, ATT_WIDTH, ATT_WIDTH, D_MODEL, D_MODEL)
D_IN_PROJ = 3 * DN_WIDTH + DN_WIDTH + 4 * DN_HEADS + 3 * ATT_WIDTH + 2 * D_MODEL
EPS = 1e-6
NEG_INF = -1e30


def rms_norm(x, w):
    xf = x.astype(jnp.float32)
    y = xf * lax.rsqrt(jnp.mean(xf * xf, axis=-1, keepdims=True) + EPS)
    return (y * w.astype(jnp.float32)).astype(x.dtype)

def l2_normalize(t):
    tf = t.astype(jnp.float32)
    return tf * lax.rsqrt(jnp.sum(tf * tf, axis=-1, keepdims=True) + EPS)

def depthwise_conv_centred(x, w):
    width, c = w.shape
    return lax.conv_general_dilated(
        x, w[:, None, :].astype(x.dtype), window_strides=(1,),
        padding=[((width - 1) // 2, width // 2)],
        dimension_numbers=('NWC', 'WIO', 'NWC'), feature_group_count=c)

def alibi_slopes(n):
    return 2.0 ** (-ALIBI_MAX * jnp.arange(1, n + 1, dtype=jnp.float32) / n)

def gated_delta_rule_chunked(q, k, v, g, beta):
    f32 = jnp.float32
    n, h, t, dk = q.shape
    dv = v.shape[-1]
    c = DN_CHUNK
    nc = t // c
    q = q.astype(f32).reshape(n, h, nc, c, dk) * (dk ** -0.5)
    k = k.astype(f32).reshape(n, h, nc, c, dk)
    v = v.astype(f32).reshape(n, h, nc, c, dv)
    beta = beta.astype(f32).reshape(n, h, nc, c)
    g = jnp.cumsum(g.astype(f32).reshape(n, h, nc, c), axis=-1)
    idx = jnp.arange(c)
    incl = idx[:, None] >= idx[None, :]
    strict = idx[:, None] > idx[None, :]
    decay = jnp.exp(jnp.where(incl, g[..., :, None] - g[..., None, :], -jnp.inf))
    kb = k * beta[..., None]
    a_low = jnp.where(strict, jnp.einsum('nhcid,nhcjd->nhcij', kb, k) * decay, 0.0)
    eye = jnp.eye(c, dtype=f32)
    tmat = lax.linalg.triangular_solve(eye + a_low, jnp.broadcast_to(eye, a_low.shape),
                                       left_side=True, lower=True, unit_diagonal=True)
    u = jnp.einsum('nhcij,nhcjv->nhciv', tmat, v * beta[..., None])
    w = jnp.einsum('nhcij,nhcjk->nhcik', tmat, kb * jnp.exp(g)[..., None])
    qk = jnp.einsum('nhcid,nhcjd->nhcij', q, k) * decay
    g_last = g[..., -1]
    q_dec = q * jnp.exp(g)[..., None]
    k_dec = k * jnp.exp(g_last[..., None] - g)[..., None]
    xs = tuple(jnp.moveaxis(arr, 2, 0) for arr in (u, w, qk, q_dec, k_dec, g_last))

    def step(state, inp):
        u_i, w_i, qk_i, qd_i, kd_i, gl_i = inp
        v_new = u_i - jnp.einsum('nhck,nhkv->nhcv', w_i, state)
        o_i = jnp.einsum('nhck,nhkv->nhcv', qd_i, state) + jnp.einsum('nhij,nhjv->nhiv', qk_i, v_new)
        state = state * jnp.exp(gl_i)[..., None, None] + jnp.einsum('nhck,nhcv->nhkv', kd_i, v_new)
        return state, o_i

    _, o = lax.scan(step, jnp.zeros((n, h, dk, dv), f32), xs)
    return jnp.moveaxis(o, 0, 2).reshape(n, h, t, dv)

def dilated_window_attention(q, k, v, slopes, dilation, radius):
    b, s, h, dh = q.shape
    blk = ATT_BLOCK
    sub = s // dilation
    nb = -(-sub // blk)
    lp = nb * blk

    def to_sub(a):
        return a.reshape(b, sub, dilation, h, dh).transpose(0, 2, 3, 1, 4)

    qs = jnp.pad(to_sub(q), ((0, 0),) * 3 + ((0, lp - sub), (0, 0))).reshape(b, dilation, h, nb, blk, dh)

    def windows(a):
        ap = jnp.pad(to_sub(a), ((0, 0),) * 3 + ((blk, lp - sub + blk), (0, 0)))
        ap = ap.reshape(b, dilation, h, nb + 2, blk, dh)
        return jnp.concatenate([ap[:, :, :, 0:nb], ap[:, :, :, 1:nb + 1], ap[:, :, :, 2:nb + 2]], axis=-2)

    kw, vw = windows(k), windows(v)
    blocks = jnp.arange(nb)[:, None, None]
    qi = blocks * blk + jnp.arange(blk)[None, :, None]
    kj = (blocks - 1) * blk + jnp.arange(3 * blk)[None, None, :]
    rel = jnp.abs(qi - kj)
    valid = (rel <= radius) & (kj >= 0) & (kj < sub)
    scores = jnp.einsum('bdhnqe,bdhnke->bdhnqk', qs, kw) * (dh ** -0.5)
    scores = scores - slopes[:, None, None, None] * (rel * dilation).astype(jnp.float32)
    scores = jnp.where(valid, scores, NEG_INF)
    m = jnp.max(scores, axis=-1, keepdims=True)
    lse = m + jnp.log(jnp.sum(jnp.exp(scores - m), axis=-1, keepdims=True))
    o = jnp.einsum('bdhnqk,bdhnke->bdhnqe', jnp.exp(scores - lse), vw)
    o = o.reshape(b, dilation, h, lp, dh)[:, :, :, :sub].transpose(0, 3, 1, 2, 4).reshape(b, s, h, dh)
    lse = lse.reshape(b, dilation, h, lp)[..., :sub].transpose(0, 3, 1, 2).reshape(b, s, h)
    return o, lse

def hybrid_block(x, norm1_w, w_in, dn_conv_w, dn_a_log, dn_dt_bias, dn_out_norm_w,
                 attn_q_norm_w, attn_k_norm_w, w_dn_out, w_attn_out, w_o,
                 norm2_w, w_ffn_up, ffn_conv_w, w_ffn_down):
    f32 = jnp.float32
    b, s, _ = x.shape
    h = rms_norm(x, norm1_w)
    proj = h @ w_in
    points = np.cumsum(np.array(IN_PROJ_SIZES))[:-1].tolist()
    qkv_a, z_a, a_in, b_in, q_b, k_b, v_b, gate_a, gate_b = jnp.split(proj, points, axis=-1)

    qkv_a = jax.nn.silu(depthwise_conv_centred(qkv_a, dn_conv_w))
    q_a, k_a, v_a = [t.reshape(b, s, DN_HEADS, DN_HEAD_DIM).transpose(0, 2, 1, 3)
                     for t in jnp.split(qkv_a, 3, axis=-1)]
    q_a, k_a = l2_normalize(q_a), l2_normalize(k_a)
    a_dir = a_in.astype(f32).reshape(b, s, 2, DN_HEADS)
    beta = jax.nn.sigmoid(b_in.astype(f32).reshape(b, s, 2, DN_HEADS))
    g = -jnp.exp(dn_a_log.astype(f32)) * jax.nn.softplus(a_dir + dn_dt_bias.astype(f32))
    g = g.transpose(2, 0, 3, 1)
    beta = beta.transpose(2, 0, 3, 1)
    both = lambda t: jnp.concatenate([t, jnp.flip(t, axis=2)], axis=0)
    o2 = gated_delta_rule_chunked(both(q_a), both(k_a), both(v_a),
                                  jnp.concatenate([g[0], jnp.flip(g[1], axis=2)], axis=0),
                                  jnp.concatenate([beta[0], jnp.flip(beta[1], axis=2)], axis=0))
    o_a = (o2[:b] + jnp.flip(o2[b:], axis=2)).transpose(0, 2, 1, 3)
    z = z_a.astype(f32).reshape(b, s, DN_HEADS, DN_HEAD_DIM)
    o_a = rms_norm(o_a, dn_out_norm_w) * jax.nn.silu(z)
    y_a = o_a.reshape(b, s, DN_WIDTH).astype(x.dtype) @ w_dn_out

    heads = lambda t: t.astype(f32).reshape(b, s, N_GROUPS, ATT_HEADS_PER_GROUP, ATT_HEAD_DIM)
    q_b = rms_norm(heads(q_b), attn_q_norm_w)
    k_b = rms_norm(heads(k_b), attn_k_norm_w)
    v_b = heads(v_b)
    slopes = alibi_slopes(ATT_HEADS).reshape(N_GROUPS, ATT_HEADS_PER_GROUP)
    outs, lses = [], []
    for gi, (window, dil) in enumerate(ATT_GROUPS):
        o_g, l_g = dilated_window_attention(q_b[:, :, gi], k_b[:, :, gi], v_b[:, :, gi],
                                            slopes[gi], dil, window // (2 * dil))
        outs.append(o_g)
        lses.append(l_g)
    wts = jax.nn.softmax(jnp.stack(lses), axis=0)
    o_b = jnp.einsum('gbsh,gbshe->bshe', wts, jnp.stack(outs))
    y_b = o_b.reshape(b, s, ATT_OUT_WIDTH).astype(x.dtype) @ w_attn_out

    mixed = jax.nn.sigmoid(gate_a) * y_a + jax.nn.sigmoid(gate_b) * y_b
    x = x + mixed @ w_o

    h2 = rms_norm(x, norm2_w)
    gate, up = jnp.split(depthwise_conv_centred(h2 @ w_ffn_up, ffn_conv_w), 2, axis=-1)
    return x + (jax.nn.silu(gate) * up) @ w_ffn_down

def first_inputs(seed: int = 0) -> dict:
    key = jax.random.key(seed)
    ks = jax.random.split(key, 17)
    f32 = jnp.float32
    normal = lambda k, shape, scale: jax.random.normal(k, shape, f32) * scale
    dt = jnp.exp(jax.random.uniform(ks[5], (DEPTH, 2, DN_HEADS), f32, np.log(1e-3), np.log(1e-1)))
    return {
        "x": normal(ks[0], (BATCH, SEQ, D_MODEL), 1.0),
        "norm1_w": 1.0 + normal(ks[1], (DEPTH, D_MODEL), 0.05),
        "w_in": normal(ks[2], (DEPTH, D_MODEL, D_IN_PROJ), D_MODEL ** -0.5),
        "dn_conv_w": normal(ks[3], (DEPTH, DN_CONV, 3 * DN_WIDTH), DN_CONV ** -0.5),
        "dn_a_log": jnp.log(jax.random.uniform(ks[4], (DEPTH, 2, DN_HEADS), f32, 1.0, 16.0)),
        "dn_dt_bias": dt + jnp.log(-jnp.expm1(-dt)),
        "dn_out_norm_w": 1.0 + normal(ks[6], (DEPTH, DN_HEAD_DIM), 0.05),
        "attn_q_norm_w": 1.0 + normal(ks[7], (DEPTH, ATT_HEAD_DIM), 0.05),
        "attn_k_norm_w": 1.0 + normal(ks[8], (DEPTH, ATT_HEAD_DIM), 0.05),
        "w_dn_out": normal(ks[9], (DEPTH, DN_WIDTH, D_MODEL), DN_WIDTH ** -0.5),
        "w_attn_out": normal(ks[10], (DEPTH, ATT_OUT_WIDTH, D_MODEL), ATT_OUT_WIDTH ** -0.5),
        "w_o": normal(ks[11], (DEPTH, D_MODEL, D_MODEL), D_MODEL ** -0.5),
        "norm2_w": 1.0 + normal(ks[12], (DEPTH, D_MODEL), 0.05),
        "w_ffn_up": normal(ks[13], (DEPTH, D_MODEL, 2 * D_FF), D_MODEL ** -0.5),
        "ffn_conv_w": normal(ks[14], (DEPTH, FFN_CONV, 2 * D_FF), FFN_CONV ** -0.5),
        "w_ffn_down": normal(ks[15], (DEPTH, D_FF, D_MODEL), D_FF ** -0.5),
    }

def first_block(x, norm1_w, w_in, dn_conv_w, dn_a_log, dn_dt_bias, dn_out_norm_w,
              attn_q_norm_w, attn_k_norm_w, w_dn_out, w_attn_out, w_o,
              norm2_w, w_ffn_up, ffn_conv_w, w_ffn_down):
    for layer in range(DEPTH):
        x = hybrid_block(x, norm1_w[layer], w_in[layer], dn_conv_w[layer], dn_a_log[layer],
                         dn_dt_bias[layer], dn_out_norm_w[layer], attn_q_norm_w[layer],
                         attn_k_norm_w[layer], w_dn_out[layer], w_attn_out[layer], w_o[layer],
                         norm2_w[layer], w_ffn_up[layer], ffn_conv_w[layer], w_ffn_down[layer])
    return x


PLE_DIM = 256
NORM_EPS = 1e-6
S5_WIDTH = 512
S5_GROUP = 16
S5_GROUPS = S5_WIDTH // S5_GROUP
S5_STATE = 64
S5_DT_MIN = 1e-3
S5_DT_MAX = 1e-1
LRU_WIDTH = 1280
LRU_HEADS = 10
LRU_HEAD_DIM = LRU_WIDTH // LRU_HEADS
LRU_C = 8.0
CONV_WIDTH = 4
IN_SPLITS = (
    S5_WIDTH,
    2 * S5_WIDTH,
    2 * S5_WIDTH + LRU_WIDTH,
    2 * S5_WIDTH + 2 * LRU_WIDTH,
    2 * S5_WIDTH + 2 * LRU_WIDTH + D_MODEL,
)
IN_COLS = 2 * S5_WIDTH + 2 * LRU_WIDTH + 2 * D_MODEL


def rms_norm_2(x, g):
    xf = x.astype(jnp.float32)
    y = xf * lax.rsqrt(jnp.mean(xf * xf, axis=-1, keepdims=True) + NORM_EPS)
    return (y * g.astype(jnp.float32)).astype(x.dtype)

def _linear_combine(e1, e2):
    a1, b1 = e1
    a2, b2 = e2
    return (a1 * a2, a2 * b1 + b2)

def s5_ssm(u, a_re, a_im, log_dt, b_re, b_im, c_re, c_im, d_skip):
    f32 = jnp.float32
    bsz, seqlen, _ = u.shape
    uf = u.astype(f32)
    ug = uf.reshape(bsz, seqlen, S5_GROUPS, S5_GROUP)
    lam = lax.complex(a_re.astype(f32), a_im.astype(f32))
    dt = jnp.exp(log_dt.astype(f32))[:, None]
    a_bar = jnp.exp(lam * dt)
    zoh = (a_bar - 1.0) / lam
    b = lax.complex(b_re.astype(f32), b_im.astype(f32))
    b_bar = zoh[..., None] * b
    bu = lax.complex(jnp.einsum('blgc,gnc->lbgn', ug, jnp.real(b_bar)),
                     jnp.einsum('blgc,gnc->lbgn', ug, jnp.imag(b_bar)))
    a_seq = jnp.broadcast_to(a_bar[None, None], (seqlen, 1, S5_GROUPS, S5_STATE))
    _, states = lax.associative_scan(_linear_combine, (a_seq, bu), axis=0)
    y = (jnp.einsum('lbgn,gcn->blgc', jnp.real(states), c_re.astype(f32))
         - jnp.einsum('lbgn,gcn->blgc', jnp.imag(states), c_im.astype(f32)))
    y = y.reshape(bsz, seqlen, S5_WIDTH) + d_skip.astype(f32) * uf
    return y.astype(u.dtype)

def causal_depthwise_conv(x, w, b):
    y = lax.conv_general_dilated(
        x, w[:, None, :].astype(x.dtype), window_strides=(1,),
        padding=[(CONV_WIDTH - 1, 0)],
        dimension_numbers=('NWC', 'WIO', 'NWC'),
        feature_group_count=x.shape[-1])
    return y + b

def rg_lru(x, w_a, b_a, w_x, b_x, lam):
    f32 = jnp.float32
    bsz, seqlen, _ = x.shape
    xf = x.astype(f32)
    xh = xf.reshape(bsz, seqlen, LRU_HEADS, LRU_HEAD_DIM)
    r = jax.nn.sigmoid(jnp.einsum('blhi,hij->blhj', xh, w_a.astype(f32)).reshape(bsz, seqlen, LRU_WIDTH)
                       + b_a.astype(f32))
    i = jax.nn.sigmoid(jnp.einsum('blhi,hij->blhj', xh, w_x.astype(f32)).reshape(bsz, seqlen, LRU_WIDTH)
                       + b_x.astype(f32))
    log_a = -LRU_C * r * jax.nn.softplus(-lam.astype(f32))
    a = jnp.exp(log_a)
    mult = jnp.sqrt(-jnp.expm1(2.0 * log_a))
    _, h = lax.associative_scan(_linear_combine, (a, mult * (i * xf)), axis=1)
    return h.astype(x.dtype)

def second_inputs(seed: int = 0) -> dict:
    key = jax.random.key(seed)
    ks = jax.random.split(key, 32)
    f32 = jnp.float32

    def nrm(k, shape, scale):
        return jax.random.normal(k, shape, f32) * scale

    L, D, G, N, C, HD = DEPTH, D_MODEL, S5_GROUPS, S5_STATE, S5_GROUP, LRU_HEAD_DIM
    x = nrm(ks[0], (BATCH, SEQ, D), 1.0)
    p = nrm(ks[1], (DEPTH, BATCH, SEQ, PLE_DIM), 1.0)
    g_pre = 1.0 + nrm(ks[2], (L, D), 0.05)
    w_in = nrm(ks[3], (L, D, IN_COLS), D ** -0.5)
    s5_a_re = -0.5 + nrm(ks[4], (L, G, N), 0.01)
    s5_a_im = math.pi * jnp.arange(N, dtype=f32)[None, None, :] + nrm(ks[5], (L, G, N), 0.01)
    s5_log_dt = jax.random.uniform(ks[6], (L, G), f32, math.log(S5_DT_MIN), math.log(S5_DT_MAX))
    s5_b_re = nrm(ks[7], (L, G, N, C), C ** -0.5)
    s5_b_im = nrm(ks[8], (L, G, N, C), C ** -0.5)
    s5_c_re = nrm(ks[9], (L, G, C, N), N ** -0.5)
    s5_c_im = nrm(ks[10], (L, G, C, N), N ** -0.5)
    s5_d = nrm(ks[11], (L, S5_WIDTH), 1.0)
    w_glu = nrm(ks[12], (L, S5_WIDTH, 2 * S5_WIDTH), S5_WIDTH ** -0.5)
    w_bs = nrm(ks[13], (L, S5_WIDTH, D), S5_WIDTH ** -0.5)
    conv_w = nrm(ks[14], (L, CONV_WIDTH, LRU_WIDTH), CONV_WIDTH ** -0.5)
    conv_b = nrm(ks[15], (L, LRU_WIDTH), 0.01)
    lru_w_a = nrm(ks[16], (L, LRU_HEADS, HD, HD), HD ** -0.5)
    lru_b_a = nrm(ks[17], (L, LRU_WIDTH), 0.01)
    lru_w_x = nrm(ks[18], (L, LRU_HEADS, HD, HD), HD ** -0.5)
    lru_b_x = nrm(ks[19], (L, LRU_WIDTH), 0.01)
    a_c = jax.random.uniform(ks[20], (L, LRU_WIDTH), f32, 0.9, 0.999)
    sig = a_c ** (1.0 / LRU_C)
    lru_lambda = jnp.log(sig) - jnp.log1p(-sig)
    w_bl = nrm(ks[21], (L, LRU_WIDTH, D), LRU_WIDTH ** -0.5)
    w_out = nrm(ks[22], (L, D, D), D ** -0.5)
    g_post = 1.0 + nrm(ks[23], (L, D), 0.05)
    w_ple = nrm(ks[24], (L, PLE_DIM, D), PLE_DIM ** -0.5)
    w_ple_gate = nrm(ks[25], (L, D, D), D ** -0.5)
    return {
        'x': x, 'p': p, 'g_pre': g_pre, 'w_in': w_in,
        's5_a_re': s5_a_re, 's5_a_im': s5_a_im, 's5_log_dt': s5_log_dt,
        's5_b_re': s5_b_re, 's5_b_im': s5_b_im, 's5_c_re': s5_c_re, 's5_c_im': s5_c_im,
        's5_d': s5_d, 'w_glu': w_glu, 'w_bs': w_bs,
        'conv_w': conv_w, 'conv_b': conv_b,
        'lru_w_a': lru_w_a, 'lru_b_a': lru_b_a, 'lru_w_x': lru_w_x, 'lru_b_x': lru_b_x,
        'lru_lambda': lru_lambda, 'w_bl': w_bl, 'w_out': w_out, 'g_post': g_post,
        'w_ple': w_ple, 'w_ple_gate': w_ple_gate,
    }

def second_block(x, p, g_pre, w_in, s5_a_re, s5_a_im, s5_log_dt, s5_b_re, s5_b_im,
              s5_c_re, s5_c_im, s5_d, w_glu, w_bs, conv_w, conv_b,
              lru_w_a, lru_b_a, lru_w_x, lru_b_x, lru_lambda, w_bl, w_out, g_post,
              w_ple, w_ple_gate):
    for i in range(DEPTH):
        h = rms_norm_2(x, g_pre[i])
        proj = h @ w_in[i]
        s5_x, s5_g, lru_x, lru_g, gate_s, gate_l = jnp.split(proj, IN_SPLITS, axis=-1)

        y_s = s5_ssm(s5_x, s5_a_re[i], s5_a_im[i], s5_log_dt[i], s5_b_re[i], s5_b_im[i],
                     s5_c_re[i], s5_c_im[i], s5_d[i])
        glu_a, glu_b = jnp.split(jax.nn.gelu(y_s) @ w_glu[i], 2, axis=-1)
        y_s = glu_a * jax.nn.sigmoid(glu_b) * jax.nn.silu(s5_g)
        z_s = y_s @ w_bs[i]

        c = causal_depthwise_conv(lru_x, conv_w[i], conv_b[i])
        y_l = rg_lru(c, lru_w_a[i], lru_b_a[i], lru_w_x[i], lru_b_x[i], lru_lambda[i])
        z_l = (y_l * jax.nn.silu(lru_g)) @ w_bl[i]

        merged = jax.nn.sigmoid(gate_s) * z_s + jax.nn.sigmoid(gate_l) * z_l
        x = x + rms_norm_2(merged @ w_out[i], g_post[i])

        x = x + (p[i] @ w_ple[i]) * jax.nn.sigmoid(x @ w_ple_gate[i])
    return x


def setup_inputs(seed=0):
    out = dict(first_inputs(seed))
    for name, value in second_inputs(seed + 1).items():
        if name != "x":
            out[name + "_2"] = value
    return out


def reference(
    x, norm1_w, w_in, dn_conv_w, dn_a_log, dn_dt_bias, dn_out_norm_w, attn_q_norm_w,
    attn_k_norm_w, w_dn_out, w_attn_out, w_o, norm2_w, w_ffn_up, ffn_conv_w, w_ffn_down, p_2,
    g_pre_2, w_in_2, s5_a_re_2, s5_a_im_2, s5_log_dt_2, s5_b_re_2, s5_b_im_2, s5_c_re_2,
    s5_c_im_2, s5_d_2, w_glu_2, w_bs_2, conv_w_2, conv_b_2, lru_w_a_2, lru_b_a_2, lru_w_x_2,
    lru_b_x_2, lru_lambda_2, w_bl_2, w_out_2, g_post_2, w_ple_2, w_ple_gate_2,
):
    x = first_block(
        x, norm1_w, w_in, dn_conv_w, dn_a_log, dn_dt_bias, dn_out_norm_w, attn_q_norm_w,
        attn_k_norm_w, w_dn_out, w_attn_out, w_o, norm2_w, w_ffn_up, ffn_conv_w, w_ffn_down,
    )
    return second_block(
        x, p_2, g_pre_2, w_in_2, s5_a_re_2, s5_a_im_2, s5_log_dt_2, s5_b_re_2, s5_b_im_2,
        s5_c_re_2, s5_c_im_2, s5_d_2, w_glu_2, w_bs_2, conv_w_2, conv_b_2, lru_w_a_2, lru_b_a_2,
        lru_w_x_2, lru_b_x_2, lru_lambda_2, w_bl_2, w_out_2, g_post_2, w_ple_2, w_ple_gate_2,
    )


_drawn_inputs = setup_inputs


def setup_inputs(seed=0):
    import zlib

    import numpy as np

    out = dict(_drawn_inputs(seed))
    spreads = {}
    factors = {'attn_q_norm_w': 8.0,
     'attn_k_norm_w': 8.0,
     's5_a_re_2': 200.0,
     'lru_b_a_2': 50.268,
     'lru_b_x_2': 30.011,
     's5_a_im_2': 36.632,
     's5_log_dt_2': 39.192,
     's5_b_re_2': 49.44,
     's5_b_im_2': 50.256,
     's5_c_re_2': 50.496,
     's5_c_im_2': 49.784}
    for name, (base, spread) in spreads.items():
        noise = np.random.default_rng([zlib.crc32(name.encode()), seed]).standard_normal(out[name].shape)
        drawn = base * np.exp(spread * noise) if base else spread * noise
        out[name] = __import__('jax').numpy.asarray(drawn.astype(out[name].dtype))
    for name, factor in factors.items():
        out[name] = (out[name] * factor).astype(out[name].dtype)
    return out
```

```python
from contextlib import ExitStack

import numpy as np
import concourse.bass as bass
from concourse import mybir

F32 = mybir.dt.float32
F32R = mybir.dt.float32r
ALU = mybir.AluOpType
ACT = mybir.ActivationFunctionType
AXX = mybir.AxisListType.X
ds = bass.ds

P = 128
T = 1024
H = T // 2
D = 1024
KD = D // P
EPS = 1e-6
NEG = -1e30
NPAIR = 4
NG = 3
NT = 8
FT = 22
KB = 1024

DENSE = [
    ("attn", NPAIR, [8] * 9),
    ("mixb", 8, [8, 4]),
    ("dnab", 1, [8]),
    ("dn", NPAIR, [8] * 4),
    ("mixa", 8, [8, 4]),
    ("wo", 4, [8, 8]),
    ("ffn0", 1, [8] * 4),
    ("ffn", FT // 2 - 1, [8] * 2 + [2] * 8 + [8] * 2),
    ("ffn1", 1, [2] * 8),
    ("s5x", 2, [8, 8]),
    ("s5g", 2, [8, 8]),
    ("glu", 4, [4, 4]),
    ("mixs", 8, [8, 4]),
    ("lru", 5, [8, 1, 1, 8] * 2 + [2] * 8),
    ("gatel", 4, [8, 8]),
    ("wout", 4, [8, 8]),
    ("ple", 8, [2, 8]),
]


class Block:

    def __init__(self, name, it, pos):
        n0, loads0, last = 0, [0, 0], 1
        for other, count, tiles in DENSE:
            if other == name:
                break
            for i in range(len(tiles)):
                loads0[i % 2] += count
            n0 += count * len(tiles)
            last = (len(tiles) - 1) % 2
        self.kt = tiles[pos]
        self.slot = pos % 2
        body = len(tiles)
        per = len([i for i in range(body) if i % 2 == self.slot])
        upto = len([i for i in range(pos + 1) if i % 2 == self.slot])
        self.n = it * body + (n0 + pos)
        self.loads = it * per + (loads0[self.slot] + upto)
        odd = (body % 2 == 1 and count > 1) or last == 0
        self.dist = 1 if pos == 0 and odd else 2
        self.row = it * body + pos

    def before(self):
        return self.n - self.dist + 1


def last_block(name):
    n = 0
    for other, count, tiles in DENSE:
        n += count * len(tiles)
        if other == name:
            return n


def att_tokens(g, t):
    if g == 0:
        return lambda a: a[:, P * t:P * t + P]
    if g == 1:
        return lambda a: a.rearrange("p (s d) -> p d s", d=4)[:, t // 2, P * (t % 2):P * (t % 2) + P]
    return lambda a: a.rearrange("p (s d) -> p d s", d=8)[:, t, :]


def att_keys(g, t):
    if g == 0:
        a, b = max(P * t - 64, 0), min(P * t + 192, T)
        return (lambda x: x[:, a:b]), b - a, (64 if t == 0 else 0), [
            (t, 64 if t == 0 else P), (t + 1, 64 if t == 7 else P)]
    if g == 1:
        r, half = t // 2, t % 2
        return (lambda x: x.rearrange("p (s d) -> p d s", d=4)[:, r, 64 * half:64 * half + 192]), 192, \
            (0 if half else 64), [(3 * r + half, P if half else 64), (3 * r + half + 1, 64 if half else P)]
    return att_tokens(2, t), P, 0, [(t, P)]


def att_chunk(g, c):
    if g == 0:
        a, b = max(P * c - 64, 0), min(P * c + 64, T)
        return (lambda x: x[:, a:b]), b - a
    if g == 1:
        r, i = c // 3, c % 3
        a, b = [(0, 64), (64, 192), (192, 256)][i]
        return (lambda x: x.rearrange("p (s d) -> p d s", d=4)[:, r, a:b]), b - a
    return att_tokens(2, c), P


CHUNKS = [9, 12, 8]
VBATCH = [3, 3, 2]
VB0 = [0, 3, 6]
VBP = 8


COLS = {}
_at = 0
for _name, _n in [("norm1", 8), ("norm2", 8), ("gpre", 8), ("gpost", 8), ("qn", 1), ("kn", 1), ("dnw", 1),
                  ("dtb", 1), ("alog", 1), ("dnconv", 3 * 12), ("ffnconv", 3 * 44), ("lruconv", 4 * 10),
                  ("convb", 10), ("ba", 10), ("bx", 10), ("lam", 10)]:
    COLS[_name] = _at
    _at += _n
NCOLS = _at

CST = {}
_at = 0
for _name, _n in [("ident", P), ("ones", P), ("blk", P), ("tri", 2 * P), ("mpos", 2 * P), ("mneg", 2 * P),
                  ("slopes", 24)]:
    CST[_name] = (_at, _n)
    _at += _n
NCST = _at


def constants():
    i, j = np.arange(P)[:, None], np.arange(P)[None, :]
    c = np.zeros((P, NCST), np.float32)

    def put(name, a):
        c[:a.shape[0], CST[name][0]:CST[name][0] + a.shape[1]] = a

    put("ident", (i == j) * 1.0)
    put("ones", np.ones((P, P)))
    put("blk", (i // 64 == j // 64) * 1.0)
    put("tri", np.concatenate([(i <= j) * 1.0, (i >= j) * 1.0], 1))
    put("mpos", np.concatenate([np.where(i > j, 0, -NEG), np.where(i < j, 0, -NEG)], 1))
    put("mneg", np.concatenate([np.where(i <= j, 0, NEG), np.where(i >= j, 0, NEG)], 1))
    slopes = 2.0 ** (-8.0 * np.arange(1, 25) / 24)
    dil = np.repeat([1, 4, 16], 8)
    put("slopes", np.tile((8.0 * slopes * dil)[None], (P, 1)))
    k = np.arange(256)[None, :]
    rel = np.abs(i + 64 - k)
    bias = np.where(rel <= 64, -rel, NEG).astype(np.float32)
    same = (i % 2) == (j % 2)
    bias16 = np.where(same, -np.abs(i // 2 - j // 2), NEG).astype(np.float32)
    levels = np.zeros((P, 7, 2, P), np.float32)
    for l in range(7):
        b = 2 ** l
        low = (i // (2 * b) == j // (2 * b)) & (i // b % 2 == 1) & (j // b % 2 == 0)
        levels[:, l, 0], levels[:, l, 1] = low, low.T
    sel = np.zeros((8, NPAIR, P), np.float32)
    for p in range(NPAIR):
        for h in range(2):
            sel[2 * p + h, p, 64 * h:64 * h + 64] = 1
    return c, np.concatenate([bias, bias16], 1).astype(np.float32), levels, sel


def program(nc, a, out):
    with ExitStack() as ctx:
        def sem(name):
            return ctx.enter_context(nc.semaphore(name))

        first = []

        def once(name):
            first.append(nc.alloc_semaphore(name))
            return first[-1]

        slab = ctx.enter_context(nc.sbuf_tensor("slab", [P, 207 * KB // 4], F32))
        base = nc.lookup_mloc(slab).addr

        def at(name, kb, shape, dt=F32):
            assert kb * KB + int(np.prod(shape[1:])) * 4 <= 207 * KB, name
            return nc.alloc_sbuf_tensor_at(name, shape, dt, offset=base + int(kb * KB))

        XH = at("XH", 0, [P, KD, T], F32R)
        XL = at("XL", 32, [P, KD, T], F32R)
        XR = at("XR", 64, [P, KD, T])
        MX = at("MX", 96, [P, KD, T])
        WRAW = [at(f"WRAW{i}", 128 + 4 * i, [P, 8, P]) for i in range(2)]
        WH = [at(f"WH{i}", 136 + 4 * i, [P, 8, P], F32R) for i in range(2)]
        WL = [at(f"WL{i}", 144 + 4 * i, [P, 8, P], F32R) for i in range(2)]
        COL = at("COL", 152, [P, NCOLS])
        CON = at("CON", 154, [P, NCST])
        S0 = 159

        def con(name, i=0, n=None):
            o, size = CST[name]
            n = n or size
            return CON[:, o + i * n:o + (i + 1) * n]

        def col(name, i=0):
            return COL[:, COLS[name] + i:COLS[name] + i + 1]

        IDENT, ONES, BLK = con("ident"), con("ones"), con("blk")

        DP = [ctx.enter_context(nc.psum_tensor(f"DP{i}", [P, T], F32)) for i in range(2)]
        B45 = ctx.enter_context(nc.psum_tensor("B45", [P, T], F32))
        B67 = ctx.enter_context(nc.psum_tensor("B67", [P, T], F32))

        w_loaded = [sem("w_loaded0"), sem("w_loaded1")]
        w_hi = sem("w_hi")
        w_split = sem("w_split")
        mm_done = sem("mm_done")
        psum_free = [sem("psum_free0"), sem("psum_free1")]

        con_in = sem("con_in")
        x_in = sem("x_in")
        sq_ready, sq_used, rs_sqrt, rs_ready = (sem(n) for n in ("sq_ready", "sq_used", "rs_sqrt", "rs_ready"))
        nt_ready, nt_used, xh_ready, xl_ready = (sem(n) for n in ("nt_ready", "nt_used", "xh_ready", "xl_ready"))

        passed = {"pe": sem("pe_passed"), "pool": sem("pool_passed")}

        def gate(e, name):
            e.sem_inc(passed[name], 1)

        def load(sp, b, src, row=None):
            sp.wait_ge(w_split, b.before())
            s = src[ds(b.row if row is None else row, 1)].rearrange("a p n -> (a p) n")
            sp.dma_start(WRAW[b.slot][:, 0:b.kt, :].rearrange("p a n -> p (a n)"), s).then_inc(w_loaded[b.slot], 16)

        def split(pool, b):
            pool.wait_ge(w_loaded[b.slot], b.loads * 16)
            pool.wait_ge(mm_done, b.before())
            gate(pool, "pool")
            pool.tensor_copy(WH[b.slot][:, 0:b.kt, :], WRAW[b.slot][:, 0:b.kt, :]).then_inc(w_hi, 1)
            pool.wait_ge(w_hi, b.n + 1)
            pool.tensor_tensor(WL[b.slot][:, 0:b.kt, :], WRAW[b.slot][:, 0:b.kt, :],
                               WH[b.slot][:, 0:b.kt, :].bitcast(F32), ALU.subtract).then_inc(w_split, 1)

        def freed(e, b):
            e.wait_ge(psum_free[b.slot], b.loads)

        def product(pe, b, hi, lo):
            pe.wait_ge(w_split, b.n + 1)
            pe.wait_ge(psum_free[b.slot], b.loads - 1)
            for k in range(b.kt):
                for w, x, one, end in ((WH, hi, k == 0, False), (WH, lo, False, False),
                                       (WL, hi, False, k == b.kt - 1)):
                    for half in range(2):
                        mm = pe.matmul(DP[b.slot][:, half * H:half * H + H], w[b.slot][:, k, :],
                                       x[:, k, half * H:half * H + H], start=one, stop=end)
            mm.then_inc(mm_done, 1)

        SQ = [at(f"SQ{i}", S0 + 4 * i, [P, T]) for i in range(2)]
        RS = at("RS", S0 + 8, [P, T])
        NTL = [at(f"NTL{i}", S0 + 12 + 4 * i, [P, T]) for i in range(2)]

        class NormCount:
            def __init__(self):
                self.sq, self.ss, self.nt = 0, 0, 0

        def norm_act(act, c, src):
            for k in range(KD):
                if c.sq + k >= 2:
                    act.wait_ge(sq_used, c.sq + k - 1)
                act.activation(SQ[k % 2][:, :], src[:, k, :], ACT.Square).then_inc(sq_ready, 1)
            act.wait_ge(sq_used, c.sq + KD)
            act.activation(RS[:, :], B67[:, :], ACT.Sqrt, scale=1.0 / D, bias=EPS).then_inc(rs_sqrt, 1)
            for k in range(KD):
                act.wait_ge(nt_ready, c.nt + k + 1)
                act.activation(XH[:, k, :], NTL[k % 2][:, :], ACT.Copy).then_inc(xh_ready, 1)

        def norm_pe(pe, c):
            for k in range(KD):
                pe.wait_ge(sq_ready, c.nt + k + 1)
                for half in range(2):
                    mm = pe.matmul(B67[:, half * H:half * H + H], ONES, SQ[k % 2][:, half * H:half * H + H],
                                   start=(k == 0), stop=(k == KD - 1))
                mm.then_inc(sq_used, 1)

        def norm_dve(dve, c, src, w):
            dve.wait_ge(rs_sqrt, c.ss + 1)
            dve.reciprocal(RS[:, :], RS[:, :]).then_inc(rs_ready, 1)
            dve.wait_ge(rs_ready, c.ss + 1)
            for k in range(KD):
                if c.nt + k >= 2:
                    dve.wait_ge(nt_used, c.nt + k - 1)
                dve.scalar_tensor_tensor(out=NTL[k % 2][:, :], in0=src[:, k, :], scalar=col(w, k), in1=RS[:, :],
                                         op0=ALU.mult, op1=ALU.mult).then_inc(nt_ready, 1)

        def norm_pool(pool, c):
            for k in range(KD):
                pool.wait_ge(xh_ready, c.nt + k + 1)
                pool.tensor_tensor(XL[:, k, :], NTL[k % 2][:, :], XH[:, k, :].bitcast(F32),
                                   ALU.subtract).then_inc(nt_used, 1)

        OG = [at(f"OG{g}", 64 + 16 * g, [P, NPAIR, T]) for g in range(NG)]
        QR, KR, VR = (at(n, S0 + o, [P, T]) for n, o in (("QR", 0), ("KR", 4), ("VR", 8)))
        ASQ = at("ASQ", S0 + 12, [P, T])
        ARS = at("ARS", S0 + 16, [P, T])
        VN = at("VN", S0 + 20, [P, 12, P])
        SS = [at(f"SS{i}", S0 + 26 + 2 * i, [P, 2, 256]) for i in range(2)]
        PP = [at(f"PP{i}", S0 + 30 + 2 * i, [P, 2, 256]) for i in range(2)]
        PTS = [at(f"PTS{i}", S0 + 34 + 2 * i, [P, 2, 2, P]) for i in range(2)]
        NM = at("NM", S0 + 38, [P, NG, NT, 8])
        LS = at("LS", S0 + 38.75, [P, NG, NT, 8])
        BIAS = at("BIAS", S0 + 39.5, [P, 384])
        MXT = at("MXT", S0 + 41, [P, 2, 2])
        SPS = [b[:, :].rearrange("p (h k) -> p h k", h=2) for b in (B45, B67)]
        PTP = [DP[0][:, i * H:i * H + H].rearrange("p (h c q) -> p h c q", h=2, c=2) for i in range(2)]
        PVP = [DP[1][:, i * H:i * H + P] for i in range(2)]
        VTP = [B45[:, 0:H], B45[:, H:T], B67[:, 0:H]]
        bias_in = once("bias_in")
        qr_ready, kr_ready, vr_ready, asq_ready, qk_normed = (once(n) for n in (
            "qr_ready", "kr_ready", "vr_ready", "asq_ready", "qk_normed"))
        vt_ready, vn_ready = once("vt_ready"), once("vn_ready")
        s_ready, s_read, mx_ready, nm_ready, p_ready, pt_ready, pt_evac, pv_ready, pv_evac = (once(n) for n in (
            "s_ready", "s_read", "mx_ready", "nm_ready", "p_ready", "pt_ready", "pt_evac", "pv_ready", "pv_evac"))

        def attn_pe(pe):
            def head_norm_sum(n):
                pe.wait_ge(asq_ready, n + 1)
                pe.wait_ge(rs_sqrt, n + 1)
                for half in range(2):
                    mm = pe.matmul(B67[:, half * H:half * H + H], BLK, ASQ[:, half * H:half * H + H],
                                   start=True, stop=True)
                mm.then_inc(sq_used, 1)

            with pe.Fori(0, NPAIR) as p:
                for g in range(NG):
                    gi = p * NG + g
                    u0 = gi * NT
                    pe.wait_ge(pt_evac, u0)
                    pe.wait_ge(pv_evac, u0)
                    product(pe, Block("attn", p, 3 * g), XH, XL)
                    product(pe, Block("attn", p, 3 * g + 1), XH, XL)
                    pe.wait_ge(s_read, u0)
                    head_norm_sum(gi * 2)
                    product(pe, Block("attn", p, 3 * g + 2), XH, XL)
                    head_norm_sum(gi * 2 + 1)
                    pe.wait_ge(vr_ready, gi + 1)
                    pe.wait_ge(rs_sqrt, gi * 2 + 3)
                    gate(pe, "pe")
                    for b in range(VBATCH[g]):
                        for c in range(4 * b, min(4 * b + 4, CHUNKS[g])):
                            view, n = att_chunk(g, c)
                            tr = pe.transpose(VTP[b][0:n, (c % 4) * P:(c % 4) * P + P],
                                              view(VR[:, :]), IDENT)
                        tr.then_inc(vt_ready, 1)
                    pe.wait_ge(vn_ready, p * VBP + (VB0[g] + VBATCH[g]))
                    pe.wait_ge(qk_normed, gi * 2 + 2)
                    freed(pe, Block("attn", p, 3 * g + 1))
                    freed(pe, Block("attn", p, 3 * g + 2))

                    def scores(t):
                        if t >= 2:
                            pe.wait_ge(s_read, u0 + (t - 1))
                        keys, w, _, _ = att_keys(g, t)
                        for h in range(2):
                            r = slice(64 * h, 64 * h + 64)
                            mm = pe.matmul(SPS[t % 2][:, h, 0:w], att_tokens(g, t)(QR[r, :]), keys(KR[r, :]),
                                           start=True, stop=True)
                        mm.then_inc(s_ready, 1)

                    def turn(t):
                        pe.wait_ge(p_ready, u0 + (t + 1))
                        if t >= 2:
                            pe.wait_ge(pt_evac, u0 + (t - 1))
                        gate(pe, "pe")
                        for h in range(2):
                            o = 0
                            for i, (_, n) in enumerate(att_keys(g, t)[3]):
                                tr = pe.transpose(PTP[t % 2][0:n, h, i, :], PP[t % 2][:, h, o:o + n], IDENT)
                                o += n
                        tr.then_inc(pt_ready, 1)

                    def values(t):
                        pe.wait_ge(pt_evac, u0 + (t + 1))
                        if t >= 2:
                            pe.wait_ge(pv_evac, u0 + (t - 1))
                        gate(pe, "pe")
                        chunks = att_keys(g, t)[3]
                        for h in range(2):
                            for i, (c, n) in enumerate(chunks):
                                mm = pe.matmul(PVP[t % 2][64 * h:64 * h + 64, :], VN[0:n, c, 64 * h:64 * h + 64],
                                               PTS[t % 2][0:n, h, i, :], start=(i == 0), stop=(i == len(chunks) - 1))
                        mm.then_inc(pv_ready, 1)

                    scores(0)
                    for t in range(NT):
                        if t + 1 < NT:
                            scores(t + 1)
                        turn(t)
                        if t >= 1:
                            values(t - 1)
                    values(NT - 1)

        def attn_act(act):
            with act.Fori(0, NPAIR) as p:
                for g in range(NG):
                    gi = p * NG + g
                    u0 = gi * NT
                    for i, (raw, ready) in enumerate(((QR, qr_ready), (KR, kr_ready))):
                        b = Block("attn", p, 3 * g + i)
                        act.wait_ge(mm_done, b.n + 1)
                        if i == 0:
                            act.wait_ge(s_ready, u0)
                        act.wait_ge(sq_used, gi * 2 + (KD + i))
                        act.activation(ASQ[:, :], DP[b.slot][:, :], ACT.Square).then_inc(asq_ready, 1)
                        act.activation(raw[:, :], DP[b.slot][:, :], ACT.Copy).then_inc(ready, 1)
                        act.wait_ge(ready, gi + 1)
                        act.sem_inc(psum_free[b.slot], 1)
                        act.wait_ge(sq_used, gi * 2 + (KD + i + 1))
                        if i == 0:
                            act.wait_ge(qk_normed, gi * 2)
                        else:
                            act.wait_ge(qk_normed, gi * 2 + 1)
                        act.activation(ARS[:, :], B67[:, :], ACT.Sqrt, scale=1.0 / 64, bias=EPS).then_inc(rs_sqrt, 1)
                    b = Block("attn", p, 3 * g + 2)
                    act.wait_ge(mm_done, b.n + 1)
                    act.activation(VR[:, :], DP[b.slot][:, :], ACT.Copy).then_inc(vr_ready, 1)
                    act.wait_ge(vr_ready, gi + 1)
                    act.sem_inc(psum_free[b.slot], 1)
                    for b in range(VBATCH[g]):
                        act.wait_ge(vt_ready, p * VBP + (VB0[g] + b + 1))
                        if b == 0:
                            act.wait_ge(pv_ready, u0)
                        c0, c1 = 4 * b, min(4 * b + 4, CHUNKS[g])
                        lens = [att_chunk(g, c)[1] for c in range(c0, c1)]
                        at_c = 0
                        while at_c < len(lens):
                            end = at_c
                            while end < len(lens) and lens[end] == lens[at_c]:
                                end += 1
                            n = lens[at_c]
                            src = VTP[b][0:n, at_c * P:end * P]
                            cp = act.activation(VN[0:n, c0 + at_c:c0 + end, :].rearrange("p c n -> p (c n)"), src,
                                                ACT.Copy)
                            at_c = end
                        cp.then_inc(vn_ready, 1)

                    def exponential(t):
                        act.wait_ge(nm_ready, u0 + (t + 1))
                        if t >= 2:
                            act.wait_ge(pt_ready, u0 + (t - 1))
                        w = att_keys(g, t)[1]
                        for h in range(2):
                            e = act.activation(PP[t % 2][:, h, 0:w], SS[t % 2][:, h, 0:w], ACT.Exp, scale=0.125,
                                               bias=NM[:, g, t, ds(p * 2 + h, 1)],
                                               accum_out=LS[:, g, t, ds(p * 2 + h, 1)])
                        e.then_inc(p_ready, 1)

                    def evacuate(t):
                        act.wait_ge(pt_ready, u0 + (t + 1))
                        if t >= 2:
                            act.wait_ge(pv_ready, u0 + (t - 1))
                        chunks = att_keys(g, t)[3]
                        if len({n for _, n in chunks}) == 1:
                            n, k = chunks[0][1], len(chunks)
                            cp = act.activation(PTS[t % 2][0:n, :, 0:k, :], PTP[t % 2][0:n, :, 0:k, :], ACT.Copy)
                        else:
                            for i, (_, n) in enumerate(chunks):
                                cp = act.activation(PTS[t % 2][0:n, :, i, :], PTP[t % 2][0:n, :, i, :], ACT.Copy)
                        cp.then_inc(pt_evac, 1)

                    for t in range(NT):
                        exponential(t)
                        if t >= 1:
                            evacuate(t - 1)
                    evacuate(NT - 1)

        def attn_dve(dve):
            dve.wait_ge(bias_in, 16)
            with dve.Fori(0, NPAIR) as p:
                for g in range(NG):
                    gi = p * NG + g
                    u0 = gi * NT
                    for i, (raw, ready, w) in enumerate(((QR, qr_ready, "qn"), (KR, kr_ready, "kn"))):
                        dve.wait_ge(rs_sqrt, gi * 2 + (i + 2))
                        dve.reciprocal(ARS[:, :], ARS[:, :]).then_inc(rs_ready, 1)
                        dve.wait_ge(rs_ready, gi * 2 + (i + 2))
                        dve.wait_ge(ready, gi + 1)
                        dve.scalar_tensor_tensor(out=raw[:, :], in0=raw[:, :], scalar=col(w), in1=ARS[:, :],
                                                 op0=ALU.mult, op1=ALU.mult).then_inc(qk_normed, 1)

                    def maximum(t):
                        dve.wait_ge(s_ready, u0 + (t + 1))
                        if t >= 2:
                            dve.wait_ge(p_ready, u0 + (t - 1))
                        _, w, off, _ = att_keys(g, t)
                        off = 256 if g == 2 else off
                        for h in range(2):
                            i = dve.scalar_tensor_tensor(out=SS[t % 2][:, h, 0:w], in0=BIAS[:, off:off + w],
                                                         scalar=CON[:, ds(p * 2 + (CST["slopes"][0] + 8 * g + h), 1)],
                                                         in1=SPS[t % 2][:, h, 0:w], op0=ALU.mult, op1=ALU.add)
                        i.then_inc(s_read, 1)
                        dve.wait_ge(s_read, u0 + (t + 1))
                        dve.tensor_reduce(MXT[:, t % 2, :], SS[t % 2][:, :, 0:w], AXX, ALU.max).then_inc(mx_ready, 1)
                        dve.wait_ge(mx_ready, u0 + (t + 1))
                        dve.tensor_scalar(NM[:, g, t, ds(p * 2, 2)], MXT[:, t % 2, :], -0.125, None,
                                          ALU.mult).then_inc(nm_ready, 1)

                    def collect(t):
                        dve.wait_ge(pv_ready, u0 + (t + 1))
                        o = att_tokens(g, t)(OG[g][:, ds(p, 1), :].rearrange("p a n -> p (a n)"))
                        src = PVP[t % 2]
                        dve.tensor_copy(o, src).then_inc(pv_evac, 1)

                    for t in range(NT):
                        maximum(t)
                        if t >= 2:
                            collect(t - 2)
                    collect(NT - 2)
                    collect(NT - 1)

        STM = [at(f"STM{g}", S0 + 4 * g, [8, T]) for g in range(NG)]
        STL = [at(f"STL{g}", S0 + 12 + 4 * g, [8, T]) for g in range(NG)]
        STX = at("STX", S0 + 24, [8, T])
        SEL = at("SEL", S0 + 46, [8, NPAIR, P])
        YH = at("YH", S0 + 30, [P, NPAIR, T], F32R)
        YL = at("YL", 64, [P, NPAIR, T], F32R)
        sel_in = once("sel_in")
        st_t, st_evac, st_max, st_sub, st_exp, st_mul, st_rec, st_w = (once(n) for n in (
            "st_t", "st_evac", "st_max", "st_sub", "st_exp", "st_mul", "st_rec", "st_w"))
        wb_ready, wb_used, og_sum = once("wb_ready"), once("wb_used"), once("og_sum")
        yh_ready, yl_ready = sem("yh_ready"), sem("yl_ready")
        BANKS = [DP[0], DP[1], B45, B67]
        UT = NPAIR * NG * NT

        def comb_pe(pe):
            pe.wait_ge(nm_ready, UT)
            pe.wait_ge(p_ready, UT)
            pe.wait_ge(pv_evac, UT)
            freed(pe, Block("attn", NPAIR - 1, 7))
            freed(pe, Block("attn", NPAIR - 1, 8))
            for n in range(6):
                g, stat = n // 2, (NM, LS)[n % 2]
                if n >= 4:
                    pe.wait_ge(st_evac, n - 3)
                for t in range(NT):
                    tr = pe.transpose(BANKS[n % 4][0:8, P * t:P * t + P], stat[:, g, t, :], IDENT)
                tr.then_inc(st_t, 1)
            pe.wait_ge(st_evac, 6)
            pe.wait_ge(st_w, NG)
            pe.wait_ge(sel_in, 16)
            for n in range(NPAIR * NG):
                p, g = n // NG, n % NG
                if n >= 4:
                    pe.wait_ge(wb_used, n - 3)
                for half in range(2):
                    mm = pe.matmul(BANKS[n % 4][:, half * H:half * H + H], SEL[:, p, :],
                                   STM[g][:, half * H:half * H + H], start=True, stop=True)
                mm.then_inc(wb_ready, 1)

        def comb_act(act):
            for n in range(6):
                g, dst = n // 2, (STM, STL)[n % 2][n // 2]
                act.wait_ge(st_t, n + 1)
                src = BANKS[n % 4][0:8, :]
                if g == 0:
                    act.activation(dst[:, :], src, ACT.Copy).then_inc(st_evac, 1)
                else:
                    r = (4, 8)[g - 1]
                    act.activation(dst[:, :].rearrange("p (s r) -> p r s", r=r),
                                   src.rearrange("p (r s) -> p r s", r=r), ACT.Copy).then_inc(st_evac, 1)
            for g in range(NG):
                act.wait_ge(st_sub, g + 1)
                act.activation(STM[g][:, :], STM[g][:, :], ACT.Exp).then_inc(st_exp, 1)
            for p in range(NPAIR):
                act.wait_ge(og_sum, 2 * p + 2)
                act.activation(YH[:, p, :], OG[0][:, p, :], ACT.Copy).then_inc(yh_ready, 1)

        def comb_dve(dve):
            dve.wait_ge(st_evac, 6)
            dve.tensor_tensor(STX[:, :], STM[0][:, :], STM[1][:, :], ALU.min).then_inc(st_max, 1)
            dve.wait_ge(st_max, 1)
            dve.tensor_tensor(STX[:, :], STX[:, :], STM[2][:, :], ALU.min).then_inc(st_max, 1)
            dve.wait_ge(st_max, 2)
            for g in range(NG):
                dve.tensor_tensor(STM[g][:, :], STX[:, :], STM[g][:, :], ALU.subtract).then_inc(st_sub, 1)
            for g in range(NG):
                dve.wait_ge(st_exp, g + 1)
                dve.tensor_tensor(STL[g][:, :], STL[g][:, :], STM[g][:, :], ALU.mult).then_inc(st_mul, 1)
            dve.wait_ge(st_mul, 3)
            dve.tensor_tensor(STX[:, :], STL[0][:, :], STL[1][:, :], ALU.add).then_inc(st_mul, 1)
            dve.wait_ge(st_mul, 4)
            dve.tensor_tensor(STX[:, :], STX[:, :], STL[2][:, :], ALU.add).then_inc(st_mul, 1)
            dve.wait_ge(st_mul, 5)
            dve.reciprocal(STX[:, :], STX[:, :]).then_inc(st_rec, 1)
            dve.wait_ge(st_rec, 1)
            for g in range(NG):
                dve.tensor_tensor(STM[g][:, :], STM[g][:, :], STX[:, :], ALU.mult).then_inc(st_w, 1)
            for n in range(NPAIR * NG):
                p, g = n // NG, n % NG
                dve.wait_ge(wb_ready, n + 1)
                dve.tensor_tensor(OG[g][:, p, :], OG[g][:, p, :], BANKS[n % 4][:, :], ALU.mult).then_inc(wb_used, 1)

        def comb_pool(pool):
            for p in range(NPAIR):
                for g in (1, 2):
                    pool.wait_ge(wb_used, NG * p + g + 1)
                    if g == 2:
                        pool.wait_ge(og_sum, 2 * p + 1)
                    pool.tensor_tensor(OG[0][:, p, :], OG[0][:, p, :], OG[g][:, p, :], ALU.add).then_inc(og_sum, 1)
                pool.wait_ge(yh_ready, p + 1)
                pool.tensor_tensor(YL[:, p, :], OG[0][:, p, :], YH[:, p, :].bitcast(F32),
                                   ALU.subtract).then_inc(yl_ready, 1)

        SG = [at(f"SG{i}", S0 + 4 * i, [P, T]) for i in range(2)]
        sg_ready, sg_used, mx_done = sem("sg_ready"), sem("sg_used"), sem("mx_done")

        def mix_pe(pe, name):
            with pe.Fori(0, 8) as m:
                product(pe, Block(name, m, 0), XH, XL)
                product(pe, Block(name, m, 1), YH, YL)

        def mix_act(act, name, done):
            with act.Fori(0, 8) as m:
                b = Block(name, m, 0)
                act.wait_ge(mm_done, b.n + 1)
                act.wait_ge(sg_used, m + done)
                act.activation(SG[0][:, :], DP[b.slot][:, :], ACT.Sigmoid).then_inc(sg_ready, 1)
                act.wait_ge(sg_ready, m + (done + 1))
                act.sem_inc(psum_free[b.slot], 1)

        def mix_dve(dve, name, done, add, first):
            with dve.Fori(0, 8) as m:
                b = Block(name, m, 1)
                dve.wait_ge(mm_done, b.n + 1)
                dve.wait_ge(sg_ready, m + (done + 1))
                o = MX[:, ds(m, 1), :].rearrange("p a n -> p (a n)")
                if add:
                    dve.tensor_tensor(SG[1][:, :], SG[0][:, :], DP[b.slot][:, :], ALU.mult).then_inc(sg_used, 1)
                    dve.wait_ge(sg_used, m + (done + 1))
                    dve.tensor_tensor(o, o, SG[1][:, :], ALU.add).then_inc(mx_done, 1)
                else:
                    dve.tensor_tensor(o, SG[0][:, :], DP[b.slot][:, :], ALU.mult).then_inc(sg_used, 1)
                    dve.wait_ge(sg_used, m + (done + 1))
                    dve.sem_inc(mx_done, 1)
                dve.wait_ge(mx_done, m + (done + 1))
                dve.sem_inc(psum_free[b.slot], 1)

        KN, VND = at("KN", 64, [P, NT, P]), at("VND", 68, [P, NT, P])
        OD = [at(f"OD{d}", 72 + 4 * d, [P, NT, P]) for d in range(2)]
        OA = at("OA", 80, [P, NPAIR, T])
        LM = at("LM", S0, [P, 7, 2, P])
        KQ = at("KQ", S0 + 7, [P, 2, T])
        ZS = at("ZS", S0 + 15, [P, T])
        ABN = at("ABN", S0 + 19, [P, NT, 48])
        CUM = at("CUM", S0 + 20.5, [P, 6, 2, NT, 8])
        PC = at("PC", S0 + 23.5, [P, 6, 2, NT, 2])
        EGT = at("EGT", S0 + 24.25, [P, 2, NT])
        Q0 = S0 + 24.5
        RB = at("RB", Q0, [P, 2, 2, P])
        EE = at("EE", Q0 + 2, [P, 2, 2, 2, P])
        ATS = at("ATS", Q0 + 6, [P, 2, 2, P])
        XX = at("XX", Q0 + 8, [P, 2, 2, 2, P])
        PM = at("PM", Q0 + 12, [P, 2, 2, P])
        QD = at("QD", Q0 + 14, [P, 2, P])
        VB = at("VB", Q0 + 15, [P, 2, 2, 64])
        KBE = at("KBE", Q0 + 16, [P, 2, 2, 64])
        KDC = at("KDC", Q0 + 17, [P, 2, 2, 64])
        WT = at("WT", Q0 + 18, [P, 2, P])
        VNEW = at("VNEW", Q0 + 19, [P, 2, 2, 64])
        ST = at("ST", Q0 + 20, [P, 2, 64])
        SS16 = at("SS16", Q0 + 20.5, [P, 2 * NT])
        CVT = at("CVT", Q0, [P, T])
        DSQ = at("DSQ", Q0 + 4, [P, T])
        DRS = at("DRS", Q0 + 8, [P, T])
        VT = at("VT", Q0 + 12, [P, T])
        AB = at("AB", Q0, [48, T])
        AB1, AB2 = at("AB1", Q0 + 4, [16, T]), at("AB2", Q0 + 8, [16, T])
        NEA = at("NEA", Q0 + 12, [16, 1])
        BA = [DP[0][:, 0:H], DP[0][:, H:T]]
        BB = [DP[1][:, 0:H], DP[1][:, H:T]]
        BC = [B45[:, 0:H], B45[:, H:T]]
        BD = [B67[:, 0:H], B67[:, H:T]]
        lm_in = once("lm_in")
        ab_set, ab_act, ab_dve, abt, abn_ready, cum_ps, cum_act, cum_dve = (once(n) for n in (
            "ab_set", "ab_act", "ab_dve", "abt", "abn_ready", "cum_ps", "cum_act", "cum_dve"))
        cv_mid, cv_dve, cv_silu, dsq_ready, dsum, drs_root, drs_rec, dn_normed, z_ready, pc_ready = (once(n) for n in (
            "cv_mid", "cv_dve", "cv_silu", "dsq_ready", "dsum", "drs_root", "drs_rec", "dn_normed", "z_ready",
            "pc_ready"))
        kv_turned, kn_ready, vnd_ready, st_zero = (once(n) for n in ("kv_turned", "kn_ready", "vnd_ready", "st_zero"))
        rb_ready, r_ready, e_dve, er_ready, e_exp, kk_ready, a_ready, at_turned, at_ready, xx_pool, xx_init = (
            once(n) for n in ("rb_ready", "r_ready", "e_dve", "er_ready", "e_exp", "kk_ready", "a_ready", "at_turned",
                             "at_ready", "xx_pool", "xx_init"))
        prod_ready, pm_ready, upd_ready, xx_ready = (once(n) for n in (
            "prod_ready", "pm_ready", "upd_ready", "xx_ready"))
        qd_ready = once("qd_ready")
        sc_ready, wt_turned, wt_ready, vnew_ps, vnew_ready, o_ps, o_read, dstate_ps, st_ready = (once(n) for n in (
            "sc_ready", "wt_turned", "wt_ready", "vnew_ps", "vnew_ready", "o_ps", "o_read", "dstate_ps", "st_ready"))
        o_sum, o_sq, o_red, o_root, o_rec, o_norm, o_turned, oa_done = (once(n) for n in (
            "o_sum", "o_sq", "o_red", "o_root", "o_rec", "o_norm", "o_turned", "oa_done"))
        NL = 6

        def bc(v, n):
            return v.rearrange("p (a k) -> p a k", a=1).broadcast_to([P, n, P])

        def delta_pe(pe):
            product(pe, Block("dnab", 0, 0), XH, XL)
            pe.wait_ge(ab_act, 5)
            pe.wait_ge(ab_dve, 2)
            pe.wait_ge(mx_done, 8)
            for c in range(NT):
                tr = pe.transpose(B45[:, 48 * c:48 * c + 48], AB[:, P * c:P * c + P], IDENT[0:48, 0:48])
            tr.then_inc(abt, 1)
            pe.wait_ge(abn_ready, 1)
            for kind in range(2):
                for d in range(2):
                    o = H + (2 * kind + d) * 64
                    mm = pe.matmul(B45[:, o:o + 64].rearrange("p (c h) -> p c h", h=8),
                                   con("ones") if kind else con("tri", d, P), ABN[:, :, 8 * d:8 * d + 8],
                                   start=True, stop=True)
            mm.then_inc(cum_ps, 1)
            with pe.Fori(0, NPAIR) as p:
                pe.wait_ge(oa_done, p)
                for i in range(4):
                    product(pe, Block("dn", p, i), XH, XL)
                    if i in (1, 2):
                        n = p * 2 + i
                        pe.wait_ge(dsq_ready, n)
                        pe.wait_ge(drs_root, n - 1)
                        for half in range(2):
                            mm = pe.matmul(B67[:, half * H:half * H + H], BLK, DSQ[:, half * H:half * H + H],
                                           start=True, stop=True)
                        mm.then_inc(dsum, 1)
                pe.wait_ge(dn_normed, p * 2 + 2)
                pe.wait_ge(cv_silu, p * 3 + 3)
                pe.wait_ge(drs_root, p * 2 + 2)
                pe.wait_ge(cum_dve, 3)
                pe.wait_ge(cum_act, 4)
                for c in range(NT):
                    pe.transpose(B45[:, P * c:P * c + P], KQ[:, 0, P * c:P * c + P], IDENT)
                    tr = pe.transpose(B67[:, P * c:P * c + P], VT[:, P * c:P * c + P], IDENT)
                tr.then_inc(kv_turned, 1)
                pe.wait_ge(kn_ready, p + 1)
                pe.wait_ge(vnd_ready, p + 1)
                freed(pe, Block("dn", p, 2))
                freed(pe, Block("dn", p, 3))
                for s in range(NT):
                    q = p * NT + s
                    j = q * 2
                    for d in range(2):
                        tok = slice(P * (7 - s if d else s), P * (7 - s if d else s) + P)
                        if s:
                            pe.wait_ge(st_ready, j + (d - 1))
                            pe.wait_ge(o_read, j + (d - 1))
                        pe.wait_ge(rb_ready, j + (d + 1))
                        pe.matmul(BA[d][:, 0:256], ONES, RB[:, d, :, :].rearrange("p h n -> p (h n)"),
                                  start=True, stop=True).then_inc(r_ready, 1)
                        for h in range(2):
                            r = slice(64 * h, 64 * h + 64)
                            mm = pe.matmul((BB, BC)[h][d][:, 0:256].rearrange("p (a n) -> p a n", a=2),
                                           KQ[r, 0, tok], KQ[r, :, tok], start=True, stop=True)
                        mm.then_inc(kk_ready, 1)
                    for d in range(2):
                        pe.wait_ge(a_ready, j + (d + 1))
                        pe.wait_ge(er_ready, j + (d + 1))
                        for h in range(2):
                            tr = pe.transpose(BA[d][:, P * h:P * h + P], EE[:, d, 0, h, :], IDENT)
                        tr.then_inc(at_turned, 1)
                    for l in range(NL):
                        for d in range(2):
                            if l == 0:
                                pe.wait_ge(xx_init, j + (d + 1))
                            else:
                                pe.wait_ge(xx_ready, q * (2 * NL) + (2 * (l - 1) + d + 1))
                            for h in range(2):
                                mm = pe.matmul(BB[d][:, P * h:P * h + P], ATS[:, d, h, :], XX[:, d, 0, h, :],
                                               start=True, stop=True)
                            mm.then_inc(prod_ready, 1)
                        for d in range(2):
                            pe.wait_ge(pm_ready, q * (2 * NL) + (2 * l + d + 1))
                            for h in range(2):
                                if l < NL - 1:
                                    pe.matmul(BC[d][:, P * h:P * h + P], XX[:, d, 1, h, :], PM[:, d, h, :],
                                              start=True, stop=True)
                                mm = pe.matmul(BC[d][:, 256 + P * h:256 + P * h + P], PM[:, d, h, :],
                                               XX[:, d, 1, h, :], start=True, stop=True)
                            mm.then_inc(upd_ready, 1)
                    for d in range(2):
                        pe.wait_ge(xx_ready, q * (2 * NL) + (2 * (NL - 1) + d + 1))
                        pe.wait_ge(sc_ready, j + (d + 1))
                        gate(pe, "pe")
                        for h in range(2):
                            mm = pe.matmul(BD[d][64 * h:64 * h + 64, 0:P], KBE[:, d, h, :], XX[:, d, 1, h, :],
                                           start=True, stop=True)
                        mm.then_inc(wt_turned, 1)
                    for d in range(2):
                        pe.wait_ge(wt_ready, j + (d + 1))
                        if s:
                            pe.wait_ge(st_ready, j + (d - 1))
                        else:
                            pe.wait_ge(st_zero, p + 1)
                        for h in range(2):
                            r = slice(64 * h, 64 * h + 64)
                            o = (BA, BB)[h][d][:, 0:64]
                            pe.matmul(o, XX[:, d, 1, h, :], VB[:, d, h, :], start=True, stop=False)
                            mm = pe.matmul(o, WT[r, d, :], ST[r, d, :], start=False, stop=True)
                        mm.then_inc(vnew_ps, 1)
                    for d in range(2):
                        pe.wait_ge(vnew_ready, j + (d + 1))
                        pe.wait_ge(qd_ready, j + (d + 1))
                        for h in range(2):
                            r = slice(64 * h, 64 * h + 64)
                            o = (BC, BD)[h][d][:, 0:64]
                            pe.matmul(o, EE[:, d, 1, h, :], VNEW[:, d, h, :], start=True, stop=False)
                            mm = pe.matmul(o, QD[r, d, :], ST[r, d, :], start=False, stop=True)
                        mm.then_inc(o_ps, 1)
                        for h in range(2):
                            mm = pe.matmul(BA[d][64 * h:64 * h + 64, P:P + 64], KDC[:, d, h, :], VNEW[:, d, h, :],
                                           start=True, stop=True)
                        mm.then_inc(dstate_ps, 1)
                pe.wait_ge(o_norm, p + 1)
                pe.wait_ge(o_read, p * 16 + 16)
                for c in range(NT):
                    tr = pe.transpose(B45[:, P * c:P * c + P], OD[0][:, c, :], IDENT)
                tr.then_inc(o_turned, 1)

        def delta_act(act):
            b = Block("dnab", 0, 0)
            act.wait_ge(mm_done, last_block("mixb"))
            act.wait_ge(ab_set, 1)
            act.activation(NEA[:, :], COL[0:16, COLS["alog"]:COLS["alog"] + 1], ACT.Exp).then_inc(ab_act, 1)
            act.wait_ge(mm_done, b.n + 1)
            dp = DP[b.slot]
            dtb = COL[0:16, COLS["dtb"]:COLS["dtb"] + 1]
            act.activation(AB1[:, :], dp[0:16, :], ACT.Abs, bias=dtb).then_inc(ab_act, 1)
            act.wait_ge(ab_act, 2)
            act.activation(AB2[:, :], AB1[:, :], ACT.Exp, scale=-1.0).then_inc(ab_act, 1)
            act.wait_ge(ab_act, 3)
            act.activation(AB1[:, :], AB2[:, :], ACT.Ln, bias=1.0).then_inc(ab_act, 1)
            act.wait_ge(ab_act, 4)
            act.activation(AB2[:, :], dp[0:16, :], ACT.Relu, bias=dtb)
            act.activation(AB[32:48, :], dp[32:48, :], ACT.Sigmoid).then_inc(ab_act, 1)
            act.wait_ge(ab_act, 5)
            act.sem_inc(psum_free[b.slot], 1)
            act.wait_ge(abt, 1)
            act.activation(ABN[:, :, :].rearrange("p c n -> p (c n)"), B45[:, 0:48 * NT], ACT.Copy).then_inc(
                abn_ready, 1)
            act.wait_ge(cum_ps, 1)
            cum = B45[:, H:H + 256].rearrange("p (k d c h) -> p k d c h", k=2, d=2, h=8)
            act.activation(CUM[:, 1].rearrange("p d c h -> p (d c h)"), B45[:, H:H + P], ACT.Copy).then_inc(cum_act, 1)
            act.activation(CUM[:, 5].rearrange("p d c h -> p (d c h)"), B45[:, H + P:H + 256], ACT.Exp).then_inc(
                cum_act, 1)
            act.activation(CUM[:, 3].rearrange("p d c h -> p (d c h)"), B45[:, H:H + P], ACT.Exp).then_inc(cum_act, 1)
            act.wait_ge(cum_dve, 1)
            act.activation(CUM[:, 4], CUM[:, 4], ACT.Exp).then_inc(cum_act, 1)
            with act.Fori(0, NPAIR) as p:
                act.wait_ge(oa_done, p)
                for i in range(3):
                    b = Block("dn", p, i)
                    act.wait_ge(mm_done, b.n + 1)
                    if i:
                        act.wait_ge(cv_silu, p * 3 + i)
                    act.activation(CVT[:, :], DP[b.slot][:, :], ACT.Copy,
                                   scale=COL[:, ds(p + (COLS["dnconv"] + 12 + 4 * i), 1)]).then_inc(cv_mid, 1)
                    act.wait_ge(cv_dve, p * 6 + (2 * i + 2))
                    dst = (KQ[:, 1, :], KQ[:, 0, :], VT[:, :])[i]
                    act.activation(dst, CVT[:, :], ACT.Silu).then_inc(cv_silu, 1)
                    if i < 2:
                        act.wait_ge(cv_silu, p * 3 + (i + 1))
                        if i:
                            act.wait_ge(dsum, p * 2 + 1)
                        act.activation(DSQ[:, :], dst, ACT.Square).then_inc(dsq_ready, 1)
                    if i:
                        act.wait_ge(dsum, p * 2 + i)
                        act.wait_ge(dn_normed, p * 2 + (i - 1))
                        act.activation(DRS[:, :], B67[:, :], ACT.Sqrt, bias=EPS).then_inc(drs_root, 1)
                b = Block("dn", p, 3)
                act.wait_ge(mm_done, b.n + 1)
                act.activation(ZS[:, :], DP[b.slot][:, :], ACT.Silu).then_inc(z_ready, 1)
                act.wait_ge(z_ready, p + 1)
                act.sem_inc(psum_free[b.slot], 1)
                act.wait_ge(kv_turned, p + 1)
                act.activation(KN[:, :, :].rearrange("p c n -> p (c n)"), B45[:, :], ACT.Copy).then_inc(kn_ready, 1)
                for s in range(NT):
                    q = p * NT + s
                    j = q * 2
                    for d in range(2):
                        act.wait_ge(r_ready, j + (d + 1))
                        act.wait_ge(vnd_ready, p + 1)
                        act.activation(RB[:, d].rearrange("p h n -> p (h n)"), BA[d][:, 0:256], ACT.Exp).then_inc(
                            er_ready, 1)
                        act.wait_ge(e_dve, j + (d + 1))
                        act.activation(EE[:, d, 0], EE[:, d, 0], ACT.Exp, scale=-1.0)
                        act.activation(EE[:, d, 1], EE[:, d, 1], ACT.Exp).then_inc(e_exp, 1)
                    for d in range(2):
                        act.wait_ge(at_turned, j + (d + 1))
                        act.activation(ATS[:, d].rearrange("p h n -> p (h n)"), BA[d][:, 0:256], ACT.Copy).then_inc(
                            at_ready, 1)
                    for d in range(2):
                        act.wait_ge(wt_turned, j + (d + 1))
                        act.activation(WT[:, d, :], BD[d][:, 0:P], ACT.Copy, scale=-1.0).then_inc(wt_ready, 1)
                    for d in range(2):
                        act.wait_ge(vnew_ps, j + (d + 1))
                        for h in range(2):
                            cp = act.activation(VNEW[:, d, h, :], (BA, BB)[h][d][:, 0:64], ACT.Copy)
                        cp.then_inc(vnew_ready, 1)
                    for d in range(2):
                        c = 7 - s if d else s
                        act.wait_ge(o_ps, j + (d + 1))
                        for h in range(2):
                            cp = act.activation(OD[d][:, c, 64 * h:64 * h + 64], (BC, BD)[h][d][:, 0:64], ACT.Copy)
                        cp.then_inc(o_read, 1)
                act.wait_ge(o_sum, p + 1)
                act.wait_ge(st_ready, p * 16 + 16)
                act.activation(OD[1][:, :, :], OD[0][:, :, :], ACT.Square).then_inc(o_sq, 1)
                act.wait_ge(o_red, p + 1)
                act.activation(SS16[:, :], SS16[:, :], ACT.Sqrt, scale=1.0 / 64, bias=EPS).then_inc(o_root, 1)

        def delta_dve(dve):
            dve.wait_ge(mm_done, last_block("mixb"))
            dve.memset(AB[:, :], 0.0).then_inc(ab_set, 1)
            dve.wait_ge(ab_set, 1)
            dve.wait_ge(ab_act, 5)
            dve.tensor_tensor(AB1[:, :], AB1[:, :], AB2[:, :], ALU.add).then_inc(ab_dve, 1)
            dve.wait_ge(ab_dve, 1)
            dve.tensor_scalar(AB[0:16, :], AB1[:, :], NEA[:, :], -1.0, ALU.mult, ALU.mult).then_inc(ab_dve, 1)
            dve.wait_ge(cum_act, 3)
            dve.tensor_tensor(CUM[:, 4].rearrange("p d c h -> p (d c h)"), B45[:, H + P:H + 256],
                              CUM[:, 1].rearrange("p d c h -> p (d c h)"), ALU.subtract).then_inc(cum_dve, 1)
            for d in range(2):
                dve.tensor_copy(CUM[:, 0, d], ABN[:, :, 8 * d:8 * d + 8])
                i = dve.tensor_copy(CUM[:, 2, d], ABN[:, :, 32 + 8 * d:40 + 8 * d])
            i.then_inc(cum_dve, 1)
            dve.wait_ge(cum_dve, 2)
            dve.tensor_tensor(CUM[:, 3], CUM[:, 3], CUM[:, 2], ALU.mult).then_inc(cum_dve, 1)
            dve.wait_ge(cum_dve, 3)
            dve.wait_ge(cum_act, 4)
            dve.wait_ge(lm_in, 16)
            with dve.Fori(0, NPAIR) as p:
                dve.tensor_copy(PC[:, :, :, :, :].rearrange("p k d c h -> p (k d c) h"),
                                CUM[:, :, :, :, ds(p * 2, 2)].rearrange("p k d c h -> p (k d c) h")).then_inc(
                    pc_ready, 1)
                dve.wait_ge(pc_ready, p * 2 + 1)
                for h in range(2):
                    i = dve.tensor_copy(EGT[64 * h:64 * h + 64], PC[64 * h:64 * h + 64, 5, :, :, h])
                i.then_inc(pc_ready, 1)
                for i in range(3):
                    b = Block("dn", p, i)
                    dve.wait_ge(cv_mid, p * 3 + (i + 1))
                    for n, tap in enumerate((0, 2)):
                        dst = CVT[:, 1:T] if tap == 0 else CVT[:, 0:T - 1]
                        src = DP[b.slot][:, 0:T - 1] if tap == 0 else DP[b.slot][:, 1:T]
                        dve.scalar_tensor_tensor(out=dst, in0=src,
                                                 scalar=COL[:, ds(p + (COLS["dnconv"] + 12 * tap + 4 * i), 1)],
                                                 in1=dst, op0=ALU.mult, op1=ALU.add).then_inc(cv_dve, 1)
                        dve.wait_ge(cv_dve, p * 6 + (2 * i + n + 1))
                    dve.sem_inc(psum_free[b.slot], 1)
                    if i:
                        dve.wait_ge(drs_root, p * 2 + i)
                        dve.reciprocal(DRS[:, :], DRS[:, :]).then_inc(drs_rec, 1)
                        dve.wait_ge(drs_rec, p * 2 + i)
                        x = KQ[:, 2 - i, :]
                        dve.scalar_tensor_tensor(out=x, in0=x, scalar=(0.125, 1.0)[i - 1], in1=DRS[:, :],
                                                 op0=ALU.mult, op1=ALU.mult).then_inc(dn_normed, 1)
                dve.wait_ge(kv_turned, p + 1)
                dve.tensor_copy(VND[:, :, :].rearrange("p c n -> p (c n)"), B67[:, :]).then_inc(vnd_ready, 1)
                dve.wait_ge(vnd_ready, p + 1)
                dve.memset(ST[:, :, :], 0.0).then_inc(st_zero, 1)
                dve.wait_ge(st_zero, p + 1)
                for s in range(NT):
                    q = p * NT + s
                    j = q * 2
                    for d in range(2):
                        c = 7 - s if d else s
                        if s:
                            dve.wait_ge(qd_ready, j + (d - 1))
                        for h in range(2):
                            i = dve.tensor_scalar(RB[:, d, h, :], con("tri", d, P), PC[:, 0, d, c, h:h + 1], None,
                                                  ALU.mult)
                        i.then_inc(rb_ready, 1)
                    for d in range(2):
                        c = 7 - s if d else s
                        dve.wait_ge(r_ready, j + (d + 1))
                        dve.wait_ge(er_ready, j + (d + 1))
                        for k, mask in ((0, "mpos"), (1, "mneg")):
                            for h in range(2):
                                i = dve.scalar_tensor_tensor(out=EE[:, d, k, h, :], in0=BA[d][:, P * h:P * h + P],
                                                             scalar=PC[:, 1, d, c, h:h + 1], in1=con(mask, d, P),
                                                             op0=ALU.subtract, op1=ALU.add)
                        i.then_inc(e_dve, 1)
                        for h in range(2):
                            r = slice(64 * h, 64 * h + 64)
                            i = dve.tensor_tensor(QD[r, d, :], KQ[r, 1, P * c:P * c + P], RB[r, d, h, :], ALU.mult)
                        i.then_inc(qd_ready, 1)
                    for d in range(2):
                        c = 7 - s if d else s
                        dve.wait_ge(kk_ready, j + (d + 1))
                        dve.wait_ge(e_exp, j + (d + 1))
                        for h in range(2):
                            ps = (BB, BC)[h][d]
                            dve.scalar_tensor_tensor(out=EE[:, d, 0, h, :], in0=ps[:, 0:P],
                                                     scalar=PC[:, 2, d, c, h:h + 1], in1=EE[:, d, 0, h, :],
                                                     op0=ALU.mult, op1=ALU.mult)
                            i = dve.tensor_tensor(EE[:, d, 1, h, :], ps[:, P:256], EE[:, d, 1, h, :], ALU.mult)
                        i.then_inc(a_ready, 1)
                    for l in range(NL):
                        for d in range(2):
                            n = q * (2 * NL) + (2 * l + d + 1)
                            dve.wait_ge(prod_ready, n)
                            dve.tensor_tensor(PM[:, d], BB[d][:, 0:256].rearrange("p (h n) -> p h n", h=2),
                                              bc(LM[:, l + 1, d, :], 2), ALU.mult).then_inc(pm_ready, 1)
                        for d in range(2):
                            n = q * (2 * NL) + (2 * l + d + 1)
                            dve.wait_ge(upd_ready, n)
                            lo = 0 if l < NL - 1 else 1
                            x = XX[:, d, lo:2].rearrange("p a h n -> p (a h n)")
                            dve.tensor_tensor(x, x, BC[d][:, 256 * lo:H], ALU.subtract).then_inc(xx_ready, 1)
                    for d in range(2):
                        c = 7 - s if d else s
                        dve.wait_ge(dstate_ps, j + (d + 1))
                        dve.scalar_tensor_tensor(out=ST[:, d, :], in0=ST[:, d, :], scalar=EGT[:, d, c:c + 1],
                                                 in1=BA[d][:, P:P + 64], op0=ALU.mult, op1=ALU.add).then_inc(
                            st_ready, 1)
                dve.wait_ge(o_sq, p + 1)
                dve.tensor_reduce(SS16[:, :], OD[1][:, :, :].rearrange("p c (h n) -> p (c h) n", h=2), AXX,
                                  ALU.add).then_inc(o_red, 1)
                dve.wait_ge(o_root, p + 1)
                dve.reciprocal(SS16[:, :], SS16[:, :]).then_inc(o_rec, 1)
                dve.wait_ge(o_rec, p + 1)
                o = OD[0][:, :, :].rearrange("p c (h n) -> p (c h) n", h=2)
                dve.tensor_tensor(o, o, SS16[:, :].rearrange("p (a k) -> p a k", k=1).broadcast_to([P, 2 * NT, 64]),
                                  ALU.mult).then_inc(o_norm, 1)
                dve.wait_ge(o_turned, p + 1)
                dve.wait_ge(z_ready, p + 1)
                dve.scalar_tensor_tensor(out=OA[:, ds(p, 1), :].rearrange("p a n -> p (a n)"), in0=B45[:, :],
                                         scalar=col("dnw"), in1=ZS[:, :], op0=ALU.mult,
                                         op1=ALU.mult).then_inc(oa_done, 1)

        def delta_pool(pool):
            split(pool, Block("dnab", 0, 0))
            pool.wait_ge(lm_in, 16)
            with pool.Fori(0, NPAIR) as p:
                for i in range(4):
                    split(pool, Block("dn", p, i))
                pool.wait_ge(pc_ready, p * 2 + 2)
                pool.wait_ge(vnd_ready, p + 1)
                for s in range(NT):
                    q = p * NT + s
                    j = q * 2
                    for d in range(2):
                        pool.wait_ge(a_ready, j + (d + 1))
                        m = j * 4 + (4 * d)
                        pool.tensor_tensor(PM[:, d], EE[:, d, 0], bc(LM[:, 0, d, :], 2), ALU.mult).then_inc(xx_pool, 1)
                        pool.wait_ge(xx_pool, m + 1)
                        pool.tensor_tensor(XX[:, d, 0], bc(IDENT, 2), PM[:, d], ALU.subtract).then_inc(xx_pool, 1)
                        pool.wait_ge(at_ready, j + (d + 1))
                        pool.wait_ge(xx_pool, m + 2)
                        pool.tensor_tensor(PM[:, d], ATS[:, d], bc(LM[:, 0, 1 - d, :], 2), ALU.mult).then_inc(
                            xx_pool, 1)
                        pool.wait_ge(xx_pool, m + 3)
                        pool.tensor_tensor(XX[:, d, 1], bc(IDENT, 2), PM[:, d], ALU.subtract).then_inc(xx_pool, 1)
                        pool.wait_ge(xx_pool, m + 4)
                        pool.sem_inc(xx_init, 1)
                    for d in range(2):
                        c = 7 - s if d else s
                        if s:
                            pool.wait_ge(dstate_ps, j + (d - 1))
                        gate(pool, "pool")
                        for h in range(2):
                            hh = slice(64 * h, 64 * h + 64)
                            pool.tensor_scalar(VB[:, d, h, :], VND[:, c, hh], PC[:, 2, d, c, h:h + 1], None, ALU.mult)
                            pool.tensor_scalar(KBE[:, d, h, :], KN[:, c, hh], PC[:, 3, d, c, h:h + 1], None, ALU.mult)
                            i = pool.tensor_scalar(KDC[:, d, h, :], KN[:, c, hh], PC[:, 4, d, c, h:h + 1], None, ALU.mult)
                        i.then_inc(sc_ready, 1)
                pool.wait_ge(o_read, p * 16 + 16)
                pool.tensor_tensor(OD[0][:, :, :], OD[0][:, :, :], OD[1][:, :, :], ALU.add).then_inc(o_sum, 1)

        def oa_split(act, pool, n0):
            if act:
                act.wait_ge(oa_done, NPAIR)
                for p in range(NPAIR):
                    act.activation(YH[:, p, :], OA[:, p, :], ACT.Copy).then_inc(yh_ready, 1)
            if pool:
                for p in range(NPAIR):
                    pool.wait_ge(yh_ready, n0 + p + 1)
                    pool.tensor_tensor(YL[:, p, :], OA[:, p, :], YH[:, p, :].bitcast(F32),
                                       ALU.subtract).then_inc(yl_ready, 1)

        ms_hi, ms_lo = sem("ms_hi"), sem("ms_lo")

        def mx_split(act, pool, n0, src, free):
            if act:
                act.wait_ge(mm_done, free)
                for k in range(KD):
                    act.activation(XH[:, k, :], src[:, k, :], ACT.Copy).then_inc(ms_hi, 1)
            if pool:
                for k in range(KD):
                    pool.wait_ge(ms_hi, n0 + k + 1)
                    pool.tensor_tensor(XL[:, k, :], src[:, k, :], XH[:, k, :].bitcast(F32),
                                       ALU.subtract).then_inc(ms_lo, 1)

        def plain_pe(pe, name, hi, lo):
            with pe.Fori(0, 4) as m:
                for i in range(2):
                    product(pe, Block(name, m, i), hi, lo)

        def add_blocks_dve(dve, name, dst):
            with dve.Fori(0, 4) as m:
                for i in range(2):
                    b = Block(name, m, i)
                    dve.wait_ge(mm_done, b.n + 1)
                    o = dst[:, ds(m * 2 + i, 1), :].rearrange("p a n -> p (a n)")
                    dve.tensor_tensor(o, o, DP[b.slot][:, :], ALU.add).then_inc(psum_free[b.slot], 1)

        TG, TU = at("TG", S0, [P, T]), at("TU", S0 + 4, [P, T])
        HB = at("HB", S0 + 8, [P, 2, T])
        FH, FL = at("FH", S0 + 16, [P, 2, T], F32R), at("FL", S0 + 24, [P, 2, T], F32R)
        fc_mid, fc_dve, fg_silu, hb_ready, fh_ready, fl_ready = (sem(n) for n in (
            "fc_mid", "fc_dve", "fg_silu", "hb_ready", "fh_ready", "fl_ready"))

        def ffn_block(f, t, part):
            if isinstance(f, int):
                return Block("ffn0", 0, 2 * t + part)
            it, _ = f
            return Block("ffn", it, (0 if t == 0 else 10) + part)

        def ffn_down(f):
            return [Block("ffn1", 0, m) for m in range(8)] if f is None else [Block("ffn", f, 2 + m) for m in range(8)]

        def ffn_pe(pe):
            def down(bs, f):
                pe.wait_ge(fl_ready, f * 2 + 2)
                for b in bs:
                    product(pe, b, FH, FL)

            for i in range(4):
                product(pe, Block("ffn0", 0, i), XH, XL)
            with pe.Fori(0, FT // 2 - 1) as it:
                for i in range(2):
                    product(pe, ffn_block((it, 1), 0, i), XH, XL)
                down(ffn_down(it), it)
                for i in range(2):
                    product(pe, ffn_block((it, 1), 1, i), XH, XL)
            down(ffn_down(None), FT // 2 - 1)

        def ffn_tile(act, dve, blocks_of, f, t):
            n = f * 2 + t
            if act:
                for part, dst in enumerate((TG, TU)):
                    b = blocks_of[part]
                    act.wait_ge(mm_done, b.n + 1)
                    act.wait_ge(hb_ready, n)
                    act.activation(dst[:, :], DP[b.slot][:, :], ACT.Copy,
                                   scale=COL[:, ds(f * 2 + (COLS["ffnconv"] + 44 + 22 * part + t), 1)]).then_inc(
                        fc_mid, 1)
                act.wait_ge(fc_dve, n * 4 + 2)
                act.activation(TG[:, :], TG[:, :], ACT.Silu).then_inc(fg_silu, 1)
            if dve:
                for part, dst in enumerate((TG, TU)):
                    b = blocks_of[part]
                    dve.wait_ge(fc_mid, n * 2 + (part + 1))
                    for i, tap in enumerate((0, 2)):
                        d = dst[:, 1:T] if tap == 0 else dst[:, 0:T - 1]
                        src = DP[b.slot][:, 0:T - 1] if tap == 0 else DP[b.slot][:, 1:T]
                        dve.scalar_tensor_tensor(
                            out=d, in0=src, scalar=COL[:, ds(f * 2 + (COLS["ffnconv"] + 44 * tap + 22 * part + t), 1)],
                            in1=d, op0=ALU.mult, op1=ALU.add).then_inc(fc_dve, 1)
                        dve.wait_ge(fc_dve, n * 4 + (2 * part + i + 1))
                    dve.sem_inc(psum_free[b.slot], 1)
                dve.wait_ge(fg_silu, n + 1)
                if t == 0 and not (isinstance(f, int) and f == 0) or t == 1:
                    dve.wait_ge(fl_ready, n - 1)
                dve.tensor_tensor(HB[:, t, :], TG[:, :], TU[:, :], ALU.mult).then_inc(hb_ready, 1)

        def ffn_split(act, pool, f, t, free):
            n = f * 2 + t
            if act:
                act.wait_ge(hb_ready, n + 1)
                if free is not None:
                    act.wait_ge(mm_done, free)
                act.activation(FH[:, t, :], HB[:, t, :], ACT.Copy).then_inc(fh_ready, 1)
            if pool:
                pool.wait_ge(fh_ready, n + 1)
                pool.tensor_tensor(FL[:, t, :], HB[:, t, :], FH[:, t, :].bitcast(F32), ALU.subtract).then_inc(
                    fl_ready, 1)

        def ffn_act(act):
            for t in range(2):
                ffn_tile(act, None, [ffn_block(0, t, i) for i in range(2)], 0, t)
                ffn_split(act, None, 0, t, None)
            with act.Fori(0, FT // 2 - 1) as it:
                done = Block("ffn", it, 9).n + 1
                for t in range(2):
                    ffn_tile(act, None, [ffn_block((it, 1), t, i) for i in range(2)], it + 1, t)
                    ffn_split(act, None, it + 1, t, done)

        def ffn_pool(pool):
            for i in range(4):
                split(pool, Block("ffn0", 0, i))
                if i % 2 == 1:
                    ffn_split(None, pool, 0, i // 2, None)
            with pool.Fori(0, FT // 2 - 1) as it:
                for i in range(12):
                    split(pool, Block("ffn", it, i))
                    if i in (10, 11):
                        ffn_split(None, pool, it + 1, i - 10, None)

        def ffn_dve(dve):
            def add(b, m):
                dve.wait_ge(mm_done, b.n + 1)
                dve.tensor_tensor(XR[:, m, :], XR[:, m, :], DP[b.slot][:, :], ALU.add).then_inc(psum_free[b.slot], 1)

            for t in range(2):
                ffn_tile(None, dve, [ffn_block(0, t, i) for i in range(2)], 0, t)
            with dve.Fori(0, FT // 2 - 1) as it:
                ffn_tile(None, dve, [ffn_block((it, 1), 0, i) for i in range(2)], it + 1, 0)
                for m, b in enumerate(ffn_down(it)):
                    if m == 0:
                        pass
                    add(b, m)
                ffn_tile(None, dve, [ffn_block((it, 1), 1, i) for i in range(2)], it + 1, 1)
            for m, b in enumerate(ffn_down(None)):
                add(b, m)

        NP5 = 16
        S5P = at("S5P", 0, [P, 3 * 16 + 4 * 256])
        SM = at("SM", 5, [P, 40, 16])
        BZ = at("BZ", 8, [P, 2, NP5, 16])
        PW = at("PW", 10, [P, 2, 9, 16])
        PD = at("PD", 11.25, [P, 2, 9, 16])
        T1, T2 = at("T1", 12.5, [P, NP5, 8, 16]), at("T2", 20.5, [P, NP5, 8, 16])
        XB = at("XB", 28.5, [P, 2, NP5, 8, 16])
        W1 = at("W1", 44.5, [P, 2, NP5, P])
        CA = at("CA", 96, [P, 2, NP5, 8, 16])
        KL = at("KL", 112, [P, 2, NP5, 8, 16])
        KS = at("KS", S0, [16, NP5, 2, P])
        ZT = at("ZT", S0 + 16, [16, P])
        EP = at("EP", S0 + 17, [P, 2, 129, 16])
        w1_dram = nc.dram_tensor("w1_dram", [P, 2, NP5, P], F32, kind="Internal").ap()
        ca_dram = nc.dram_tensor("ca_dram", [P, 2, NP5, P], F32, kind="Internal").ap()
        ep_dram = nc.dram_tensor("ep_dram", [P, 2, 129 * 16], F32, kind="Internal").ap()
        r8_dram = nc.dram_tensor("r8_dram", [P, 16], F32, kind="Internal").ap()
        kp_dram = nc.dram_tensor("kp_dram", [16, 32, 256], F32, kind="Internal").ap()
        x2_dram = nc.dram_tensor("x2_dram", [P, KD, T], F32, kind="Internal").ap()
        s5p_in, pr_chain, pr_dt, pr_angle, pr_act, pr_xb, pr_ca, pr_kl, pr_ep = (once(n) for n in (
            "s5p_in", "pr_chain", "pr_dt", "pr_angle", "pr_act", "pr_xb", "pr_ca", "pr_kl", "pr_ep"))
        pr_w1t, pr_w1, pr_kps, pr_ks, pr_zero, pr_out = (once(n) for n in (
            "pr_w1t", "pr_w1", "pr_kps", "pr_ks", "pr_zero", "pr_out"))
        HALF = [x[:, i * H:i * H + H] for x in BANKS for i in range(2)]
        are, aim, ldt = (S5P[:, 16 * i:16 * i + 16] for i in range(3))
        Bre, Bim, Cre, Cim = (S5P[:, 48 + 256 * i:48 + 256 * i + 256].rearrange("p (t c) -> p t c", c=16)
                              for i in range(4))

        def prep_sp(sp):
            sp.wait_ge(pr_w1, 8)
            sp.dma_start(w1_dram, W1[:, :, :, :]).then_inc(pr_out, 16)
            sp.wait_ge(pr_ca, 1)
            sp.dma_start(ca_dram, CA[:, :, :, :, :].rearrange("p r t j c -> p r t (j c)")).then_inc(pr_out, 16)
            sp.wait_ge(pr_ep, 1)
            sp.dma_start(ep_dram, EP[:, :, :, :].rearrange("p r c t -> p r (c t)")).then_inc(pr_out, 16)
            sp.dma_start(r8_dram, SM[:, 8, :]).then_inc(pr_out, 16)
            sp.wait_ge(pr_zero, 1)
            sp.dma_start(kp_dram[:, :, 0:P],
                         ZT[:, :].rearrange("p (a k) -> p a k", a=1).broadcast_to([16, 32, P])).then_inc(pr_out, 16)
            sp.wait_ge(pr_ks, 8)
            sp.dma_start(kp_dram[:, :, P:256], KS[:, :, :, :].rearrange("p t g n -> p (t g) n")).then_inc(pr_out, 16)

        def prep_act(act):
            act.wait_ge(s5p_in, 16)
            act.activation(SM[:, 0, :], ldt, ACT.Exp).then_inc(pr_dt, 1)
            act.wait_ge(pr_angle, 1)
            act.activation(SM[:, 7, :], SM[:, 1, :], ACT.Exp)
            act.activation(SM[:, 8, :], SM[:, 1, :], ACT.Exp, scale=8.0)
            act.activation(SM[:, 9, :], SM[:, 1, :], ACT.Tanh, scale=0.5)
            act.activation(SM[:, 10:12, :], SM[:, 4:6, :], ACT.Sin, scale=0.5)
            act.activation(SM[:, 12:14, :], SM[:, 4:6, :], ACT.Sin).then_inc(pr_act, 1)
            for n in range(8):
                act.wait_ge(pr_w1t, n + 1)
                act.activation(W1[:, n // 4, 4 * (n % 4):4 * (n % 4) + 4, :].rearrange("p t n -> p (t n)"), HALF[n],
                               ACT.Copy).then_inc(pr_w1, 1)
            for n in range(8):
                act.wait_ge(pr_kps, n + 1)
                act.activation(KS[:, 4 * (n // 2):4 * (n // 2) + 4, n % 2, :],
                               HALF[n][0:16, :].rearrange("p (t n) -> p t n", t=4), ACT.Copy).then_inc(pr_ks, 1)

        def prep_pe(pe):
            pe.wait_ge(pr_xb, 1)
            for n in range(8):
                for i in range(4):
                    t = 4 * (n % 4) + i
                    tr = pe.transpose(HALF[n][:, P * i:P * i + P], XB[:, n // 4, t].rearrange("p j c -> p (j c)"),
                                      IDENT)
                tr.then_inc(pr_w1t, 1)
            pe.wait_ge(pr_w1, 8)
            pe.wait_ge(pr_kl, 1)
            for n in range(8):
                g = n % 2
                r = slice(64 * g, 64 * g + 64)
                for i in range(4):
                    t = 4 * (n // 2) + i
                    for ri in range(2):
                        mm = pe.matmul(HALF[n][0:16, P * i:P * i + P], BZ[r, ri, t, :],
                                       KL[r, ri, t].rearrange("p j c -> p (j c)"), start=(ri == 0), stop=(ri == 1))
                mm.then_inc(pr_kps, 1)

        def prep_dve(dve):
            n = [0]

            def link(ins):
                n[0] += 1
                ins.then_inc(pr_chain, 1)
                dve.wait_ge(pr_chain, n[0])

            def tt(o, x, y, op):
                link(dve.tensor_tensor(o, x, y, op))

            dve.memset(ZT[:, :], 0.0).then_inc(pr_zero, 1)
            s = lambda i: SM[:, i, :]
            dve.wait_ge(s5p_in, 16)
            dve.wait_ge(pr_dt, 1)
            tt(s(1), are, s(0), ALU.mult)
            tt(s(2), aim, s(0), ALU.mult)
            link(dve.tensor_scalar(s(3), s(2), 8.0, None, ALU.mult))
            magic = 12582912.0
            c1, c2 = 6.28125, 2029.0 / 2 ** 20
            c3 = 2 * np.pi - c1 - c2
            k, ph = SM[:, 14:16, :], SM[:, 4:6, :]
            link(dve.tensor_scalar(k, SM[:, 2:4, :], 1 / (2 * np.pi), magic, ALU.mult, ALU.add))
            link(dve.tensor_scalar(k, k, magic, None, ALU.subtract))
            link(dve.scalar_tensor_tensor(out=ph, in0=k, scalar=-c1, in1=SM[:, 2:4, :], op0=ALU.mult, op1=ALU.add))
            link(dve.scalar_tensor_tensor(out=ph, in0=k, scalar=-c2, in1=ph, op0=ALU.mult, op1=ALU.add))
            link(dve.scalar_tensor_tensor(out=ph, in0=k, scalar=-c3, in1=ph, op0=ALU.mult, op1=ALU.add))
            link(dve.tensor_scalar(ph, ph, 3.1415925, -3.1415925, ALU.min, ALU.max))
            dve.sem_inc(pr_angle, 1)
            dve.wait_ge(pr_act, 1)
            link(dve.scalar_tensor_tensor(out=SM[:, 16:18, :], in0=SM[:, 10:12, :], scalar=-2.0,
                                          in1=SM[:, 10:12, :], op0=ALU.mult, op1=ALU.mult))
            link(dve.tensor_scalar(SM[:, 18:20, :], SM[:, 16:18, :], 1.0, None, ALU.add))
            link(dve.tensor_scalar(s(20), s(9), -1.0, 1.0, ALU.mult, ALU.add))
            link(dve.reciprocal(s(20), s(20)))
            link(dve.scalar_tensor_tensor(out=s(20), in0=s(9), scalar=2.0, in1=s(20), op0=ALU.mult, op1=ALU.mult))
            tt(s(21), s(7), s(18), ALU.mult)
            tt(s(22), s(7), s(12), ALU.mult)
            tt(s(23), s(20), s(18), ALU.mult)
            tt(s(23), s(23), s(16), ALU.add)
            tt(s(24), are, are, ALU.mult)
            tt(s(25), aim, aim, ALU.mult)
            tt(s(24), s(24), s(25), ALU.add)
            link(dve.reciprocal(s(24), s(24)))
            tt(s(25), s(23), are, ALU.mult)
            tt(s(26), s(22), aim, ALU.mult)
            tt(s(25), s(25), s(26), ALU.add)
            tt(s(25), s(25), s(24), ALU.mult)
            tt(s(26), s(22), are, ALU.mult)
            tt(s(27), s(23), aim, ALU.mult)
            tt(s(26), s(26), s(27), ALU.subtract)
            tt(s(26), s(26), s(24), ALU.mult)

            def cmul(ore, oim, xre, xim, yre, yim, t1, t2, sign=1):
                tt(ore, xre, yre, ALU.mult)
                tt(t1, xim, yim, ALU.mult)
                tt(ore, ore, t1, ALU.subtract)
                tt(oim, xre, yim, ALU.mult)
                tt(t2, xim, yre, ALU.mult)
                if sign > 0:
                    tt(oim, oim, t2, ALU.add)
                else:
                    link(dve.scalar_tensor_tensor(out=oim, in0=oim, scalar=-1.0, in1=t2, op0=ALU.mult,
                                                  op1=ALU.subtract))

            def over(v, m):
                return v.rearrange("p (t k) -> p t k", k=1).broadcast_to([P, 16, m])

            t1, t2 = T1[:, :, 0, :], T2[:, :, 0, :]
            cmul(BZ[:, 0], BZ[:, 1], over(s(25), 16), over(s(26), 16), Bre, Bim, t1, t2)
            link(dve.memset(PW[:, 0, 0, :], 1.0))
            link(dve.memset(PW[:, 1, 0, :], 0.0))
            link(dve.tensor_copy(PW[:, 0, 1, :], s(21)))
            link(dve.tensor_copy(PW[:, 1, 1, :], s(22)))
            for m in (1, 2, 4):
                y = [PW[:, ri, m:m + 1, :].broadcast_to([P, m, 16]) for ri in range(2)]
                cmul(PW[:, 0, m + 1:2 * m + 1, :], PW[:, 1, m + 1:2 * m + 1, :], PW[:, 0, 1:m + 1, :],
                     PW[:, 1, 1:m + 1, :], y[0], y[1], T1[:, 0, 0:m, :], T2[:, 0, 0:m, :])
            for ri in range(2):
                for m in range(9):
                    link(dve.tensor_copy(PD[:, ri, m, :], PW[:, ri, 8 - m, :]))

            def power(src, ri, lo):
                return src[:, ri, lo:lo + 8, :].rearrange("p (k a) t -> p t k a", a=1).broadcast_to([P, 16, 8, 16])

            def coef(v):
                return v.rearrange("p t (a c) -> p t a c", a=1).broadcast_to([P, 16, 8, 16])

            cmul(XB[:, 0], XB[:, 1], power(PD, 0, 1), power(PD, 1, 1), coef(BZ[:, 0]), coef(BZ[:, 1]), T1[:, :], T2[:, :])
            dve.sem_inc(pr_xb, 1)
            cmul(CA[:, 0], CA[:, 1], power(PW, 0, 1), power(PW, 1, 1), coef(Cre), coef(Cim), T1[:, :], T2[:, :], -1)
            dve.sem_inc(pr_ca, 1)
            cmul(KL[:, 0], KL[:, 1], power(PW, 0, 0), power(PW, 1, 0), coef(Cre), coef(Cim), T1[:, :], T2[:, :], -1)
            dve.sem_inc(pr_kl, 1)
            link(dve.memset(EP[:, 0, 0, :], 1.0))
            link(dve.memset(EP[:, 1, 0, :], 0.0))
            link(dve.tensor_copy(EP[:, 0, 1, :], s(19)))
            link(dve.tensor_copy(EP[:, 1, 1, :], s(13)))
            m = 1
            f1 = T1[:, :, :, :].rearrange("p t j c -> p (t j) c")
            f2 = T2[:, :, :, :].rearrange("p t j c -> p (t j) c")
            while m < P:
                y = [EP[:, ri, m:m + 1, :].broadcast_to([P, m, 16]) for ri in range(2)]
                cmul(EP[:, 0, m + 1:2 * m + 1, :], EP[:, 1, m + 1:2 * m + 1, :], EP[:, 0, 1:m + 1, :],
                     EP[:, 1, 1:m + 1, :], y[0], y[1], f1[:, 0:m, :], f2[:, 0:m, :])
                m *= 2
            dve.sem_inc(pr_ep, 1)


        c1 = NormCount()
        c2 = NormCount()
        c2.sq, c2.ss, c2.nt = KD + 2 * NG * NPAIR, 1 + 2 * NG * NPAIR, KD
        c3 = NormCount()
        c3.sq, c3.ss, c3.nt = c2.sq + KD, c2.ss + 1, c2.nt + KD
        c4 = NormCount()
        c4.sq, c4.ss, c4.nt = c3.sq + KD, c3.ss + 1, c3.nt + KD

        with nc.Block() as block:
            @block.sync
            def _(sp):
                sp.dma_start(COL[:, :], a["cols"]).then_inc(con_in, 16)
                sp.dma_start(CON[:, :], a["cst"]).then_inc(con_in, 16)
                sp.dma_start(S5P[:, :], a["s5p"]).then_inc(s5p_in, 16)
                sp.dma_start(XR[:, :, :], a["x"]).then_inc(x_in, 16)
                prep_sp(sp)
                sp.wait_ge(pr_out, 96)
                sp.dma_start(BIAS[:, :], a["bias"]).then_inc(bias_in, 16)
                sp.dma_start(SEL[:, :, :], a["sel"]).then_inc(sel_in, 16)
                with sp.Fori(0, NPAIR) as p:
                    for i in range(9):
                        load(sp, Block("attn", p, i), a["w_attn"])
                with sp.Fori(0, 8) as m:
                    load(sp, Block("mixb", m, 0), a["w_gateb"], m)
                    load(sp, Block("mixb", m, 1), a["w_attnout"], m)
                sp.wait_ge(mx_done, 8)
                sp.dma_start(LM[:, :, :, :], a["levels"]).then_inc(lm_in, 16)
                load(sp, Block("dnab", 0, 0), a["w_ab"])
                with sp.Fori(0, NPAIR) as p:
                    for i in range(4):
                        load(sp, Block("dn", p, i), a["w_dn"])
                with sp.Fori(0, 8) as m:
                    load(sp, Block("mixa", m, 0), a["w_gatea"], m)
                    load(sp, Block("mixa", m, 1), a["w_dnout"], m)
                sp.wait_ge(mm_done, last_block("mixa"))
                sp.wait_ge(yl_ready, 8)
                sp.dma_start(XR[:, :, :], a["x"]).then_inc(x_in, 16)
                with sp.Fori(0, 4) as m:
                    for i in range(2):
                        load(sp, Block("wo", m, i), a["w_o"])
                for i in range(4):
                    load(sp, Block("ffn0", 0, i), a["w_up"], i)
                with sp.Fori(0, FT // 2 - 1) as it:
                    for i in range(2):
                        load(sp, Block("ffn", it, i), a["w_up"], it * 4 + (4 + i))
                    for m in range(8):
                        load(sp, Block("ffn", it, 2 + m), a["w_down"], it * 8 + m)
                    for i in range(2):
                        load(sp, Block("ffn", it, 10 + i), a["w_up"], it * 4 + (6 + i))
                for m in range(8):
                    load(sp, Block("ffn1", 0, m), a["w_down"], 80 + m)

            @block.gpsimd
            def _(pool):
                pool.wait_ge(pr_out, 96)
                norm_pool(pool, c1)
                with pool.Fori(0, NPAIR) as p:
                    for i in range(9):
                        split(pool, Block("attn", p, i))
                comb_pool(pool)
                with pool.Fori(0, 8) as m:
                    split(pool, Block("mixb", m, 0))
                    split(pool, Block("mixb", m, 1))
                delta_pool(pool)
                oa_split(None, pool, 4)
                with pool.Fori(0, 8) as m:
                    split(pool, Block("mixa", m, 0))
                    split(pool, Block("mixa", m, 1))
                mx_split(None, pool, 0, MX, None)
                with pool.Fori(0, 4) as m:
                    for i in range(2):
                        split(pool, Block("wo", m, i))
                norm_pool(pool, c2)
                ffn_pool(pool)
                for m in range(8):
                    split(pool, Block("ffn1", 0, m))

            @block.scalar
            def _(act):
                act.wait_ge(con_in, 32)
                act.wait_ge(x_in, 16)
                prep_act(act)
                act.wait_ge(pr_out, 96)
                norm_act(act, c1, XR)
                attn_act(act)
                comb_act(act)
                act.wait_ge(st_w, NG)
                mix_act(act, "mixb", 0)
                delta_act(act)
                oa_split(act, None, 4)
                mix_act(act, "mixa", 8)
                act.wait_ge(mx_done, 16)
                mx_split(act, None, 0, MX, last_block("mixa"))
                freed(act, Block("wo", 3, 0))
                freed(act, Block("wo", 3, 1))
                norm_act(act, c2, XR)
                ffn_act(act)
                freed(act, Block("ffn1", 0, 6))
                freed(act, Block("ffn1", 0, 7))

            @block.vector
            def _(dve):
                dve.wait_ge(con_in, 32)
                dve.wait_ge(x_in, 16)
                prep_dve(dve)
                dve.wait_ge(pr_out, 96)
                norm_dve(dve, c1, XR, "norm1")
                attn_dve(dve)
                comb_dve(dve)
                dve.wait_ge(og_sum, 2 * NPAIR)
                mix_dve(dve, "mixb", 0, False, True)
                delta_dve(dve)
                dve.wait_ge(yh_ready, 8)
                mix_dve(dve, "mixa", 8, True, False)
                dve.wait_ge(x_in, 32)
                add_blocks_dve(dve, "wo", XR)
                norm_dve(dve, c2, XR, "norm2")
                ffn_dve(dve)

            @block.tensor
            def _(pe):
                pe.wait_ge(con_in, 32)
                prep_pe(pe)
                pe.wait_ge(pr_ks, 8)
                norm_pe(pe, c1)
                pe.wait_ge(xh_ready, KD)
                pe.wait_ge(nt_used, KD)
                attn_pe(pe)
                comb_pe(pe)
                pe.wait_ge(wb_used, NPAIR * NG)
                pe.wait_ge(yl_ready, 4)
                mix_pe(pe, "mixb")
                delta_pe(pe)
                pe.wait_ge(oa_done, NPAIR)
                pe.wait_ge(yl_ready, 8)
                mix_pe(pe, "mixa")
                pe.wait_ge(ms_hi, KD)
                pe.wait_ge(ms_lo, KD)
                plain_pe(pe, "wo", XH, XL)
                norm_pe(pe, c2)
                pe.wait_ge(xh_ready, c2.nt + KD)
                pe.wait_ge(nt_used, c2.nt + KD)
                ffn_pe(pe)


        nc.clear_and_free_semaphores(first)
        nc.all_engine_barrier()
        X5 = at("X5", 96, [P, 32, 8, 16])
        U5 = at("U5", 112, [P, 32, P])
        E5 = at("E5", S0, [P, 2, 129, 16])
        QZ = at("QZ", S0 + 16.5, [P, 2, NP5, P])
        D0 = at("D0", S0 + 32.5, [P, NP5, P])
        SV = [at(f"SV{i}", S0 + 32.5 + 4 * i, [P, 2, 4, P]) for i in range(2)]
        MS = at("MS", S0 + 40.5, [P, 8, P])
        DROW = at("DROW", 64, [P, 32, 16])
        F1, F2 = at("F1", 66, [P, 4, P]), at("F2", 68, [P, 4, P])
        WS = [at(f"WS{i}", 70 + 4 * i, [P, 2, 4, P]) for i in range(2)]
        G5 = at("G5", 80, [P, NPAIR, T])
        R8 = at("R8", 153.25, [P, 16])
        YH5 = at("YH5", S0 + 20, [P, NPAIR, T], F32R)
        YL5 = at("YL5", 64, [P, NPAIR, T], F32R)
        s5_in, ws_in, ms_in, x2_out = [sem("s5_in"), [sem("ws_in0"), sem("ws_in1")], sem("ms_in"), sem("x2_out")]
        x5_ready, g5_ready, d0_ready, ut, u5_ready, u5_dve, x5_scaled, p_ps, q_ready, q_chain, z_done = (
            sem(n) for n in ("x5_ready", "g5_ready", "d0_ready", "ut", "u5_ready", "u5_dve", "x5_scaled", "p_ps",
                             "q_ready", "q_chain", "z_done"))
        sv_ready, y_ps, y_ready, ge_ready, yt, yh5_ready, yl5_ready = (sem(n) for n in (
            "sv_ready", "y_ps", "y_ready", "ge_ready", "yt", "yh5_ready", "yl5_ready"))
        ga_ready, g5_mul, g5_done = sem("ga_ready"), sem("g5_mul"), sem("g5_done")

        def s5_sp(sp):
            sp.dma_start(x2_dram, XR[:, :, :]).then_inc(x2_out, 16)
            sp.wait_ge(nt_used, c3.nt + KD)
            sp.wait_ge(xh_ready, c3.nt + KD)
            sp.dma_start(E5[:, :, :, :].rearrange("p r c t -> p r (c t)"), ep_dram).then_inc(s5_in, 16)
            sp.dma_start(R8[:, :], r8_dram).then_inc(s5_in, 16)
            sp.wait_ge(x2_out, 16)
            sp.dma_start(DROW[:, :, :].rearrange("p g c -> p (g c)"), a["s5d"].broadcast_to([P, 512])).then_inc(
                s5_in, 16)

        def s5_sp_stream(sp):
            for b in range(8):
                if b >= 2:
                    if b < 6:
                        sp.wait_ge(p_ps, b - 1)
                    else:
                        sp.wait_ge(y_ps, b - 5)
                src = (w1_dram, ca_dram)[b // 4]
                sp.dma_start(WS[b % 2][:, :, :, :], src[:, :, 4 * (b % 4):4 * (b % 4) + 4, :]).then_inc(
                    ws_in[b % 2], 16)
                if b >= 4:
                    m = b - 4
                    if m:
                        sp.wait_ge(y_ps, m)
                    for j in range(8):
                        sp.dma_start(MS[16 * j:16 * j + 16, :, :],
                                     kp_dram[:, 8 * m:8 * m + 8, P - 16 * j:256 - 16 * j]).then_inc(ms_in, 16)

        def s5_pe(pe):
            with pe.Fori(0, 2) as m:
                for i in range(2):
                    b = Block("s5x", m, i)
                    pe.wait_ge(w_split, b.n + 1)
                    pe.wait_ge(psum_free[b.slot], b.loads - 1)
                    for j in range(8):
                        for k in range(KD):
                            for x, w, one, end in ((XH, WH, k == 0, False), (XL, WH, False, False),
                                                   (XH, WL, False, k == KD - 1)):
                                mm = pe.matmul(DP[b.slot][:, P * j:P * j + P],
                                               x[:, k, :].rearrange("p (s j) -> p j s", j=8)[:, j, :],
                                               w[b.slot][:, k, :], start=one, stop=end)
                    mm.then_inc(mm_done, 1)
            with pe.Fori(0, 2) as m:
                for i in range(2):
                    product(pe, Block("s5g", m, i), XH, XL)
            freed(pe, Block("s5g", 1, 0))
            freed(pe, Block("s5g", 1, 1))
            pe.wait_ge(x5_ready, 4)
            for n in range(8):
                for i in range(4):
                    tr = pe.transpose(HALF[n][:, P * i:P * i + P], X5[:, 4 * n + i].rearrange("p j c -> p (j c)"),
                                      IDENT)
                tr.then_inc(ut, 1)
            pe.wait_ge(u5_ready, 4)
            pe.wait_ge(u5_dve, 4)
            for b in range(4):
                pe.wait_ge(ws_in[b % 2], 16 * (b // 2 + 1))
                for ri in range(2):
                    for i in range(4):
                        for g in range(2):
                            mm = pe.matmul(HALF[2 * b + ri][64 * g:64 * g + 64, P * i:P * i + P],
                                           WS[b % 2][:, ri, i, 64 * g:64 * g + 64], U5[:, 2 * (4 * b + i) + g, :],
                                           start=True, stop=True)
                mm.then_inc(p_ps, 1)
            for b in range(4):
                pe.wait_ge(ws_in[b % 2], 16 * (b // 2 + 3))
                pe.wait_ge(ms_in, 128 * (b + 1))
                pe.wait_ge(sv_ready, b + 1)
                for g in range(2):
                    r = slice(64 * g, 64 * g + 64)
                    for i in range(4):
                        o = HALF[2 * b + g][:, P * i:P * i + P]
                        pe.matmul(o, U5[:, 2 * (4 * b + i) + g, :], MS[:, 2 * i + g, :], start=True, stop=False)
                        pe.matmul(o, SV[b % 2][r, 0, i, :], WS[b % 2][r, 0, i, :], start=False, stop=False)
                        mm = pe.matmul(o, SV[b % 2][r, 1, i, :], WS[b % 2][r, 1, i, :], start=False, stop=True)
                mm.then_inc(y_ps, 1)
            for b in range(4):
                pe.wait_ge(ge_ready, b + 1)
                for j in range(8):
                    tr = pe.transpose(BANKS[b][:, P * j:P * j + P], U5[:, 8 * b + j, :], IDENT)
                tr.then_inc(yt, 1)
            pe.wait_ge(yh5_ready, 4)
            pe.wait_ge(yl5_ready, 4)
            with pe.Fori(0, 4) as m:
                for i in range(2):
                    product(pe, Block("glu", m, i), YH5, YL5)

        def s5_act(act):
            with act.Fori(0, 2) as m:
                for i in range(2):
                    b = Block("s5x", m, i)
                    act.wait_ge(mm_done, b.n + 1)
                    act.activation(X5[:, ds(m * 16 + 8 * i, 8)].rearrange("p g j c -> p j g c"),
                                   DP[b.slot][:, :].rearrange("p (j g c) -> p j g c", j=8, g=8), ACT.Copy).then_inc(
                        x5_ready, 1)
                    act.wait_ge(x5_ready, m * 2 + (i + 1))
                    act.sem_inc(psum_free[b.slot], 1)
            with act.Fori(0, 2) as m:
                for i in range(2):
                    b = Block("s5g", m, i)
                    act.wait_ge(mm_done, b.n + 1)
                    act.wait_ge(x2_out, 16)
                    act.activation(G5[:, ds(m * 2 + i, 1), :].rearrange("p a n -> p (a n)"), DP[b.slot][:, :],
                                   ACT.Silu).then_inc(psum_free[b.slot], 1)
            for n in range(0, 8, 2):
                act.wait_ge(ut, n + 1)
                act.activation(U5[:, 4 * n:4 * n + 4, :].rearrange("p t n -> p (t n)"), HALF[n], ACT.Copy).then_inc(
                    u5_ready, 1)
            for b in range(4):
                act.wait_ge(y_ready, 2 * b + 2)
                act.activation(U5[:, 8 * b:8 * b + 8, :].rearrange("p j (g c) -> p g j c", g=8),
                               X5[:, 8 * b:8 * b + 8], ACT.Gelu_apprx_tanh).then_inc(ge_ready, 1)
            act.wait_ge(z_done, 2)
            act.wait_ge(sv_ready, 4)
            for b in range(4):
                act.wait_ge(yt, b + 1)
                act.activation(YH5[:, b, :].rearrange("p (s j) -> p j s", j=8),
                               BANKS[b][:, :].rearrange("p (j s) -> p j s", j=8), ACT.Copy).then_inc(yh5_ready, 1)
            act.wait_ge(yh5_ready, 4)
            with act.Fori(0, 4) as m:
                b = Block("glu", m, 1)
                act.wait_ge(mm_done, b.n + 1)
                act.wait_ge(g5_mul, m)
                act.activation(SG[0][:, :], DP[b.slot][:, :], ACT.Sigmoid).then_inc(ga_ready, 1)
                act.wait_ge(ga_ready, m + 1)
                act.sem_inc(psum_free[b.slot], 1)
            act.wait_ge(g5_done, 4)
            act.wait_ge(mm_done, last_block("glu"))
            for p in range(NPAIR):
                act.activation(YH[:, p, :], G5[:, p, :], ACT.Copy).then_inc(yh_ready, 1)

        def s5_dve(dve):
            dve.wait_ge(s5_in, 48)
            dve.tensor_copy(D0[:, :, :], R8[:, :].rearrange("p (t k) -> p t k", k=1).broadcast_to([P, NP5, P])).then_inc(
                d0_ready, 1)
            dve.wait_ge(d0_ready, 1)
            dve.memset(D0[:, :, 0:1], 0.0).then_inc(d0_ready, 1)
            for n in range(1, 8, 2):
                dve.wait_ge(ut, n + 1)
                dve.tensor_copy(U5[:, 4 * n:4 * n + 4, :].rearrange("p t n -> p (t n)"), HALF[n]).then_inc(u5_dve, 1)
            c = [0]

            def link(ins):
                c[0] += 1
                ins.then_inc(q_chain, 1)
                dve.wait_ge(q_chain, c[0])

            def phase(ri, b, lo, hi):
                return E5[:, ri, lo:hi, 4 * b:4 * b + 4].rearrange("p c t -> p t c")

            for b in range(4):
                dve.wait_ge(p_ps, b + 1)
                pr, pi = (HALF[2 * b + ri].rearrange("p (t n) -> p t n", t=4) for ri in range(2))
                er, ei = phase(0, b, 1, 129), phase(1, b, 1, 129)
                qr, qi = QZ[:, 0, 4 * b:4 * b + 4, :], QZ[:, 1, 4 * b:4 * b + 4, :]
                dve.tensor_tensor(qr, pr, er, ALU.mult)
                dve.tensor_tensor(F1[:, :, :], pi, ei, ALU.mult)
                dve.tensor_tensor(qi, pi, er, ALU.mult)
                link(dve.tensor_tensor(F2[:, :, :], pr, ei, ALU.mult))
                dve.tensor_tensor(qr, qr, F1[:, :, :], ALU.add)
                link(dve.tensor_tensor(qi, qi, F2[:, :, :], ALU.subtract))
            dve.wait_ge(d0_ready, 2)
            for ri in range(2):
                z = QZ[:, ri].rearrange("p t n -> p (t n)")
                dve.tensor_tensor_scan(z, D0[:, :, :].rearrange("p t n -> p (t n)"), z, 0.0, ALU.mult,
                                       ALU.add).then_inc(z_done, 1)
            dve.wait_ge(z_done, 2)
            for b in range(4):
                if b >= 2:
                    dve.wait_ge(y_ps, b - 1)
                er, ei = phase(0, b, 1, P), phase(1, b, 1, P)
                zr, zi = QZ[:, 0, 4 * b:4 * b + 4, 0:P - 1], QZ[:, 1, 4 * b:4 * b + 4, 0:P - 1]
                sr, si = SV[b % 2][:, 0, :, 1:P], SV[b % 2][:, 1, :, 1:P]
                f1, f2 = F1[:, :, 0:P - 1], F2[:, :, 0:P - 1]
                dve.memset(SV[b % 2][:, :, :, 0:1], 0.0)
                dve.tensor_tensor(sr, zr, er, ALU.mult)
                dve.tensor_tensor(f1, zi, ei, ALU.mult)
                dve.tensor_tensor(si, zi, er, ALU.mult)
                link(dve.tensor_tensor(f2, zr, ei, ALU.mult))
                dve.tensor_tensor(sr, sr, f1, ALU.subtract)
                link(dve.tensor_tensor(si, si, f2, ALU.add))
                dve.sem_inc(sv_ready, 1)
            dve.wait_ge(x5_scaled, 1)
            for b in range(4):
                dve.wait_ge(y_ps, b + 1)
                for g in range(2):
                    x = X5[:, 8 * b + g:8 * b + 8:2].rearrange("p t j c -> p t (j c)")
                    dve.tensor_tensor(x, x, HALF[2 * b + g].rearrange("p (t n) -> p t n", t=4), ALU.add).then_inc(
                        y_ready, 1)
            dve.wait_ge(y_ps, 4)
            for b in range(4):
                dve.wait_ge(yh5_ready, b + 1)
                dve.tensor_tensor(YL5[:, b, :].rearrange("p (s j) -> p j s", j=8),
                                  BANKS[b][:, :].rearrange("p (j s) -> p j s", j=8),
                                  YH5[:, b, :].bitcast(F32).rearrange("p (s j) -> p j s", j=8),
                                  ALU.subtract).then_inc(yl5_ready, 1)
            dve.wait_ge(yl5_ready, 4)
            with dve.Fori(0, 4) as m:
                b = Block("glu", m, 0)
                dve.wait_ge(mm_done, b.n + 1)
                dve.wait_ge(ga_ready, m + 1)
                dve.wait_ge(g5_done, m)
                dve.tensor_tensor(SG[1][:, :], SG[0][:, :], DP[b.slot][:, :], ALU.mult).then_inc(g5_mul, 1)
                dve.wait_ge(g5_mul, m + 1)
                dve.sem_inc(psum_free[b.slot], 1)
                g = G5[:, ds(m, 1), :].rearrange("p a n -> p (a n)")
                dve.tensor_tensor(g, g, SG[1][:, :], ALU.mult).then_inc(g5_done, 1)

        def s5_pool(pool):
            for name in ("s5x", "s5g"):
                with pool.Fori(0, 2) as m:
                    for i in range(2):
                        split(pool, Block(name, m, i))
            pool.wait_ge(s5_in, 48)
            pool.wait_ge(ut, 8)
            pool.tensor_tensor(X5[:, :, :, :], X5[:, :, :, :],
                               DROW[:, :, :].rearrange("p g (a c) -> p g a c", a=1).broadcast_to([P, 32, 8, 16]),
                               ALU.mult).then_inc(x5_scaled, 1)
            with pool.Fori(0, 4) as m:
                for i in range(2):
                    split(pool, Block("glu", m, i))
            for p in range(NPAIR):
                pool.wait_ge(yh_ready, 8 + p + 1)
                pool.wait_ge(mm_done, last_block("glu"))
                pool.tensor_tensor(YL[:, p, :], G5[:, p, :], YH[:, p, :].bitcast(F32), ALU.subtract).then_inc(
                    yl_ready, 1)

        LC = at("LC", S0, [P, T])
        LCH, LCL = at("LCH", S0 + 4, [P, 1, T], F32R), at("LCL", S0 + 8, [P, 1, T], F32R)
        LR, LI, LA, LD, LG = (at(n, S0 + 12 + 4 * i, [P, T]) for i, n in enumerate(("LR", "LI", "LA", "LD", "LG")))
        LH, LL = at("LH", S0 + 32, [P, 2, T], F32R), at("LL", S0 + 40, [P, 2, T], F32R)
        ZL = at("ZL", 64, [P, KD, T])
        SP4, SPA, SPB = at("SP4", 153.5, [P, 10]), at("SPA", 153.625, [P, 10]), at("SPB", 153.75, [P, 10])
        sp_act, sp4_ready, zl_zero = sem("sp_act"), sem("sp4_ready"), sem("zl_zero")
        lc_mid, lc_conv, lc_ready, lch_ready, lcl_ready, lr_ready, li_ready, lt_ready, l_dve, lm2_ready, lroot = (
            sem(n) for n in ("lc_mid", "lc_conv", "lc_ready", "lch_ready", "lcl_ready", "lr_ready", "li_ready",
                             "lt_ready", "l_dve", "lm2_ready", "lroot"))
        lic_ready, lin_ready, lscan, lg_ready, lhb_ready, lh_ready, ll_ready = (sem(n) for n in (
            "lic_ready", "lin_ready", "lscan", "lg_ready", "lhb_ready", "lh_ready", "ll_ready"))

        def lru_pe(pe):
            with pe.Fori(0, 5) as it:
                for h in range(2):
                    n = it * 2 + h
                    product(pe, Block("lru", it, 4 * h), XH, XL)
                    pe.wait_ge(lch_ready, n + 1)
                    pe.wait_ge(lcl_ready, n + 1)
                    for i in (1, 2):
                        product(pe, Block("lru", it, 4 * h + i), LCH, LCL)
                    product(pe, Block("lru", it, 4 * h + 3), XH, XL)
                pe.wait_ge(ll_ready, it * 2 + 2)
                for m in range(8):
                    product(pe, Block("lru", it, 8 + m), LH, LL)

        def lru_act(act):
            lam = COL[:, COLS["lam"]:COLS["lam"] + 10]
            act.activation(SPA[:, :], lam, ACT.Abs).then_inc(sp_act, 1)
            act.wait_ge(sp_act, 1)
            act.activation(SPB[:, :], SPA[:, :], ACT.Exp, scale=-1.0).then_inc(sp_act, 1)
            act.wait_ge(sp_act, 2)
            act.activation(SPA[:, :], SPB[:, :], ACT.Ln, bias=1.0).then_inc(sp_act, 1)
            act.wait_ge(sp_act, 3)
            act.activation(SPB[:, :], lam, ACT.Relu, scale=-1.0).then_inc(sp_act, 1)
            act.wait_ge(sp4_ready, 1)
            act.wait_ge(mm_done, last_block("mixs"))
            act.wait_ge(mx_done, 24)
            with act.Fori(0, 5) as it:
                for h in range(2):
                    n = it * 2 + h

                    def column(name, i=0):
                        return COL[:, ds(it * 2 + (COLS[name] + h + i), 1)]

                    b = Block("lru", it, 4 * h)
                    act.wait_ge(mm_done, b.n + 1)
                    act.wait_ge(lcl_ready, n)
                    act.wait_ge(lic_ready, n)
                    act.activation(LC[:, :], DP[b.slot][:, :], ACT.Identity, scale=column("lruconv", 30),
                                   bias=column("convb")).then_inc(lc_mid, 1)
                    b1, b2 = Block("lru", it, 4 * h + 1), Block("lru", it, 4 * h + 2)
                    act.wait_ge(lc_ready, n + 1)
                    act.wait_ge(mm_done, Block("lru", it, 4 * h).n)
                    act.activation(LCH[:, 0, :], LC[:, :], ACT.Copy).then_inc(lch_ready, 1)
                    act.wait_ge(mm_done, b1.n + 1)
                    act.wait_ge(lhb_ready, n)
                    act.activation(LR[:, :], DP[b1.slot][:, :], ACT.Sigmoid, bias=column("ba")).then_inc(lr_ready, 1)
                    act.wait_ge(lr_ready, n + 1)
                    act.sem_inc(psum_free[b1.slot], 1)
                    act.wait_ge(mm_done, b2.n + 1)
                    act.wait_ge(lscan, n)
                    act.activation(LI[:, :], DP[b2.slot][:, :], ACT.Sigmoid, bias=column("bx")).then_inc(li_ready, 1)
                    act.wait_ge(li_ready, n + 1)
                    act.sem_inc(psum_free[b2.slot], 1)
                    act.activation(LR[:, :], LR[:, :], ACT.Tanh, scale=SP4[:, ds(it * 2 + h, 1)]).then_inc(lt_ready, 1)
                    b3 = Block("lru", it, 4 * h + 3)
                    act.wait_ge(mm_done, b3.n + 1)
                    act.wait_ge(ll_ready, n)
                    act.activation(LG[:, :], DP[b3.slot][:, :], ACT.Silu).then_inc(lg_ready, 1)
                    act.wait_ge(lg_ready, n + 1)
                    act.sem_inc(psum_free[b3.slot], 1)
                    act.wait_ge(lm2_ready, n + 1)
                    act.activation(LR[:, :], LR[:, :], ACT.Sqrt).then_inc(lroot, 1)
                    act.wait_ge(lhb_ready, n + 1)
                    act.wait_ge(mm_done, Block("lru", it, 0).n)
                    act.activation(LH[:, h, :], LG[:, :], ACT.Copy).then_inc(lh_ready, 1)

        def lru_dve(dve):
            dve.wait_ge(sp_act, 4)
            dve.tensor_tensor(SPA[:, :], SPA[:, :], SPB[:, :], ALU.add).then_inc(sp_act, 1)
            dve.wait_ge(sp_act, 5)
            dve.tensor_scalar(SP4[:, :], SPA[:, :], 4.0, None, ALU.mult).then_inc(sp4_ready, 1)
            dve.wait_ge(zl_zero, 1)
            with dve.Fori(0, 5) as it:
                for h in range(2):
                    n = it * 2 + h
                    b = Block("lru", it, 4 * h)
                    dve.wait_ge(lc_mid, n + 1)
                    for i, back in enumerate((1, 2, 3)):
                        dve.scalar_tensor_tensor(out=LC[:, back:T], in0=DP[b.slot][:, 0:T - back],
                                                 scalar=COL[:, ds(it * 2 + (COLS["lruconv"] + 10 * (3 - back) + h), 1)],
                                                 in1=LC[:, back:T], op0=ALU.mult, op1=ALU.add).then_inc(lc_conv, 1)
                        dve.wait_ge(lc_conv, n * 3 + (i + 1))
                    dve.sem_inc(psum_free[b.slot], 1)
                    dve.sem_inc(lc_ready, 1)
                    dve.wait_ge(lt_ready, n + 1)
                    steps = [
                        lambda: dve.tensor_scalar(LD[:, :], LR[:, :], 1.0, None, ALU.add),
                        lambda: dve.reciprocal(LD[:, :], LD[:, :]),
                        lambda: dve.tensor_scalar(LA[:, :], LR[:, :], -1.0, 1.0, ALU.mult, ALU.add),
                        lambda: dve.tensor_tensor(LA[:, :], LA[:, :], LD[:, :], ALU.mult),
                        lambda: dve.scalar_tensor_tensor(out=LR[:, :], in0=LR[:, :], scalar=2.0, in1=LD[:, :],
                                                         op0=ALU.mult, op1=ALU.mult),
                    ]
                    for i, step in enumerate(steps):
                        step().then_inc(l_dve, 1)
                        dve.wait_ge(l_dve, n * 5 + (i + 1))
                    dve.scalar_tensor_tensor(out=LR[:, :], in0=LA[:, :], scalar=1.0, in1=LR[:, :], op0=ALU.add,
                                             op1=ALU.mult).then_inc(lm2_ready, 1)
                    dve.wait_ge(lroot, n + 1)
                    dve.wait_ge(lic_ready, n + 1)
                    dve.tensor_tensor(LI[:, :], LI[:, :], LR[:, :], ALU.mult).then_inc(lin_ready, 1)
                    dve.wait_ge(lin_ready, n + 1)
                    dve.tensor_tensor_scan(LR[:, :], LA[:, :], LI[:, :], 0.0, ALU.mult, ALU.add).then_inc(lscan, 1)
                    dve.wait_ge(lscan, n + 1)
                    dve.wait_ge(lg_ready, n + 1)
                    dve.tensor_tensor(LG[:, :], LG[:, :], LR[:, :], ALU.mult).then_inc(lhb_ready, 1)
                for m in range(8):
                    b = Block("lru", it, 8 + m)
                    dve.wait_ge(mm_done, b.n + 1)
                    dve.tensor_tensor(ZL[:, m, :], ZL[:, m, :], DP[b.slot][:, :], ALU.add).then_inc(
                        psum_free[b.slot], 1)

        def lru_pool(pool):
            pool.wait_ge(mm_done, last_block("mixs"))
            pool.memset(ZL[:, :, :], 0.0).then_inc(zl_zero, 1)
            with pool.Fori(0, 5) as it:
                for h in range(2):
                    n = it * 2 + h
                    for i in range(4):
                        split(pool, Block("lru", it, 4 * h + i))
                        if i == 0:
                            pool.wait_ge(lch_ready, n + 1)
                            pool.tensor_tensor(LCL[:, 0, :], LC[:, :], LCH[:, 0, :].bitcast(F32),
                                               ALU.subtract).then_inc(lcl_ready, 1)
                        if i == 2:
                            pool.wait_ge(li_ready, n + 1)
                            pool.tensor_tensor(LI[:, :], LI[:, :], LC[:, :], ALU.mult).then_inc(lic_ready, 1)
                    pool.wait_ge(lh_ready, n + 1)
                    pool.tensor_tensor(LL[:, h, :], LG[:, :], LH[:, h, :].bitcast(F32), ALU.subtract).then_inc(
                        ll_ready, 1)
                for m in range(8):
                    split(pool, Block("lru", it, 8 + m))

        TO = at("TO", 64, [P, KD, T])
        PR = at("PR", S0 + 20, [P, 2, T])
        PH, PL = at("PH", S0 + 28, [P, 2, T], F32R), at("PL", S0 + 36, [P, 2, T], F32R)
        gl_ready, gl_used, gl_done, to_ready, x3_in, x3_ready = (sem(n) for n in (
            "gl_ready", "gl_used", "gl_done", "to_ready", "x3_in", "x3_ready"))
        p_in, ph_ready, pl_ready, pg_ready, pg_used, out_ready, out_done = (sem(n) for n in (
            "p_in", "ph_ready", "pl_ready", "pg_ready", "pg_used", "out_ready", "out_done"))

        def end_pe(pe):
            plain_pe(pe, "gatel", XH, XL)
            pe.wait_ge(ms_hi, 2 * KD)
            pe.wait_ge(ms_lo, 2 * KD)
            plain_pe(pe, "wout", XH, XL)
            norm_pe(pe, c4)
            pe.wait_ge(xh_ready, c4.nt + KD)
            pe.wait_ge(nt_used, c4.nt + KD)
            pe.wait_ge(ph_ready, 1)
            pe.wait_ge(pl_ready, 1)
            with pe.Fori(0, 8) as m:
                product(pe, Block("ple", m, 0), PH, PL)
                product(pe, Block("ple", m, 1), XH, XL)

        def end_act(act):
            act.wait_ge(mm_done, last_block("lru"))
            act.wait_ge(ll_ready, 10)
            act.wait_ge(lc_ready, 10)
            with act.Fori(0, 4) as m:
                for i in range(2):
                    b = Block("gatel", m, i)
                    act.wait_ge(mm_done, b.n + 1)
                    if i == 0:
                        act.wait_ge(gl_done, m * 2)
                    else:
                        act.wait_ge(gl_done, m * 2)
                    act.activation(SG[i][:, :], DP[b.slot][:, :], ACT.Sigmoid).then_inc(gl_ready, 1)
                    act.wait_ge(gl_ready, m * 2 + (i + 1))
                    act.sem_inc(psum_free[b.slot], 1)
            act.wait_ge(gl_done, 8)
            mx_split(act, None, KD, MX, last_block("gatel"))
            with act.Fori(0, 4) as m:
                for i in range(2):
                    b = Block("wout", m, i)
                    act.wait_ge(mm_done, b.n + 1)
                    act.activation(TO[:, ds(m * 2 + i, 1), :].rearrange("p a n -> p (a n)"), DP[b.slot][:, :],
                                   ACT.Copy).then_inc(to_ready, 1)
                    act.wait_ge(to_ready, m * 2 + (i + 1))
                    act.sem_inc(psum_free[b.slot], 1)
            for k in range(KD):
                act.wait_ge(sq_used, c4.sq + k - 1)
                act.activation(SQ[k % 2][:, :], TO[:, k, :], ACT.Square).then_inc(sq_ready, 1)
            act.wait_ge(sq_used, c4.sq + KD)
            act.activation(RS[:, :], B67[:, :], ACT.Sqrt, scale=1.0 / D, bias=EPS).then_inc(rs_sqrt, 1)
            act.wait_ge(p_in, 16)
            act.activation(PH[:, :, :], PR[:, :, :], ACT.Copy).then_inc(ph_ready, 1)
            for k in range(KD):
                act.wait_ge(x3_ready, k + 1)
                act.activation(XH[:, k, :], MX[:, k, :], ACT.Copy).then_inc(xh_ready, 1)
            with act.Fori(0, 8) as m:
                b = Block("ple", m, 1)
                act.wait_ge(mm_done, b.n + 1)
                act.wait_ge(pg_used, m)
                act.activation(SG[0][:, :], DP[b.slot][:, :], ACT.Sigmoid).then_inc(pg_ready, 1)
                act.wait_ge(pg_ready, m + 1)
                act.sem_inc(psum_free[b.slot], 1)

        def end_dve(dve):
            with dve.Fori(0, 4) as m:
                for i in range(2):
                    n = m * 2 + i
                    dve.wait_ge(gl_ready, m * 2 + (i + 1))
                    zl = ZL[:, ds(n, 1), :].rearrange("p a n -> p (a n)")
                    mx = MX[:, ds(n, 1), :].rearrange("p a n -> p (a n)")
                    dve.tensor_tensor(SG[i][:, :], SG[i][:, :], zl, ALU.mult).then_inc(gl_used, 1)
                    dve.wait_ge(gl_used, m * 2 + (i + 1))
                    dve.tensor_tensor(mx, mx, SG[i][:, :], ALU.add).then_inc(gl_done, 1)
            dve.wait_ge(rs_sqrt, c4.ss + 1)
            dve.reciprocal(RS[:, :], RS[:, :]).then_inc(rs_ready, 1)
            dve.wait_ge(rs_ready, c4.ss + 1)
            dve.wait_ge(x3_in, 16)
            for k in range(KD):
                if k >= 2:
                    dve.wait_ge(x3_ready, k - 1)
                dve.scalar_tensor_tensor(out=NTL[k % 2][:, :], in0=TO[:, k, :], scalar=col("gpost", k),
                                         in1=RS[:, :], op0=ALU.mult, op1=ALU.mult).then_inc(nt_ready, 1)
                dve.wait_ge(nt_ready, c4.nt + k + 1)
                dve.tensor_tensor(MX[:, k, :], MX[:, k, :], NTL[k % 2][:, :], ALU.add).then_inc(x3_ready, 1)
            dve.wait_ge(sq_used, c4.sq + KD)
            with dve.Fori(0, 8) as m:
                b = Block("ple", m, 0)
                dve.wait_ge(mm_done, b.n + 1)
                dve.wait_ge(pg_ready, m + 1)
                dve.wait_ge(out_ready, m)
                dve.wait_ge(nt_used, c4.nt + KD)
                dve.tensor_tensor(SG[1][:, :], SG[0][:, :], DP[b.slot][:, :], ALU.mult).then_inc(pg_used, 1)
                dve.wait_ge(pg_used, m + 1)
                dve.sem_inc(psum_free[b.slot], 1)
                o = MX[:, ds(m, 1), :].rearrange("p a n -> p (a n)")
                dve.tensor_tensor(o, o, SG[1][:, :], ALU.add).then_inc(out_ready, 1)

        def end_pool(pool):
            with pool.Fori(0, 4) as m:
                for i in range(2):
                    split(pool, Block("gatel", m, i))
            mx_split(None, pool, KD, MX, None)
            with pool.Fori(0, 4) as m:
                for i in range(2):
                    split(pool, Block("wout", m, i))
            pool.wait_ge(ph_ready, 1)
            pool.tensor_tensor(PL[:, :, :], PR[:, :, :], PH[:, :, :].bitcast(F32), ALU.subtract).then_inc(pl_ready, 1)
            for k in range(KD):
                pool.wait_ge(xh_ready, c4.nt + k + 1)
                pool.tensor_tensor(XL[:, k, :], MX[:, k, :], XH[:, k, :].bitcast(F32), ALU.subtract).then_inc(
                    nt_used, 1)
            with pool.Fori(0, 8) as m:
                split(pool, Block("ple", m, 0))
                split(pool, Block("ple", m, 1))

        with nc.Block() as block:
            @block.sync
            def _(sp):
                s5_sp(sp)
                for name, w in (("s5x", "w_s5x"), ("s5g", "w_s5g")):
                    with sp.Fori(0, 2) as m:
                        for i in range(2):
                            load(sp, Block(name, m, i), a[w])
                s5_sp_stream(sp)
                with sp.Fori(0, 4) as m:
                    load(sp, Block("glu", m, 0), a["w_glua"], m)
                    load(sp, Block("glu", m, 1), a["w_glub"], m)
                with sp.Fori(0, 8) as m:
                    load(sp, Block("mixs", m, 0), a["w_gates"], m)
                    load(sp, Block("mixs", m, 1), a["w_bs"], m)
                with sp.Fori(0, 5) as it:
                    for h in range(2):
                        load(sp, Block("lru", it, 4 * h), a["w_lrux"], it * 2 + h)
                        load(sp, Block("lru", it, 4 * h + 1), a["w_lrua"], it * 2 + h)
                        load(sp, Block("lru", it, 4 * h + 2), a["w_lrui"], it * 2 + h)
                        load(sp, Block("lru", it, 4 * h + 3), a["w_lrug"], it * 2 + h)
                    for m in range(8):
                        load(sp, Block("lru", it, 8 + m), a["w_bl"], it * 8 + m)
                for name, w in (("gatel", "w_gatel"), ("wout", "w_out")):
                    with sp.Fori(0, 4) as m:
                        for i in range(2):
                            load(sp, Block(name, m, i), a[w])
                    if name == "gatel":
                        sp.wait_ge(gl_done, 8)
                sp.wait_ge(ms_lo, 2 * KD)
                sp.wait_ge(ms_hi, 2 * KD)
                sp.dma_start(MX[:, :, :], x2_dram).then_inc(x3_in, 16)
                sp.dma_start(PR[:, :, :], a["p"]).then_inc(p_in, 16)
                with sp.Fori(0, 8) as m:
                    load(sp, Block("ple", m, 0), a["w_ple"], m)
                    load(sp, Block("ple", m, 1), a["w_pleg"], m)
                sp.wait_ge(out_ready, 8)
                sp.dma_start(out, MX[:, :, :]).then_inc(out_done, 16)
                sp.wait_ge(out_done, 16)

            @block.gpsimd
            def _(pool):
                norm_pool(pool, c3)
                s5_pool(pool)
                with pool.Fori(0, 8) as m:
                    split(pool, Block("mixs", m, 0))
                    split(pool, Block("mixs", m, 1))
                lru_pool(pool)
                end_pool(pool)

            @block.scalar
            def _(act):
                norm_act(act, c3, XR)
                s5_act(act)
                mix_act(act, "mixs", 16)
                lru_act(act)
                end_act(act)

            @block.vector
            def _(dve):
                norm_dve(dve, c3, XR, "gpre")
                s5_dve(dve)
                dve.wait_ge(yh_ready, 12)
                mix_dve(dve, "mixs", 16, False, True)
                lru_dve(dve)
                end_dve(dve)

            @block.tensor
            def _(pe):
                norm_pe(pe, c3)
                pe.wait_ge(xh_ready, c3.nt + KD)
                pe.wait_ge(nt_used, c3.nt + KD)
                s5_pe(pe)
                pe.wait_ge(yh_ready, 12)
                pe.wait_ge(yl_ready, 12)
                mix_pe(pe, "mixs")
                lru_pe(pe)
                end_pe(pe)



def blocks(w, cols=None):
    k, n = w.shape
    return np.ascontiguousarray(w.reshape(k // P, P, n // P, P).transpose(2, 1, 0, 3)).reshape(n // P, P, k)


def columns(v):
    return np.ascontiguousarray(np.asarray(v).reshape(-1, P).T)


def pack(i):
    w_in = i["w_in"][0]
    arrays = {}
    cst, bias, levels, sel = constants()
    arrays.update(cst=cst, bias=bias, levels=levels, sel=sel)
    arrays["x"] = np.ascontiguousarray(i["x"][0].T.reshape(KD, P, T).transpose(1, 0, 2))
    qb, kb, vb = 2080, 2080 + 1536, 2080 + 3072
    ga, gb = 2080 + 4608, 2080 + 4608 + 1024
    arrays["w_attn"] = blocks(np.concatenate(
        [w_in[:, o + 512 * g + 128 * p:o + 512 * g + 128 * p + 128]
         for p in range(NPAIR) for g in range(NG) for o in (qb, kb, vb)], 1))
    arrays["w_gateb"], arrays["w_gatea"] = blocks(w_in[:, gb:gb + D]), blocks(w_in[:, ga:ga + D])
    arrays["w_attnout"], arrays["w_dnout"] = blocks(i["w_attn_out"][0]), blocks(i["w_dn_out"][0])
    arrays["w_o"] = blocks(i["w_o"][0])
    up, down, dff = i["w_ffn_up"][0], i["w_ffn_down"][0], FT * P
    arrays["w_up"] = blocks(np.concatenate(
        [up[:, dff * part + P * t:dff * part + P * t + P] for t in range(FT) for part in range(2)], 1))
    arrays["w_down"] = np.ascontiguousarray(
        down.reshape(FT // 2, 2, P, KD, P).transpose(0, 3, 2, 1, 4)).reshape(FT // 2 * KD, P, 2 * P)
    w2 = i["w_in_2"][0]
    for name, o, n in (("w_s5x", 0, 512), ("w_s5g", 512, 512), ("w_lrux", 1024, 1280), ("w_lrug", 2304, 1280),
                       ("w_gates", 3584, D), ("w_gatel", 4608, D)):
        arrays[name] = blocks(w2[:, o:o + n])
    arrays["w_glua"], arrays["w_glub"] = blocks(i["w_glu_2"][0][:, 0:512]), blocks(i["w_glu_2"][0][:, 512:])
    arrays["w_bs"], arrays["w_out"] = blocks(i["w_bs_2"][0]), blocks(i["w_out_2"][0])
    arrays["w_lrua"], arrays["w_lrui"] = i["lru_w_a_2"][0], i["lru_w_x_2"][0]
    arrays["w_bl"] = np.ascontiguousarray(
        i["w_bl_2"][0].reshape(5, 2, P, KD, P).transpose(0, 3, 2, 1, 4)).reshape(5 * KD, P, 2 * P)
    arrays["w_ple"], arrays["w_pleg"] = blocks(i["w_ple_2"][0]), blocks(i["w_ple_gate_2"][0])
    arrays["p"] = np.ascontiguousarray(i["p_2"][0, 0].T.reshape(2, P, T).transpose(1, 0, 2))
    arrays["s5d"] = i["s5_d_2"]

    def states(v):
        v = v.reshape((16, 2, 64) + v.shape[2:])
        return np.moveaxis(v, 0, 2).reshape(P, -1)

    arrays["s5p"] = np.ascontiguousarray(np.concatenate(
        [states(i["s5_a_re_2"][0]), states(i["s5_a_im_2"][0]), states(np.repeat(i["s5_log_dt_2"][0][:, None], 64, 1)),
         states(i["s5_b_re_2"][0]), states(i["s5_b_im_2"][0]),
         states(i["s5_c_re_2"][0].transpose(0, 2, 1)), states(i["s5_c_im_2"][0].transpose(0, 2, 1))], 1))
    ab = np.zeros((D, P), np.float32)
    ab[:, 0:16], ab[:, 32:48] = w_in[:, 2048:2064], w_in[:, 2064:2080]
    arrays["w_ab"] = blocks(ab)
    arrays["w_dn"] = blocks(np.concatenate(
        [w_in[:, 512 * o + 128 * p:512 * o + 128 * p + 128] for p in range(NPAIR) for o in range(4)], 1))
    c = np.zeros((P, NCOLS), np.float32)

    def put(name, v):
        c[:v.shape[0], COLS[name]:COLS[name] + v.shape[1]] = v

    put("norm1", columns(i["norm1_w"]))
    put("norm2", columns(i["norm2_w"]))
    put("gpre", columns(i["g_pre_2"]))
    put("gpost", columns(i["g_post_2"]))
    put("qn", columns(np.tile(i["attn_q_norm_w"][0], 2)))
    put("kn", columns(np.tile(i["attn_k_norm_w"][0], 2)))
    put("dnw", columns(np.tile(i["dn_out_norm_w"][0], 2)))
    put("dtb", i["dn_dt_bias"].reshape(16, 1))
    put("alog", i["dn_a_log"].reshape(16, 1))
    put("lruconv", columns(i["conv_w_2"]))
    for name, key in (("convb", "conv_b_2"), ("ba", "lru_b_a_2"), ("bx", "lru_b_x_2"), ("lam", "lru_lambda_2")):
        put(name, columns(i[key]))
    put("ffnconv", columns(i["ffn_conv_w"]))
    put("dnconv", columns(i["dn_conv_w"]))
    arrays["cols"] = c
    return arrays


def kernel(**inputs):
    import numpy as _np
    import concourse.bacc as _bacc
    from concourse import mybir as _mybir
    from concourse.bass_utils import run_bass_kernel_spmd as _run

    inputs = {k: _np.asarray(v) for k, v in inputs.items()}
    arrays = {f"in_{k}": _np.ascontiguousarray(v) for k, v in pack(inputs).items()}
    nc = _bacc.Bacc("TRN2", target_bir_lowering=False, num_devices=1)
    a = {k[3:]: nc.dram_tensor(k, list(v.shape), _mybir.dt.from_np(v.dtype), kind="ExternalInput").ap()
         for k, v in arrays.items()}
    out = nc.dram_tensor("out", [P, KD, T], _mybir.dt.float32, kind="ExternalOutput").ap()
    program(nc, a, out)
    result = _run(nc, [arrays], core_ids=[0])
    out_t = result.results[0]["out"]
    return _np.ascontiguousarray(out_t.transpose(2, 1, 0)).reshape(1, T, D)
```

```python
from contextlib import ExitStack

import numpy as np
import concourse.bass as bass
from concourse import mybir

F32 = mybir.dt.float32
F32R = mybir.dt.float32r
ALU = mybir.AluOpType
ACT = mybir.ActivationFunctionType
AXX = mybir.AxisListType.X
ds = bass.ds

P = 128
T = 1024
H = T // 2
D = 1024
KD = D // P
EPS = 1e-6
NEG = -1e30
NPAIR = 4
NG = 3
NT = 8
FT = 22
KB = 1024

DENSE = [
    ("attn", NPAIR, [8] * 9),
    ("mixb", 8, [8, 4]),
    ("dnab", 1, [8]),
    ("dn", NPAIR, [8] * 4),
    ("mixa", 8, [8, 4]),
    ("wo", 4, [8, 8]),
    ("ffn0", 1, [8] * 4),
    ("ffn", FT // 2 - 1, [8] * 6),
    ("ffn1", 1, [8, 8]),
    ("s5x", 2, [8, 8]),
    ("s5g", 2, [8, 8]),
    ("glu", 4, [4, 4]),
    ("mixs", 8, [8, 4]),
    ("lru0", 1, [8, 8, 2, 8, 2, 8]),
    ("lru", 4, [8, 8, 8, 2, 8, 8, 2, 8]),
    ("lru1", 1, [8, 8]),
    ("gatel", 4, [8, 8]),
    ("wout", 4, [8, 8]),
    ("ple", 8, [2, 8]),
]


class Block:

    def __init__(self, name, it, pos):
        n0, loads0, last = 0, [0, 0], 1
        for other, count, tiles in DENSE:
            if other == name:
                break
            for i in range(len(tiles)):
                loads0[i % 2] += count
            n0 += count * len(tiles)
            last = (len(tiles) - 1) % 2
        self.kt = tiles[pos]
        self.slot = pos % 2
        body = len(tiles)
        per = len([i for i in range(body) if i % 2 == self.slot])
        upto = len([i for i in range(pos + 1) if i % 2 == self.slot])
        self.n = it * body + (n0 + pos)
        self.loads = it * per + (loads0[self.slot] + upto)
        odd = (body % 2 == 1 and count > 1) or last == 0
        self.dist = 1 if pos == 0 and odd else 2
        self.row = it * body + pos

    def before(self):
        return self.n - self.dist + 1


def last_block(name):
    n = 0
    for other, count, tiles in DENSE:
        n += count * len(tiles)
        if other == name:
            return n


def att_tokens(g, t):
    if g == 0:
        return lambda a: a[:, P * t:P * t + P]
    if g == 1:
        return lambda a: a.rearrange("p (s d) -> p d s", d=4)[:, t // 2, P * (t % 2):P * (t % 2) + P]
    return lambda a: a.rearrange("p (s d) -> p d s", d=8)[:, t, :]


def att_keys(g, t):
    if g == 0:
        a, b = max(P * t - 64, 0), min(P * t + 192, T)
        return (lambda x: x[:, a:b]), b - a, (64 if t == 0 else 0), [
            (t, 64 if t == 0 else P), (t + 1, 64 if t == 7 else P)]
    if g == 1:
        r, half = t // 2, t % 2
        return (lambda x: x.rearrange("p (s d) -> p d s", d=4)[:, r, 64 * half:64 * half + 192]), 192, \
            (0 if half else 64), [(3 * r + half, P if half else 64), (3 * r + half + 1, 64 if half else P)]
    return att_tokens(2, t), P, 0, [(t, P)]


def att_chunk(g, c):
    if g == 0:
        a, b = max(P * c - 64, 0), min(P * c + 64, T)
        return (lambda x: x[:, a:b]), b - a
    if g == 1:
        r, i = c // 3, c % 3
        a, b = [(0, 64), (64, 192), (192, 256)][i]
        return (lambda x: x.rearrange("p (s d) -> p d s", d=4)[:, r, a:b]), b - a
    return att_tokens(2, c), P


CHUNKS = [9, 12, 8]
VBATCH = [3, 3, 2]
VB0 = [0, 3, 6]
VBP = 8


COLS = {}
_at = 0
for _name, _n in [("norm1", 8), ("norm2", 8), ("gpre", 8), ("gpost", 8), ("qn", 1), ("kn", 1), ("dnw", 1),
                  ("dtb", 1), ("alog", 1), ("dnconv", 3 * 12), ("ffnconv", 3 * 44), ("lruconv", 4 * 10),
                  ("convb", 10), ("ba", 10), ("bx", 10), ("lam", 10)]:
    COLS[_name] = _at
    _at += _n
NCOLS = _at

CST = {}
_at = 0
for _name, _n in [("ident", P), ("ones", P), ("blk", P), ("tri", 2 * P), ("mpos", 2 * P), ("mneg", 2 * P),
                  ("slopes", 24)]:
    CST[_name] = (_at, _n)
    _at += _n
NCST = _at


def constants():
    i, j = np.arange(P)[:, None], np.arange(P)[None, :]
    c = np.zeros((P, NCST), np.float32)

    def put(name, a):
        c[:a.shape[0], CST[name][0]:CST[name][0] + a.shape[1]] = a

    put("ident", (i == j) * 1.0)
    put("ones", np.ones((P, P)))
    put("blk", (i // 64 == j // 64) * 1.0)
    put("tri", np.concatenate([(i <= j) * 1.0, (i >= j) * 1.0], 1))
    put("mpos", np.concatenate([np.where(i > j, 0, -NEG), np.where(i < j, 0, -NEG)], 1))
    put("mneg", np.concatenate([np.where(i <= j, 0, NEG), np.where(i >= j, 0, NEG)], 1))
    slopes = 2.0 ** (-8.0 * np.arange(1, 25) / 24)
    dil = np.repeat([1, 4, 16], 8)
    put("slopes", np.tile((8.0 * slopes * dil)[None], (P, 1)))
    k = np.arange(256)[None, :]
    rel = np.abs(i + 64 - k)
    bias = np.where(rel <= 64, -rel, NEG).astype(np.float32)
    same = (i % 2) == (j % 2)
    bias16 = np.where(same, -np.abs(i // 2 - j // 2), NEG).astype(np.float32)
    levels = np.zeros((P, 7, 2, P), np.float32)
    for l in range(7):
        b = 2 ** l
        low = (i // (2 * b) == j // (2 * b)) & (i // b % 2 == 1) & (j // b % 2 == 0)
        levels[:, l, 0], levels[:, l, 1] = low, low.T
    sel = np.zeros((8, NPAIR, P), np.float32)
    for p in range(NPAIR):
        for h in range(2):
            sel[2 * p + h, p, 64 * h:64 * h + 64] = 1
    return c, np.concatenate([bias, bias16], 1).astype(np.float32), levels, sel


def program(nc, a, out):
    with ExitStack() as ctx:
        def sem(name):
            return ctx.enter_context(nc.semaphore(name))

        first = []

        def once(name):
            first.append(nc.alloc_semaphore(name))
            return first[-1]

        slab = ctx.enter_context(nc.sbuf_tensor("slab", [P, 207 * KB // 4], F32))
        base = nc.lookup_mloc(slab).addr

        def at(name, kb, shape, dt=F32):
            assert kb * KB + int(np.prod(shape[1:])) * 4 <= 207 * KB, name
            return nc.alloc_sbuf_tensor_at(name, shape, dt, offset=base + int(kb * KB))

        XH = at("XH", 0, [P, KD, T], F32R)
        XL = at("XL", 32, [P, KD, T], F32R)
        XR = at("XR", 64, [P, KD, T])
        MX = at("MX", 96, [P, KD, T])
        WRAW = [at(f"WRAW{i}", 128 + 4 * i, [P, 8, P]) for i in range(2)]
        WH = [at(f"WH{i}", 136 + 4 * i, [P, 8, P], F32R) for i in range(2)]
        WL = [at(f"WL{i}", 144 + 4 * i, [P, 8, P], F32R) for i in range(2)]
        COL = at("COL", 152, [P, NCOLS])
        CON = at("CON", 154, [P, NCST])
        S0 = 159

        def con(name, i=0, n=None):
            o, size = CST[name]
            n = n or size
            return CON[:, o + i * n:o + (i + 1) * n]

        def col(name, i=0):
            return COL[:, COLS[name] + i:COLS[name] + i + 1]

        IDENT, ONES, BLK = con("ident"), con("ones"), con("blk")

        DP = [ctx.enter_context(nc.psum_tensor(f"DP{i}", [P, T], F32)) for i in range(2)]
        B45 = ctx.enter_context(nc.psum_tensor("B45", [P, T], F32))
        B67 = ctx.enter_context(nc.psum_tensor("B67", [P, T], F32))

        w_loaded = [sem("w_loaded0"), sem("w_loaded1")]
        w_hi = sem("w_hi")
        w_split = sem("w_split")
        mm_done = sem("mm_done")
        psum_free = [sem("psum_free0"), sem("psum_free1")]

        con_in = sem("con_in")
        x_in = sem("x_in")
        sq_ready, sq_used, rs_sqrt, rs_ready = (sem(n) for n in ("sq_ready", "sq_used", "rs_sqrt", "rs_ready"))
        nt_ready, nt_used, xh_ready, xl_ready = (sem(n) for n in ("nt_ready", "nt_used", "xh_ready", "xl_ready"))

        passed = {"pe": sem("pe_passed"), "pool": sem("pool_passed")}

        def gate(e, name):
            e.sem_inc(passed[name], 1)

        def load(sp, b, src, row=None):
            sp.wait_ge(w_split, b.before())
            s = src[ds(b.row if row is None else row, 1)].rearrange("a p n -> (a p) n")
            sp.dma_start(WRAW[b.slot][:, 0:b.kt, :].rearrange("p a n -> p (a n)"), s).then_inc(w_loaded[b.slot], 16)

        def split(pool, b):
            pool.wait_ge(w_loaded[b.slot], b.loads * 16)
            pool.wait_ge(mm_done, b.before())
            gate(pool, "pool")
            pool.tensor_copy(WH[b.slot][:, 0:b.kt, :], WRAW[b.slot][:, 0:b.kt, :]).then_inc(w_hi, 1)
            pool.wait_ge(w_hi, b.n + 1)
            pool.tensor_tensor(WL[b.slot][:, 0:b.kt, :], WRAW[b.slot][:, 0:b.kt, :],
                               WH[b.slot][:, 0:b.kt, :].bitcast(F32), ALU.subtract).then_inc(w_split, 1)

        def freed(e, b):
            e.wait_ge(psum_free[b.slot], b.loads)

        def product(pe, b, hi, lo):
            pe.wait_ge(w_split, b.n + 1)
            pe.wait_ge(psum_free[b.slot], b.loads - 1)
            for k in range(b.kt):
                for w, x, one, end in ((WH, hi, k == 0, False), (WH, lo, False, False),
                                       (WL, hi, False, k == b.kt - 1)):
                    for half in range(2):
                        mm = pe.matmul(DP[b.slot][:, half * H:half * H + H], w[b.slot][:, k, :],
                                       x[:, k, half * H:half * H + H], start=one, stop=end)
            mm.then_inc(mm_done, 1)

        part_ready = sem("part_ready")
        part_read = sem("part_read")

        def product_into(pe, b, dst, k0, kt, hi, lo):
            for k in range(kt):
                for w, x, one, end in ((WH, hi, k == 0, False), (WH, lo, False, False),
                                       (WL, hi, False, k == kt - 1)):
                    for half in range(2):
                        mm = pe.matmul(dst[:, half * H:half * H + H], w[b.slot][:, k0 + k, :],
                                       x[:, k, half * H:half * H + H], start=one, stop=end)
            return mm

        def product4(pe, b, group, hi, lo, second):
            pe.wait_ge(w_split, b.n + 1)
            pe.wait_ge(psum_free[b.slot], b.loads - 1)
            for o in range(4):
                pe.wait_ge(part_read, group * 4 + (o - 1 if second else max(o - 1, 0)))
                product_into(pe, b, (B45, B67)[o % 2], 2 * o, 2, hi, lo).then_inc(
                    part_ready if o < 3 else mm_done, 1)

        def add4(dve, b, group, dst, outputs=range(4), m0=0):
            for o in outputs:
                if o < 3:
                    dve.wait_ge(part_ready, group * 3 + (o + 1))
                else:
                    dve.wait_ge(mm_done, b.n + 1)
                dve.tensor_tensor(dst[:, m0 + o, :], dst[:, m0 + o, :], (B45, B67)[o % 2][:, :], ALU.add).then_inc(
                    part_read, 1)
                if o == 3:
                    dve.wait_ge(part_read, group * 4 + 4)
                    dve.sem_inc(psum_free[b.slot], 1)

        SQ = [at(f"SQ{i}", S0 + 4 * i, [P, T]) for i in range(2)]
        RS = at("RS", S0 + 8, [P, T])
        NTL = [at(f"NTL{i}", S0 + 12 + 4 * i, [P, T]) for i in range(2)]

        class NormCount:
            def __init__(self):
                self.sq, self.ss, self.nt = 0, 0, 0

        def norm_act(act, c, src):
            for k in range(KD):
                if c.sq + k >= 2:
                    act.wait_ge(sq_used, c.sq + k - 1)
                act.activation(SQ[k % 2][:, :], src[:, k, :], ACT.Square).then_inc(sq_ready, 1)
            act.wait_ge(sq_used, c.sq + KD)
            act.activation(RS[:, :], B67[:, :], ACT.Sqrt, scale=1.0 / D, bias=EPS).then_inc(rs_sqrt, 1)
            for k in range(KD):
                act.wait_ge(nt_ready, c.nt + k + 1)
                act.activation(XH[:, k, :], NTL[k % 2][:, :], ACT.Copy).then_inc(xh_ready, 1)

        def norm_pe(pe, c):
            for k in range(KD):
                pe.wait_ge(sq_ready, c.nt + k + 1)
                for half in range(2):
                    mm = pe.matmul(B67[:, half * H:half * H + H], ONES, SQ[k % 2][:, half * H:half * H + H],
                                   start=(k == 0), stop=(k == KD - 1))
                mm.then_inc(sq_used, 1)

        def norm_dve(dve, c, src, w):
            dve.wait_ge(rs_sqrt, c.ss + 1)
            dve.reciprocal(RS[:, :], RS[:, :]).then_inc(rs_ready, 1)
            dve.wait_ge(rs_ready, c.ss + 1)
            for k in range(KD):
                if c.nt + k >= 2:
                    dve.wait_ge(nt_used, c.nt + k - 1)
                dve.scalar_tensor_tensor(out=NTL[k % 2][:, :], in0=src[:, k, :], scalar=col(w, k), in1=RS[:, :],
                                         op0=ALU.mult, op1=ALU.mult).then_inc(nt_ready, 1)

        def norm_pool(pool, c):
            for k in range(KD):
                pool.wait_ge(xh_ready, c.nt + k + 1)
                pool.tensor_tensor(XL[:, k, :], NTL[k % 2][:, :], XH[:, k, :].bitcast(F32),
                                   ALU.subtract).then_inc(nt_used, 1)

        OG = [at(f"OG{g}", 64 + 16 * g, [P, NPAIR, T]) for g in range(NG)]
        QR, KR, VR = (at(n, S0 + o, [P, T]) for n, o in (("QR", 0), ("KR", 4), ("VR", 8)))
        ASQ = at("ASQ", S0 + 12, [P, T])
        ARS = at("ARS", S0 + 16, [P, T])
        VN = at("VN", S0 + 20, [P, 12, P])
        SS = [at(f"SS{i}", S0 + 26 + 2 * i, [P, 2, 256]) for i in range(2)]
        PP = [at(f"PP{i}", S0 + 30 + 2 * i, [P, 2, 256]) for i in range(2)]
        PTS = [at(f"PTS{i}", S0 + 34 + 2 * i, [P, 2, 2, P]) for i in range(2)]
        NM = at("NM", S0 + 38, [P, NG, NT, 8])
        LS = at("LS", S0 + 38.75, [P, NG, NT, 8])
        BIAS = at("BIAS", S0 + 39.5, [P, 384])
        MXT = at("MXT", S0 + 41, [P, 2, 2])
        SPS = [b[:, :].rearrange("p (h k) -> p h k", h=2) for b in (B45, B67)]
        PTP = [DP[0][:, i * H:i * H + H].rearrange("p (h c q) -> p h c q", h=2, c=2) for i in range(2)]
        PVP = [DP[1][:, i * H:i * H + P] for i in range(2)]
        VTP = [B45[:, 0:H], B45[:, H:T], B67[:, 0:H]]
        bias_in = once("bias_in")
        qr_ready, kr_ready, vr_ready, asq_ready, qk_normed = (once(n) for n in (
            "qr_ready", "kr_ready", "vr_ready", "asq_ready", "qk_normed"))
        vt_ready, vn_ready = once("vt_ready"), once("vn_ready")
        s_ready, s_read, mx_ready, nm_ready, p_ready, pt_ready, pt_evac, pv_ready, pv_evac = (once(n) for n in (
            "s_ready", "s_read", "mx_ready", "nm_ready", "p_ready", "pt_ready", "pt_evac", "pv_ready", "pv_evac"))

        def attn_pe(pe):
            def head_norm_sum(n):
                pe.wait_ge(asq_ready, n + 1)
                pe.wait_ge(rs_sqrt, n + 1)
                for half in range(2):
                    mm = pe.matmul(B67[:, half * H:half * H + H], BLK, ASQ[:, half * H:half * H + H],
                                   start=True, stop=True)
                mm.then_inc(sq_used, 1)

            with pe.Fori(0, NPAIR) as p:
                for g in range(NG):
                    gi = p * NG + g
                    u0 = gi * NT
                    pe.wait_ge(pt_evac, u0)
                    pe.wait_ge(pv_evac, u0)
                    product(pe, Block("attn", p, 3 * g), XH, XL)
                    product(pe, Block("attn", p, 3 * g + 1), XH, XL)
                    pe.wait_ge(s_read, u0)
                    head_norm_sum(gi * 2)
                    product(pe, Block("attn", p, 3 * g + 2), XH, XL)
                    head_norm_sum(gi * 2 + 1)
                    pe.wait_ge(vr_ready, gi + 1)
                    pe.wait_ge(rs_sqrt, gi * 2 + 3)
                    gate(pe, "pe")
                    for b in range(VBATCH[g]):
                        for c in range(4 * b, min(4 * b + 4, CHUNKS[g])):
                            view, n = att_chunk(g, c)
                            tr = pe.transpose(VTP[b][0:n, (c % 4) * P:(c % 4) * P + P],
                                              view(VR[:, :]), IDENT)
                        tr.then_inc(vt_ready, 1)
                    pe.wait_ge(vn_ready, p * VBP + (VB0[g] + VBATCH[g]))
                    pe.wait_ge(qk_normed, gi * 2 + 2)
                    freed(pe, Block("attn", p, 3 * g + 1))
                    freed(pe, Block("attn", p, 3 * g + 2))

                    def scores(t):
                        if t >= 2:
                            pe.wait_ge(s_read, u0 + (t - 1))
                        keys, w, _, _ = att_keys(g, t)
                        for h in range(2):
                            r = slice(64 * h, 64 * h + 64)
                            mm = pe.matmul(SPS[t % 2][:, h, 0:w], att_tokens(g, t)(QR[r, :]), keys(KR[r, :]),
                                           start=True, stop=True)
                        mm.then_inc(s_ready, 1)

                    def turn(t):
                        pe.wait_ge(p_ready, u0 + (t + 1))
                        if t >= 2:
                            pe.wait_ge(pt_evac, u0 + (t - 1))
                        gate(pe, "pe")
                        for h in range(2):
                            o = 0
                            for i, (_, n) in enumerate(att_keys(g, t)[3]):
                                tr = pe.transpose(PTP[t % 2][0:n, h, i, :], PP[t % 2][:, h, o:o + n], IDENT)
                                o += n
                        tr.then_inc(pt_ready, 1)

                    def values(t):
                        pe.wait_ge(pt_evac, u0 + (t + 1))
                        if t >= 2:
                            pe.wait_ge(pv_evac, u0 + (t - 1))
                        gate(pe, "pe")
                        chunks = att_keys(g, t)[3]
                        for h in range(2):
                            for i, (c, n) in enumerate(chunks):
                                mm = pe.matmul(PVP[t % 2][64 * h:64 * h + 64, :], VN[0:n, c, 64 * h:64 * h + 64],
                                               PTS[t % 2][0:n, h, i, :], start=(i == 0), stop=(i == len(chunks) - 1))
                        mm.then_inc(pv_ready, 1)

                    scores(0)
                    for t in range(NT):
                        if t + 1 < NT:
                            scores(t + 1)
                        turn(t)
                        if t >= 1:
                            values(t - 1)
                    values(NT - 1)

        def attn_act(act):
            with act.Fori(0, NPAIR) as p:
                for g in range(NG):
                    gi = p * NG + g
                    u0 = gi * NT
                    for i, (raw, ready) in enumerate(((QR, qr_ready), (KR, kr_ready))):
                        b = Block("attn", p, 3 * g + i)
                        act.wait_ge(mm_done, b.n + 1)
                        if i == 0:
                            act.wait_ge(s_ready, u0)
                        act.wait_ge(sq_used, gi * 2 + (KD + i))
                        act.activation(ASQ[:, :], DP[b.slot][:, :], ACT.Square).then_inc(asq_ready, 1)
                        act.activation(raw[:, :], DP[b.slot][:, :], ACT.Copy).then_inc(ready, 1)
                        act.wait_ge(ready, gi + 1)
                        act.sem_inc(psum_free[b.slot], 1)
                        act.wait_ge(sq_used, gi * 2 + (KD + i + 1))
                        if i == 0:
                            act.wait_ge(qk_normed, gi * 2)
                        else:
                            act.wait_ge(qk_normed, gi * 2 + 1)
                        act.activation(ARS[:, :], B67[:, :], ACT.Sqrt, scale=1.0 / 64, bias=EPS).then_inc(rs_sqrt, 1)
                    b = Block("attn", p, 3 * g + 2)
                    act.wait_ge(mm_done, b.n + 1)
                    act.activation(VR[:, :], DP[b.slot][:, :], ACT.Copy).then_inc(vr_ready, 1)
                    act.wait_ge(vr_ready, gi + 1)
                    act.sem_inc(psum_free[b.slot], 1)
                    for b in range(VBATCH[g]):
                        act.wait_ge(vt_ready, p * VBP + (VB0[g] + b + 1))
                        if b == 0:
                            act.wait_ge(pv_ready, u0)
                        c0, c1 = 4 * b, min(4 * b + 4, CHUNKS[g])
                        lens = [att_chunk(g, c)[1] for c in range(c0, c1)]
                        at_c = 0
                        while at_c < len(lens):
                            end = at_c
                            while end < len(lens) and lens[end] == lens[at_c]:
                                end += 1
                            n = lens[at_c]
                            src = VTP[b][0:n, at_c * P:end * P]
                            cp = act.activation(VN[0:n, c0 + at_c:c0 + end, :].rearrange("p c n -> p (c n)"), src,
                                                ACT.Copy)
                            at_c = end
                        cp.then_inc(vn_ready, 1)

                    def exponential(t):
                        act.wait_ge(nm_ready, u0 + (t + 1))
                        if t >= 2:
                            act.wait_ge(pt_ready, u0 + (t - 1))
                        w = att_keys(g, t)[1]
                        for h in range(2):
                            e = act.activation(PP[t % 2][:, h, 0:w], SS[t % 2][:, h, 0:w], ACT.Exp, scale=0.125,
                                               bias=NM[:, g, t, ds(p * 2 + h, 1)],
                                               accum_out=LS[:, g, t, ds(p * 2 + h, 1)])
                        e.then_inc(p_ready, 1)

                    def evacuate(t):
                        act.wait_ge(pt_ready, u0 + (t + 1))
                        if t >= 2:
                            act.wait_ge(pv_ready, u0 + (t - 1))
                        chunks = att_keys(g, t)[3]
                        if len({n for _, n in chunks}) == 1:
                            n, k = chunks[0][1], len(chunks)
                            cp = act.activation(PTS[t % 2][0:n, :, 0:k, :], PTP[t % 2][0:n, :, 0:k, :], ACT.Copy)
                        else:
                            for i, (_, n) in enumerate(chunks):
                                cp = act.activation(PTS[t % 2][0:n, :, i, :], PTP[t % 2][0:n, :, i, :], ACT.Copy)
                        cp.then_inc(pt_evac, 1)

                    for t in range(NT):
                        exponential(t)
                        if t >= 1:
                            evacuate(t - 1)
                    evacuate(NT - 1)

        def attn_dve(dve):
            dve.wait_ge(bias_in, 16)
            with dve.Fori(0, NPAIR) as p:
                for g in range(NG):
                    gi = p * NG + g
                    u0 = gi * NT
                    for i, (raw, ready, w) in enumerate(((QR, qr_ready, "qn"), (KR, kr_ready, "kn"))):
                        dve.wait_ge(rs_sqrt, gi * 2 + (i + 2))
                        dve.reciprocal(ARS[:, :], ARS[:, :]).then_inc(rs_ready, 1)
                        dve.wait_ge(rs_ready, gi * 2 + (i + 2))
                        dve.wait_ge(ready, gi + 1)
                        dve.scalar_tensor_tensor(out=raw[:, :], in0=raw[:, :], scalar=col(w), in1=ARS[:, :],
                                                 op0=ALU.mult, op1=ALU.mult).then_inc(qk_normed, 1)

                    def maximum(t):
                        dve.wait_ge(s_ready, u0 + (t + 1))
                        if t >= 2:
                            dve.wait_ge(p_ready, u0 + (t - 1))
                        _, w, off, _ = att_keys(g, t)
                        off = 256 if g == 2 else off
                        for h in range(2):
                            i = dve.scalar_tensor_tensor(out=SS[t % 2][:, h, 0:w], in0=BIAS[:, off:off + w],
                                                         scalar=CON[:, ds(p * 2 + (CST["slopes"][0] + 8 * g + h), 1)],
                                                         in1=SPS[t % 2][:, h, 0:w], op0=ALU.mult, op1=ALU.add)
                        i.then_inc(s_read, 1)
                        dve.wait_ge(s_read, u0 + (t + 1))
                        dve.tensor_reduce(MXT[:, t % 2, :], SS[t % 2][:, :, 0:w], AXX, ALU.max).then_inc(mx_ready, 1)
                        dve.wait_ge(mx_ready, u0 + (t + 1))
                        dve.tensor_scalar(NM[:, g, t, ds(p * 2, 2)], MXT[:, t % 2, :], -0.125, None,
                                          ALU.mult).then_inc(nm_ready, 1)

                    def collect(t):
                        dve.wait_ge(pv_ready, u0 + (t + 1))
                        o = att_tokens(g, t)(OG[g][:, ds(p, 1), :].rearrange("p a n -> p (a n)"))
                        src = PVP[t % 2]
                        dve.tensor_copy(o, src).then_inc(pv_evac, 1)

                    for t in range(NT):
                        maximum(t)
                        if t >= 2:
                            collect(t - 2)
                    collect(NT - 2)
                    collect(NT - 1)

        STM = [at(f"STM{g}", S0 + 4 * g, [8, T]) for g in range(NG)]
        STL = [at(f"STL{g}", S0 + 12 + 4 * g, [8, T]) for g in range(NG)]
        STX = at("STX", S0 + 24, [8, T])
        SEL = at("SEL", S0 + 46, [8, NPAIR, P])
        YH = at("YH", S0 + 30, [P, NPAIR, T], F32R)
        YL = at("YL", 64, [P, NPAIR, T], F32R)
        sel_in = once("sel_in")
        st_t, st_evac, st_max, st_sub, st_exp, st_mul, st_rec, st_w = (once(n) for n in (
            "st_t", "st_evac", "st_max", "st_sub", "st_exp", "st_mul", "st_rec", "st_w"))
        wb_ready, wb_used, og_sum = once("wb_ready"), once("wb_used"), once("og_sum")
        yh_ready, yl_ready = sem("yh_ready"), sem("yl_ready")
        BANKS = [DP[0], DP[1], B45, B67]
        UT = NPAIR * NG * NT

        def comb_pe(pe):
            pe.wait_ge(nm_ready, UT)
            pe.wait_ge(p_ready, UT)
            pe.wait_ge(pv_evac, UT)
            freed(pe, Block("attn", NPAIR - 1, 7))
            freed(pe, Block("attn", NPAIR - 1, 8))
            for n in range(6):
                g, stat = n // 2, (NM, LS)[n % 2]
                if n >= 4:
                    pe.wait_ge(st_evac, n - 3)
                for t in range(NT):
                    tr = pe.transpose(BANKS[n % 4][0:8, P * t:P * t + P], stat[:, g, t, :], IDENT)
                tr.then_inc(st_t, 1)
            pe.wait_ge(st_evac, 6)
            pe.wait_ge(st_w, NG)
            pe.wait_ge(sel_in, 16)
            for n in range(NPAIR * NG):
                p, g = n // NG, n % NG
                if n >= 4:
                    pe.wait_ge(wb_used, n - 3)
                for half in range(2):
                    mm = pe.matmul(BANKS[n % 4][:, half * H:half * H + H], SEL[:, p, :],
                                   STM[g][:, half * H:half * H + H], start=True, stop=True)
                mm.then_inc(wb_ready, 1)

        def comb_act(act):
            for n in range(6):
                g, dst = n // 2, (STM, STL)[n % 2][n // 2]
                act.wait_ge(st_t, n + 1)
                src = BANKS[n % 4][0:8, :]
                if g == 0:
                    act.activation(dst[:, :], src, ACT.Copy).then_inc(st_evac, 1)
                else:
                    r = (4, 8)[g - 1]
                    act.activation(dst[:, :].rearrange("p (s r) -> p r s", r=r),
                                   src.rearrange("p (r s) -> p r s", r=r), ACT.Copy).then_inc(st_evac, 1)
            for g in range(NG):
                act.wait_ge(st_sub, g + 1)
                act.activation(STM[g][:, :], STM[g][:, :], ACT.Exp).then_inc(st_exp, 1)
            for p in range(NPAIR):
                act.wait_ge(og_sum, 2 * p + 2)
                act.activation(YH[:, p, :], OG[0][:, p, :], ACT.Copy).then_inc(yh_ready, 1)

        def comb_dve(dve):
            dve.wait_ge(st_evac, 6)
            dve.tensor_tensor(STX[:, :], STM[0][:, :], STM[1][:, :], ALU.min).then_inc(st_max, 1)
            dve.wait_ge(st_max, 1)
            dve.tensor_tensor(STX[:, :], STX[:, :], STM[2][:, :], ALU.min).then_inc(st_max, 1)
            dve.wait_ge(st_max, 2)
            for g in range(NG):
                dve.tensor_tensor(STM[g][:, :], STX[:, :], STM[g][:, :], ALU.subtract).then_inc(st_sub, 1)
            for g in range(NG):
                dve.wait_ge(st_exp, g + 1)
                dve.tensor_tensor(STL[g][:, :], STL[g][:, :], STM[g][:, :], ALU.mult).then_inc(st_mul, 1)
            dve.wait_ge(st_mul, 3)
            dve.tensor_tensor(STX[:, :], STL[0][:, :], STL[1][:, :], ALU.add).then_inc(st_mul, 1)
            dve.wait_ge(st_mul, 4)
            dve.tensor_tensor(STX[:, :], STX[:, :], STL[2][:, :], ALU.add).then_inc(st_mul, 1)
            dve.wait_ge(st_mul, 5)
            dve.reciprocal(STX[:, :], STX[:, :]).then_inc(st_rec, 1)
            dve.wait_ge(st_rec, 1)
            for g in range(NG):
                dve.tensor_tensor(STM[g][:, :], STM[g][:, :], STX[:, :], ALU.mult).then_inc(st_w, 1)
            for n in range(NPAIR * NG):
                p, g = n // NG, n % NG
                dve.wait_ge(wb_ready, n + 1)
                dve.tensor_tensor(OG[g][:, p, :], OG[g][:, p, :], BANKS[n % 4][:, :], ALU.mult).then_inc(wb_used, 1)

        def comb_pool(pool):
            for p in range(NPAIR):
                for g in (1, 2):
                    pool.wait_ge(wb_used, NG * p + g + 1)
                    if g == 2:
                        pool.wait_ge(og_sum, 2 * p + 1)
                    pool.tensor_tensor(OG[0][:, p, :], OG[0][:, p, :], OG[g][:, p, :], ALU.add).then_inc(og_sum, 1)
                pool.wait_ge(yh_ready, p + 1)
                pool.tensor_tensor(YL[:, p, :], OG[0][:, p, :], YH[:, p, :].bitcast(F32),
                                   ALU.subtract).then_inc(yl_ready, 1)

        SG = [at(f"SG{i}", S0 + 4 * i, [P, T]) for i in range(2)]
        sg_ready, sg_used, mx_done = sem("sg_ready"), sem("sg_used"), sem("mx_done")

        def mix_pe(pe, name):
            with pe.Fori(0, 8) as m:
                product(pe, Block(name, m, 0), XH, XL)
                product(pe, Block(name, m, 1), YH, YL)

        def mix_act(act, name, done):
            with act.Fori(0, 8) as m:
                b = Block(name, m, 0)
                act.wait_ge(mm_done, b.n + 1)
                act.wait_ge(sg_used, m + done)
                act.activation(SG[0][:, :], DP[b.slot][:, :], ACT.Sigmoid).then_inc(sg_ready, 1)
                act.wait_ge(sg_ready, m + (done + 1))
                act.sem_inc(psum_free[b.slot], 1)

        def mix_dve(dve, name, done, add, first):
            with dve.Fori(0, 8) as m:
                b = Block(name, m, 1)
                dve.wait_ge(mm_done, b.n + 1)
                dve.wait_ge(sg_ready, m + (done + 1))
                o = MX[:, ds(m, 1), :].rearrange("p a n -> p (a n)")
                if add:
                    dve.tensor_tensor(SG[1][:, :], SG[0][:, :], DP[b.slot][:, :], ALU.mult).then_inc(sg_used, 1)
                    dve.wait_ge(sg_used, m + (done + 1))
                    dve.tensor_tensor(o, o, SG[1][:, :], ALU.add).then_inc(mx_done, 1)
                else:
                    dve.tensor_tensor(o, SG[0][:, :], DP[b.slot][:, :], ALU.mult).then_inc(sg_used, 1)
                    dve.wait_ge(sg_used, m + (done + 1))
                    dve.sem_inc(mx_done, 1)
                dve.wait_ge(mx_done, m + (done + 1))
                dve.sem_inc(psum_free[b.slot], 1)

        KN, VND = at("KN", 64, [P, NT, P]), at("VND", 68, [P, NT, P])
        OD = [at(f"OD{d}", 72 + 4 * d, [P, NT, P]) for d in range(2)]
        OA = at("OA", 80, [P, NPAIR, T])
        LM = at("LM", S0, [P, 7, 2, P])
        KQ = at("KQ", S0 + 7, [P, 2, T])
        ZS = at("ZS", S0 + 15, [P, T])
        ABN = at("ABN", S0 + 19, [P, NT, 48])
        CUM = at("CUM", S0 + 20.5, [P, 6, 2, NT, 8])
        PC = at("PC", S0 + 23.5, [P, 6, 2, NT, 2])
        EGT = at("EGT", S0 + 24.25, [P, 2, NT])
        Q0 = S0 + 24.5
        RB = at("RB", Q0, [P, 2, 2, P])
        EEs = [at(f"EE{i}", x, [P, 2, 2, 2, P]) for i, x in enumerate((Q0 + 2, 96))]
        ATSs = [at(f"ATS{i}", x, [P, 2, 2, P]) for i, x in enumerate((Q0 + 6, 100))]
        XXs = [at(f"XX{i}", x, [P, 2, 2, 2, P]) for i, x in enumerate((Q0 + 8, 102))]
        QDs = [at(f"QD{i}", x, [P, 2, P]) for i, x in enumerate((Q0 + 14, 106))]
        PM0 = at("PM0", 107, [P, 2, 2, P])
        PM = at("PM", Q0 + 12, [P, 2, 2, P])
        mx_dram = nc.dram_tensor("mx_dram", [P, KD, T], F32, kind="Internal").ap()
        mx_out, mx_in = once("mx_out"), once("mx_in")
        VB = at("VB", Q0 + 15, [P, 2, 2, 64])
        KBE = at("KBE", Q0 + 16, [P, 2, 2, 64])
        KDC = at("KDC", Q0 + 17, [P, 2, 2, 64])
        WT = at("WT", Q0 + 18, [P, 2, P])
        VNEW = at("VNEW", Q0 + 19, [P, 2, 2, 64])
        ST = at("ST", Q0 + 20, [P, 2, 64])
        SS16 = at("SS16", Q0 + 20.5, [P, 2 * NT])
        CVT = at("CVT", Q0, [P, T])
        DSQ = at("DSQ", Q0 + 4, [P, T])
        DRS = at("DRS", Q0 + 8, [P, T])
        VT = at("VT", Q0 + 12, [P, T])
        AB = at("AB", Q0, [48, T])
        AB1, AB2 = at("AB1", Q0 + 4, [16, T]), at("AB2", Q0 + 8, [16, T])
        NEA = at("NEA", Q0 + 12, [16, 1])
        BA = [DP[0][:, 0:H], DP[0][:, H:T]]
        BB = [DP[1][:, 0:H], DP[1][:, H:T]]
        BC = [B45[:, 0:H], B45[:, H:T]]
        BD = [B67[:, 0:H], B67[:, H:T]]
        BK = [[b[:, 0:256], b[:, 256:H]] for b in BD]
        lm_in = once("lm_in")
        ab_set, ab_act, ab_dve, abt, abn_ready, cum_ps, cum_act, cum_dve = (once(n) for n in (
            "ab_set", "ab_act", "ab_dve", "abt", "abn_ready", "cum_ps", "cum_act", "cum_dve"))
        cv_mid, cv_dve, cv_silu, dsq_ready, dsum, drs_root, drs_rec, dn_normed, z_ready, pc_ready = (once(n) for n in (
            "cv_mid", "cv_dve", "cv_silu", "dsq_ready", "dsum", "drs_root", "drs_rec", "dn_normed", "z_ready",
            "pc_ready"))
        kv_turned, kn_ready, vnd_ready, st_zero = (once(n) for n in ("kv_turned", "kn_ready", "vnd_ready", "st_zero"))
        rb_ready, r_ready, e_dve, er_ready, e_exp, kk_ready, a_ready, at_turned, at_ready, xx_pool, xx_init = (
            once(n) for n in ("rb_ready", "r_ready", "e_dve", "er_ready", "e_exp", "kk_ready", "a_ready", "at_turned",
                             "at_ready", "xx_pool", "xx_init"))
        prod_ready, pm_ready, upd_ready, xx_ready = (once(n) for n in (
            "prod_ready", "pm_ready", "upd_ready", "xx_ready"))
        qd_ready, kk_first = once("qd_ready"), once("kk_first")
        sc_ready, wt_turned, wt_ready, vnew_ps, vnew_ready, o_ps, o_read, dstate_ps, st_ready = (once(n) for n in (
            "sc_ready", "wt_turned", "wt_ready", "vnew_ps", "vnew_ready", "o_ps", "o_read", "dstate_ps", "st_ready"))
        o_sum, o_sq, o_red, o_root, o_rec, o_norm, o_turned, oa_done = (once(n) for n in (
            "o_sum", "o_sq", "o_red", "o_root", "o_rec", "o_norm", "o_turned", "oa_done"))
        NL = 6

        def bc(v, n):
            return v.rearrange("p (a k) -> p a k", a=1).broadcast_to([P, n, P])

        def part(x, l, t):
            return x.rearrange("p (m t b) -> p t m b", t=2, b=2 << l)[:, t]

        def part2(x, l, t):
            return x.rearrange("p h (m t b) -> p t h m b", t=2, b=2 << l)[:, t]

        def bc_part(d, kind, h, l):
            o = P * kind + 64 * h
            return BC[d][:, o:o + 64].rearrange("p (m b) -> p m b", b=2 << l)

        def bc_part2(d, kind, l):
            return BC[d][:, P * kind:P * kind + P].rearrange("p (h m b) -> p h m b", h=2, b=2 << l)

        def delta_pe(pe):
            product(pe, Block("dnab", 0, 0), XH, XL)
            pe.wait_ge(ab_act, 5)
            pe.wait_ge(ab_dve, 2)
            pe.wait_ge(mx_done, 8)
            for c in range(NT):
                tr = pe.transpose(B45[:, 48 * c:48 * c + 48], AB[:, P * c:P * c + P], IDENT[0:48, 0:48])
            tr.then_inc(abt, 1)
            pe.wait_ge(abn_ready, 1)
            for kind in range(2):
                for d in range(2):
                    o = H + (2 * kind + d) * 64
                    mm = pe.matmul(B45[:, o:o + 64].rearrange("p (c h) -> p c h", h=8),
                                   con("ones") if kind else con("tri", d, P), ABN[:, :, 8 * d:8 * d + 8],
                                   start=True, stop=True)
            mm.then_inc(cum_ps, 1)
            with pe.Fori(0, NPAIR) as p:
                pe.wait_ge(oa_done, p)
                for i in range(4):
                    product(pe, Block("dn", p, i), XH, XL)
                    if i in (1, 2):
                        n = p * 2 + i
                        pe.wait_ge(dsq_ready, n)
                        pe.wait_ge(drs_root, n - 1)
                        for half in range(2):
                            mm = pe.matmul(B67[:, half * H:half * H + H], BLK, DSQ[:, half * H:half * H + H],
                                           start=True, stop=True)
                        mm.then_inc(dsum, 1)
                pe.wait_ge(dn_normed, p * 2 + 2)
                pe.wait_ge(cv_silu, p * 3 + 3)
                pe.wait_ge(drs_root, p * 2 + 2)
                pe.wait_ge(cum_dve, 3)
                pe.wait_ge(cum_act, 4)
                for c in range(NT):
                    pe.transpose(B45[:, P * c:P * c + P], KQ[:, 0, P * c:P * c + P], IDENT)
                    tr = pe.transpose(B67[:, P * c:P * c + P], VT[:, P * c:P * c + P], IDENT)
                tr.then_inc(kv_turned, 1)
                pe.wait_ge(kn_ready, p + 1)
                pe.wait_ge(vnd_ready, p + 1)
                freed(pe, Block("dn", p, 2))
                freed(pe, Block("dn", p, 3))

                def decays(s):
                    j = (p * NT + s) * 2
                    for d in range(2):
                        tok = slice(P * (7 - s if d else s), P * (7 - s if d else s) + P)
                        if s > 1:
                            pe.wait_ge(st_ready, j + (d - 3))
                            pe.wait_ge(o_read, j + (d - 3))
                        pe.wait_ge(rb_ready, j + (d + 1))
                        pe.matmul(BA[d][:, 0:256], ONES, RB[:, d, :, :].rearrange("p h n -> p (h n)"),
                                  start=True, stop=True).then_inc(r_ready, 1)
                        for h in range(2):
                            r = slice(64 * h, 64 * h + 64)
                            mm = pe.matmul(BK[d][h].rearrange("p (a n) -> p a n", a=2),
                                           KQ[r, 0, tok], KQ[r, :, tok], start=True, stop=True)
                            if h == 0:
                                mm.then_inc(kk_first, 1)
                                pe.wait_ge(kk_first, j + (d + 1))
                        mm.then_inc(kk_ready, 1)

                def turn_a(s, d):
                    j = (p * NT + s) * 2
                    pe.wait_ge(a_ready, j + (d + 1))
                    pe.wait_ge(er_ready, j + (d + 1))
                    for h in range(2):
                        tr = pe.transpose(BA[d][:, P * h:P * h + P], EEs[s % 2][:, d, 0, h, :], IDENT)
                    tr.then_inc(at_turned, 1)

                decays(0)
                for d in range(2):
                    turn_a(0, d)
                for s in range(NT):
                    q = p * NT + s
                    j = q * 2
                    EE, ATS, XX, QD = EEs[s % 2], ATSs[s % 2], XXs[s % 2], QDs[s % 2]
                    more = s < NT - 1
                    for l in range(NL):
                        for d in range(2):
                            if l == 0:
                                pe.wait_ge(xx_init, j + (d + 1))
                            else:
                                pe.wait_ge(xx_ready, q * (2 * NL) + (2 * (l - 1) + d + 1))
                            for h in range(2):
                                mm = pe.matmul(BB[d][:, P * h:P * h + P], ATS[:, d, h, :], XX[:, d, 0, h, :],
                                               start=True, stop=True)
                            mm.then_inc(prod_ready, 1)
                        if more and l in (3, 4):
                            turn_a(s + 1, l - 3)
                        for d in range(2):
                            if l == 0 and s:
                                pe.wait_ge(o_read, j + (d - 1))
                            pe.wait_ge(pm_ready, q * (2 * NL) + (2 * l + d + 1))
                            for h in range(2):
                                if l < NL - 1:
                                    pe.matmul(bc_part(d, 0, h, l), XX[:, d, 1, h, :], part(PM[:, d, h, :], l, d),
                                              start=True, stop=True)
                                mm = pe.matmul(bc_part(d, 1, h, l), PM[:, d, h, :],
                                               part(XX[:, d, 1, h, :], l, 1 - d), start=True, stop=True)
                            mm.then_inc(upd_ready, 1)
                        if more and l == 0:
                            decays(s + 1)
                    for d in range(2):
                        pe.wait_ge(xx_ready, q * (2 * NL) + (2 * (NL - 1) + d + 1))
                        pe.wait_ge(sc_ready, j + (d + 1))
                        gate(pe, "pe")
                        for h in range(2):
                            mm = pe.matmul(BD[d][64 * h:64 * h + 64, 0:P], KBE[:, d, h, :], XX[:, d, 1, h, :],
                                           start=True, stop=True)
                        mm.then_inc(wt_turned, 1)
                    for d in range(2):
                        pe.wait_ge(wt_ready, j + (d + 1))
                        if more:
                            pe.wait_ge(at_ready, j + (d + 3))
                        if s:
                            pe.wait_ge(st_ready, j + (d - 1))
                        else:
                            pe.wait_ge(st_zero, p + 1)
                        for h in range(2):
                            r = slice(64 * h, 64 * h + 64)
                            o = (BA, BB)[h][d][:, 0:64]
                            pe.matmul(o, XX[:, d, 1, h, :], VB[:, d, h, :], start=True, stop=False)
                            mm = pe.matmul(o, WT[r, d, :], ST[r, d, :], start=False, stop=True)
                        mm.then_inc(vnew_ps, 1)
                    for d in range(2):
                        pe.wait_ge(vnew_ready, j + (d + 1))
                        pe.wait_ge(qd_ready, j + (d + 1))
                        for h in range(2):
                            r = slice(64 * h, 64 * h + 64)
                            o = (BC, BD)[h][d][:, 0:64]
                            pe.matmul(o, EE[:, d, 1, h, :], VNEW[:, d, h, :], start=True, stop=False)
                            mm = pe.matmul(o, QD[r, d, :], ST[r, d, :], start=False, stop=True)
                        mm.then_inc(o_ps, 1)
                        for h in range(2):
                            mm = pe.matmul(BA[d][64 * h:64 * h + 64, P:P + 64], KDC[:, d, h, :], VNEW[:, d, h, :],
                                           start=True, stop=True)
                        mm.then_inc(dstate_ps, 1)
                pe.wait_ge(o_norm, p + 1)
                pe.wait_ge(o_read, p * 16 + 16)
                for c in range(NT):
                    tr = pe.transpose(B45[:, P * c:P * c + P], OD[0][:, c, :], IDENT)
                tr.then_inc(o_turned, 1)

        def delta_act(act):
            b = Block("dnab", 0, 0)
            act.wait_ge(mm_done, last_block("mixb"))
            act.wait_ge(ab_set, 1)
            act.activation(NEA[:, :], COL[0:16, COLS["alog"]:COLS["alog"] + 1], ACT.Exp).then_inc(ab_act, 1)
            act.wait_ge(mm_done, b.n + 1)
            dp = DP[b.slot]
            dtb = COL[0:16, COLS["dtb"]:COLS["dtb"] + 1]
            act.activation(AB1[:, :], dp[0:16, :], ACT.Abs, bias=dtb).then_inc(ab_act, 1)
            act.wait_ge(ab_act, 2)
            act.activation(AB2[:, :], AB1[:, :], ACT.Exp, scale=-1.0).then_inc(ab_act, 1)
            act.wait_ge(ab_act, 3)
            act.activation(AB1[:, :], AB2[:, :], ACT.Ln, bias=1.0).then_inc(ab_act, 1)
            act.wait_ge(ab_act, 4)
            act.activation(AB2[:, :], dp[0:16, :], ACT.Relu, bias=dtb)
            act.activation(AB[32:48, :], dp[32:48, :], ACT.Sigmoid).then_inc(ab_act, 1)
            act.wait_ge(ab_act, 5)
            act.sem_inc(psum_free[b.slot], 1)
            act.wait_ge(abt, 1)
            act.activation(ABN[:, :, :].rearrange("p c n -> p (c n)"), B45[:, 0:48 * NT], ACT.Copy).then_inc(
                abn_ready, 1)
            act.wait_ge(cum_ps, 1)
            cum = B45[:, H:H + 256].rearrange("p (k d c h) -> p k d c h", k=2, d=2, h=8)
            act.activation(CUM[:, 1].rearrange("p d c h -> p (d c h)"), B45[:, H:H + P], ACT.Copy).then_inc(cum_act, 1)
            act.activation(CUM[:, 5].rearrange("p d c h -> p (d c h)"), B45[:, H + P:H + 256], ACT.Exp).then_inc(
                cum_act, 1)
            act.activation(CUM[:, 3].rearrange("p d c h -> p (d c h)"), B45[:, H:H + P], ACT.Exp).then_inc(cum_act, 1)
            act.wait_ge(cum_dve, 1)
            act.activation(CUM[:, 4], CUM[:, 4], ACT.Exp).then_inc(cum_act, 1)
            with act.Fori(0, NPAIR) as p:
                act.wait_ge(oa_done, p)
                for i in range(3):
                    b = Block("dn", p, i)
                    act.wait_ge(mm_done, b.n + 1)
                    if i:
                        act.wait_ge(cv_silu, p * 3 + i)
                    act.activation(CVT[:, :], DP[b.slot][:, :], ACT.Copy,
                                   scale=COL[:, ds(p + (COLS["dnconv"] + 12 + 4 * i), 1)]).then_inc(cv_mid, 1)
                    act.wait_ge(cv_dve, p * 6 + (2 * i + 2))
                    dst = (KQ[:, 1, :], KQ[:, 0, :], VT[:, :])[i]
                    act.activation(dst, CVT[:, :], ACT.Silu).then_inc(cv_silu, 1)
                    if i < 2:
                        act.wait_ge(cv_silu, p * 3 + (i + 1))
                        if i:
                            act.wait_ge(dsum, p * 2 + 1)
                        act.activation(DSQ[:, :], dst, ACT.Square).then_inc(dsq_ready, 1)
                    if i:
                        act.wait_ge(dsum, p * 2 + i)
                        act.wait_ge(dn_normed, p * 2 + (i - 1))
                        act.activation(DRS[:, :], B67[:, :], ACT.Sqrt, bias=EPS).then_inc(drs_root, 1)
                b = Block("dn", p, 3)
                act.wait_ge(mm_done, b.n + 1)
                act.activation(ZS[:, :], DP[b.slot][:, :], ACT.Silu).then_inc(z_ready, 1)
                act.wait_ge(z_ready, p + 1)
                act.sem_inc(psum_free[b.slot], 1)
                act.wait_ge(kv_turned, p + 1)
                act.activation(KN[:, :, :].rearrange("p c n -> p (c n)"), B45[:, :], ACT.Copy).then_inc(kn_ready, 1)

                def exponentials(s):
                    j = (p * NT + s) * 2
                    EE, ATS = EEs[s % 2], ATSs[s % 2]
                    for d in range(2):
                        act.wait_ge(r_ready, j + (d + 1))
                        act.wait_ge(vnd_ready, p + 1)
                        act.activation(RB[:, d].rearrange("p h n -> p (h n)"), BA[d][:, 0:256], ACT.Exp).then_inc(
                            er_ready, 1)
                        act.wait_ge(e_dve, j + (d + 1))
                        act.activation(EE[:, d, 0], EE[:, d, 0], ACT.Exp, scale=-1.0)
                        act.activation(EE[:, d, 1], EE[:, d, 1], ACT.Exp).then_inc(e_exp, 1)
                    for d in range(2):
                        act.wait_ge(at_turned, j + (d + 1))
                        act.activation(ATS[:, d].rearrange("p h n -> p (h n)"), BA[d][:, 0:256], ACT.Copy).then_inc(
                            at_ready, 1)

                exponentials(0)
                for s in range(NT):
                    q = p * NT + s
                    j = q * 2
                    if s < NT - 1:
                        exponentials(s + 1)
                    for d in range(2):
                        act.wait_ge(wt_turned, j + (d + 1))
                        act.activation(WT[:, d, :], BD[d][:, 0:P], ACT.Copy, scale=-1.0).then_inc(wt_ready, 1)
                    for d in range(2):
                        act.wait_ge(vnew_ps, j + (d + 1))
                        for h in range(2):
                            cp = act.activation(VNEW[:, d, h, :], (BA, BB)[h][d][:, 0:64], ACT.Copy)
                        cp.then_inc(vnew_ready, 1)
                    for d in range(2):
                        c = 7 - s if d else s
                        act.wait_ge(o_ps, j + (d + 1))
                        for h in range(2):
                            cp = act.activation(OD[d][:, c, 64 * h:64 * h + 64], (BC, BD)[h][d][:, 0:64], ACT.Copy)
                        cp.then_inc(o_read, 1)
                act.wait_ge(o_sum, p + 1)
                act.wait_ge(st_ready, p * 16 + 16)
                act.activation(OD[1][:, :, :], OD[0][:, :, :], ACT.Square).then_inc(o_sq, 1)
                act.wait_ge(o_red, p + 1)
                act.activation(SS16[:, :], SS16[:, :], ACT.Sqrt, scale=1.0 / 64, bias=EPS).then_inc(o_root, 1)

        def delta_dve(dve):
            dve.wait_ge(mm_done, last_block("mixb"))
            dve.memset(AB[:, :], 0.0).then_inc(ab_set, 1)
            dve.wait_ge(ab_set, 1)
            dve.wait_ge(ab_act, 5)
            dve.tensor_tensor(AB1[:, :], AB1[:, :], AB2[:, :], ALU.add).then_inc(ab_dve, 1)
            dve.wait_ge(ab_dve, 1)
            dve.tensor_scalar(AB[0:16, :], AB1[:, :], NEA[:, :], -1.0, ALU.mult, ALU.mult).then_inc(ab_dve, 1)
            dve.wait_ge(cum_act, 3)
            dve.tensor_tensor(CUM[:, 4].rearrange("p d c h -> p (d c h)"), B45[:, H + P:H + 256],
                              CUM[:, 1].rearrange("p d c h -> p (d c h)"), ALU.subtract).then_inc(cum_dve, 1)
            for d in range(2):
                dve.tensor_copy(CUM[:, 0, d], ABN[:, :, 8 * d:8 * d + 8])
                i = dve.tensor_copy(CUM[:, 2, d], ABN[:, :, 32 + 8 * d:40 + 8 * d])
            i.then_inc(cum_dve, 1)
            dve.wait_ge(cum_dve, 2)
            dve.tensor_tensor(CUM[:, 3], CUM[:, 3], CUM[:, 2], ALU.mult).then_inc(cum_dve, 1)
            dve.wait_ge(cum_dve, 3)
            dve.wait_ge(cum_act, 4)
            dve.wait_ge(lm_in, 16)
            dve.wait_ge(mx_out, 16)
            with dve.Fori(0, NPAIR) as p:
                dve.tensor_copy(PC[:, :, :, :, :].rearrange("p k d c h -> p (k d c) h"),
                                CUM[:, :, :, :, ds(p * 2, 2)].rearrange("p k d c h -> p (k d c) h")).then_inc(
                    pc_ready, 1)
                dve.wait_ge(pc_ready, p * 2 + 1)
                for h in range(2):
                    i = dve.tensor_copy(EGT[64 * h:64 * h + 64], PC[64 * h:64 * h + 64, 5, :, :, h])
                i.then_inc(pc_ready, 1)
                for i in range(3):
                    b = Block("dn", p, i)
                    dve.wait_ge(cv_mid, p * 3 + (i + 1))
                    for n, tap in enumerate((0, 2)):
                        dst = CVT[:, 1:T] if tap == 0 else CVT[:, 0:T - 1]
                        src = DP[b.slot][:, 0:T - 1] if tap == 0 else DP[b.slot][:, 1:T]
                        dve.scalar_tensor_tensor(out=dst, in0=src,
                                                 scalar=COL[:, ds(p + (COLS["dnconv"] + 12 * tap + 4 * i), 1)],
                                                 in1=dst, op0=ALU.mult, op1=ALU.add).then_inc(cv_dve, 1)
                        dve.wait_ge(cv_dve, p * 6 + (2 * i + n + 1))
                    dve.sem_inc(psum_free[b.slot], 1)
                    if i:
                        dve.wait_ge(drs_root, p * 2 + i)
                        dve.reciprocal(DRS[:, :], DRS[:, :]).then_inc(drs_rec, 1)
                        dve.wait_ge(drs_rec, p * 2 + i)
                        x = KQ[:, 2 - i, :]
                        dve.scalar_tensor_tensor(out=x, in0=x, scalar=(0.125, 1.0)[i - 1], in1=DRS[:, :],
                                                 op0=ALU.mult, op1=ALU.mult).then_inc(dn_normed, 1)
                dve.wait_ge(kv_turned, p + 1)
                dve.tensor_copy(VND[:, :, :].rearrange("p c n -> p (c n)"), B67[:, :]).then_inc(vnd_ready, 1)
                dve.wait_ge(vnd_ready, p + 1)
                dve.memset(ST[:, :, :], 0.0).then_inc(st_zero, 1)
                dve.wait_ge(st_zero, p + 1)

                def spread(s):
                    j = (p * NT + s) * 2
                    for d in range(2):
                        c = 7 - s if d else s
                        if s:
                            dve.wait_ge(qd_ready, j + (d - 1))
                        for h in range(2):
                            i = dve.tensor_scalar(RB[:, d, h, :], con("tri", d, P), PC[:, 0, d, c, h:h + 1], None,
                                                  ALU.mult)
                        i.then_inc(rb_ready, 1)

                def exponents(s, d):
                    j = (p * NT + s) * 2
                    EE, QD = EEs[s % 2], QDs[s % 2]
                    c = 7 - s if d else s
                    dve.wait_ge(r_ready, j + (d + 1))
                    dve.wait_ge(er_ready, j + (d + 1))
                    for k, mask in ((0, "mpos"), (1, "mneg")):
                        for h in range(2):
                            i = dve.scalar_tensor_tensor(out=EE[:, d, k, h, :], in0=BA[d][:, P * h:P * h + P],
                                                         scalar=PC[:, 1, d, c, h:h + 1], in1=con(mask, d, P),
                                                         op0=ALU.subtract, op1=ALU.add)
                    i.then_inc(e_dve, 1)
                    for h in range(2):
                        r = slice(64 * h, 64 * h + 64)
                        i = dve.tensor_tensor(QD[r, d, :], KQ[r, 1, P * c:P * c + P], RB[r, d, h, :], ALU.mult)
                    i.then_inc(qd_ready, 1)

                def decayed(s, d):
                    j = (p * NT + s) * 2
                    EE = EEs[s % 2]
                    c = 7 - s if d else s
                    dve.wait_ge(kk_ready, j + (d + 1))
                    dve.wait_ge(e_exp, j + (d + 1))
                    for h in range(2):
                        dve.scalar_tensor_tensor(out=EE[:, d, 0, h, :], in0=BK[d][h][:, 0:P],
                                                 scalar=PC[:, 2, d, c, h:h + 1], in1=EE[:, d, 0, h, :],
                                                 op0=ALU.mult, op1=ALU.mult)
                        i = dve.tensor_tensor(EE[:, d, 1, h, :], BK[d][h][:, P:256], EE[:, d, 1, h, :], ALU.mult)
                    i.then_inc(a_ready, 1)

                spread(0)
                for d in range(2):
                    exponents(0, d)
                for d in range(2):
                    decayed(0, d)
                for s in range(NT):
                    q = p * NT + s
                    j = q * 2
                    XX = XXs[s % 2]
                    more = s < NT - 1
                    if more:
                        spread(s + 1)
                    for l in range(NL):
                        if more and l in (1, 2):
                            exponents(s + 1, l - 1)
                        if more and l in (3, 4):
                            decayed(s + 1, l - 3)
                        for d in range(2):
                            n = q * (2 * NL) + (2 * l + d + 1)
                            dve.wait_ge(prod_ready, n)
                            dve.tensor_tensor(PM[:, d], BB[d][:, 0:256].rearrange("p (h n) -> p h n", h=2),
                                              bc(LM[:, l + 1, d, :], 2), ALU.mult).then_inc(pm_ready, 1)
                        for d in range(2):
                            n = q * (2 * NL) + (2 * l + d + 1)
                            dve.wait_ge(upd_ready, n)
                            for kind in range(0 if l < NL - 1 else 1, 2):
                                x = part2(XX[:, d, kind], l, (d, 1 - d)[kind])
                                i = dve.tensor_tensor(x, x, bc_part2(d, kind, l), ALU.subtract)
                            i.then_inc(xx_ready, 1)
                    for d in range(2):
                        c = 7 - s if d else s
                        dve.wait_ge(dstate_ps, j + (d + 1))
                        dve.scalar_tensor_tensor(out=ST[:, d, :], in0=ST[:, d, :], scalar=EGT[:, d, c:c + 1],
                                                 in1=BA[d][:, P:P + 64], op0=ALU.mult, op1=ALU.add).then_inc(
                            st_ready, 1)
                dve.wait_ge(o_sq, p + 1)
                dve.tensor_reduce(SS16[:, :], OD[1][:, :, :].rearrange("p c (h n) -> p (c h) n", h=2), AXX,
                                  ALU.add).then_inc(o_red, 1)
                dve.wait_ge(o_root, p + 1)
                dve.reciprocal(SS16[:, :], SS16[:, :]).then_inc(o_rec, 1)
                dve.wait_ge(o_rec, p + 1)
                o = OD[0][:, :, :].rearrange("p c (h n) -> p (c h) n", h=2)
                dve.tensor_tensor(o, o, SS16[:, :].rearrange("p (a k) -> p a k", k=1).broadcast_to([P, 2 * NT, 64]),
                                  ALU.mult).then_inc(o_norm, 1)
                dve.wait_ge(o_turned, p + 1)
                dve.wait_ge(z_ready, p + 1)
                dve.scalar_tensor_tensor(out=OA[:, ds(p, 1), :].rearrange("p a n -> p (a n)"), in0=B45[:, :],
                                         scalar=col("dnw"), in1=ZS[:, :], op0=ALU.mult,
                                         op1=ALU.mult).then_inc(oa_done, 1)

        def delta_pool(pool):
            split(pool, Block("dnab", 0, 0))
            pool.wait_ge(lm_in, 16)
            pool.wait_ge(mx_out, 16)
            with pool.Fori(0, NPAIR) as p:
                for i in range(4):
                    split(pool, Block("dn", p, i))
                pool.wait_ge(pc_ready, p * 2 + 2)
                pool.wait_ge(vnd_ready, p + 1)

                def first_level(s):
                    j = (p * NT + s) * 2
                    EE, ATS, XX = EEs[s % 2], ATSs[s % 2], XXs[s % 2]
                    for d in range(2):
                        pool.wait_ge(a_ready, j + (d + 1))
                        m = j * 4 + (4 * d)
                        pool.tensor_tensor(PM0[:, d], EE[:, d, 0], bc(LM[:, 0, d, :], 2), ALU.mult).then_inc(xx_pool, 1)
                        pool.wait_ge(xx_pool, m + 1)
                        pool.tensor_tensor(XX[:, d, 0], bc(IDENT, 2), PM0[:, d], ALU.subtract).then_inc(xx_pool, 1)
                        pool.wait_ge(at_ready, j + (d + 1))
                        pool.wait_ge(xx_pool, m + 2)
                        pool.tensor_tensor(PM0[:, d], ATS[:, d], bc(LM[:, 0, 1 - d, :], 2), ALU.mult).then_inc(
                            xx_pool, 1)
                        pool.wait_ge(xx_pool, m + 3)
                        pool.tensor_tensor(XX[:, d, 1], bc(IDENT, 2), PM0[:, d], ALU.subtract).then_inc(xx_pool, 1)
                        pool.wait_ge(xx_pool, m + 4)
                        pool.sem_inc(xx_init, 1)

                first_level(0)
                for s in range(NT):
                    q = p * NT + s
                    j = q * 2
                    for d in range(2):
                        c = 7 - s if d else s
                        if s:
                            pool.wait_ge(dstate_ps, j + (d - 1))
                        gate(pool, "pool")
                        for h in range(2):
                            hh = slice(64 * h, 64 * h + 64)
                            pool.tensor_scalar(VB[:, d, h, :], VND[:, c, hh], PC[:, 2, d, c, h:h + 1], None, ALU.mult)
                            pool.tensor_scalar(KBE[:, d, h, :], KN[:, c, hh], PC[:, 3, d, c, h:h + 1], None, ALU.mult)
                            i = pool.tensor_scalar(KDC[:, d, h, :], KN[:, c, hh], PC[:, 4, d, c, h:h + 1], None, ALU.mult)
                        i.then_inc(sc_ready, 1)
                    if s < NT - 1:
                        first_level(s + 1)
                pool.wait_ge(o_read, p * 16 + 16)
                pool.tensor_tensor(OD[0][:, :, :], OD[0][:, :, :], OD[1][:, :, :], ALU.add).then_inc(o_sum, 1)

        def oa_split(act, pool, n0):
            if act:
                act.wait_ge(oa_done, NPAIR)
                for p in range(NPAIR):
                    act.activation(YH[:, p, :], OA[:, p, :], ACT.Copy).then_inc(yh_ready, 1)
            if pool:
                for p in range(NPAIR):
                    pool.wait_ge(yh_ready, n0 + p + 1)
                    pool.tensor_tensor(YL[:, p, :], OA[:, p, :], YH[:, p, :].bitcast(F32),
                                       ALU.subtract).then_inc(yl_ready, 1)

        ms_hi, ms_lo = sem("ms_hi"), sem("ms_lo")

        def mx_split(act, pool, n0, src, free):
            if act:
                act.wait_ge(mm_done, free)
                for k in range(KD):
                    act.activation(XH[:, k, :], src[:, k, :], ACT.Copy).then_inc(ms_hi, 1)
            if pool:
                for k in range(KD):
                    pool.wait_ge(ms_hi, n0 + k + 1)
                    pool.tensor_tensor(XL[:, k, :], src[:, k, :], XH[:, k, :].bitcast(F32),
                                       ALU.subtract).then_inc(ms_lo, 1)

        def plain_pe(pe, name, hi, lo):
            with pe.Fori(0, 4) as m:
                for i in range(2):
                    product(pe, Block(name, m, i), hi, lo)

        def add_blocks_dve(dve, name, dst):
            with dve.Fori(0, 4) as m:
                for i in range(2):
                    b = Block(name, m, i)
                    dve.wait_ge(mm_done, b.n + 1)
                    o = dst[:, ds(m * 2 + i, 1), :].rearrange("p a n -> p (a n)")
                    dve.tensor_tensor(o, o, DP[b.slot][:, :], ALU.add).then_inc(psum_free[b.slot], 1)

        TG, TU = at("TG", S0, [P, T]), at("TU", S0 + 4, [P, T])
        HB = at("HB", S0 + 8, [P, 2, T])
        FH, FL = at("FH", S0 + 16, [P, 2, T], F32R), at("FL", S0 + 24, [P, 2, T], F32R)
        fc_mid, fc_dve, fg_silu, hb_ready, fh_ready, fl_ready = (sem(n) for n in (
            "fc_mid", "fc_dve", "fg_silu", "hb_ready", "fh_ready", "fl_ready"))

        def ffn_block(f, t, part):
            if isinstance(f, int):
                return Block("ffn0", 0, 2 * t + part)
            return Block("ffn", f[0], (0 if t == 0 else 4) + part)

        def ffn_pe(pe):
            for i in range(4):
                product(pe, Block("ffn0", 0, i), XH, XL)
            with pe.Fori(0, FT // 2 - 1) as it:
                for i in range(2):
                    product(pe, ffn_block((it, 1), 0, i), XH, XL)
                pe.wait_ge(fl_ready, it * 2 + 2)
                for i in range(2):
                    product4(pe, Block("ffn", it, 2 + i), it * 2 + i, FH, FL, i == 1)
                for i in range(2):
                    product(pe, ffn_block((it, 1), 1, i), XH, XL)
            pe.wait_ge(fl_ready, FT)
            for i in range(2):
                product4(pe, Block("ffn1", 0, i), FT - 2 + i, FH, FL, i == 1)

        def ffn_tile(act, dve, blocks_of, f, t):
            n = f * 2 + t
            if act:
                for part, dst in enumerate((TG, TU)):
                    b = blocks_of[part]
                    act.wait_ge(mm_done, b.n + 1)
                    act.wait_ge(hb_ready, n)
                    act.activation(dst[:, :], DP[b.slot][:, :], ACT.Copy,
                                   scale=COL[:, ds(f * 2 + (COLS["ffnconv"] + 44 + 22 * part + t), 1)]).then_inc(
                        fc_mid, 1)
                act.wait_ge(fc_dve, n * 4 + 2)
                act.activation(TG[:, :], TG[:, :], ACT.Silu).then_inc(fg_silu, 1)
            if dve:
                for part, dst in enumerate((TG, TU)):
                    b = blocks_of[part]
                    dve.wait_ge(fc_mid, n * 2 + (part + 1))
                    for i, tap in enumerate((0, 2)):
                        d = dst[:, 1:T] if tap == 0 else dst[:, 0:T - 1]
                        src = DP[b.slot][:, 0:T - 1] if tap == 0 else DP[b.slot][:, 1:T]
                        dve.scalar_tensor_tensor(
                            out=d, in0=src, scalar=COL[:, ds(f * 2 + (COLS["ffnconv"] + 44 * tap + 22 * part + t), 1)],
                            in1=d, op0=ALU.mult, op1=ALU.add).then_inc(fc_dve, 1)
                        dve.wait_ge(fc_dve, n * 4 + (2 * part + i + 1))
                    dve.sem_inc(psum_free[b.slot], 1)
                dve.wait_ge(fg_silu, n + 1)
                if t == 0 and not (isinstance(f, int) and f == 0) or t == 1:
                    dve.wait_ge(fl_ready, n - 1)
                dve.tensor_tensor(HB[:, t, :], TG[:, :], TU[:, :], ALU.mult).then_inc(hb_ready, 1)

        def ffn_split(act, pool, f, t, free):
            n = f * 2 + t
            if act:
                act.wait_ge(hb_ready, n + 1)
                if free is not None:
                    act.wait_ge(mm_done, free)
                act.activation(FH[:, t, :], HB[:, t, :], ACT.Copy).then_inc(fh_ready, 1)
            if pool:
                pool.wait_ge(fh_ready, n + 1)
                pool.tensor_tensor(FL[:, t, :], HB[:, t, :], FH[:, t, :].bitcast(F32), ALU.subtract).then_inc(
                    fl_ready, 1)

        def ffn_act(act):
            for t in range(2):
                ffn_tile(act, None, [ffn_block(0, t, i) for i in range(2)], 0, t)
                ffn_split(act, None, 0, t, None)
            with act.Fori(0, FT // 2 - 1) as it:
                done = Block("ffn", it, 3).n + 1
                for t in range(2):
                    ffn_tile(act, None, [ffn_block((it, 1), t, i) for i in range(2)], it + 1, t)
                    ffn_split(act, None, it + 1, t, done)

        def ffn_pool(pool):
            for i in range(4):
                split(pool, Block("ffn0", 0, i))
                if i == 1:
                    ffn_split(None, pool, 0, 0, None)
            with pool.Fori(0, FT // 2 - 1) as it:
                for i in range(6):
                    split(pool, Block("ffn", it, i))
                    if i == 1:
                        ffn_split(None, pool, it, 1, None)
                    if i == 5:
                        ffn_split(None, pool, it + 1, 0, None)
            ffn_split(None, pool, FT // 2 - 1, 1, None)

        def ffn_dve(dve):
            for t in range(2):
                ffn_tile(None, dve, [ffn_block(0, t, i) for i in range(2)], 0, t)
            with dve.Fori(0, FT // 2 - 1) as it:
                ffn_tile(None, dve, [ffn_block((it, 1), 0, i) for i in range(2)], it + 1, 0)
                for i in range(2):
                    add4(dve, Block("ffn", it, 2 + i), it * 2 + i, XR, m0=4 * i)
                ffn_tile(None, dve, [ffn_block((it, 1), 1, i) for i in range(2)], it + 1, 1)
            for i in range(2):
                add4(dve, Block("ffn1", 0, i), FT - 2 + i, XR, m0=4 * i)

        NP5 = 16
        S5P = at("S5P", 0, [P, 3 * 16 + 4 * 256])
        SM = at("SM", 5, [P, 40, 16])
        BZ = at("BZ", 8, [P, 2, NP5, 16])
        PW = at("PW", 10, [P, 2, 9, 16])
        PD = at("PD", 11.25, [P, 2, 9, 16])
        T1, T2 = at("T1", 12.5, [P, NP5, 8, 16]), at("T2", 20.5, [P, NP5, 8, 16])
        XB = at("XB", 28.5, [P, 2, NP5, 8, 16])
        W1 = at("W1", 44.5, [P, 2, NP5, P])
        CA = at("CA", 96, [P, 2, NP5, 8, 16])
        KL = at("KL", 112, [P, 2, NP5, 8, 16])
        KS = at("KS", S0, [16, NP5, 2, P])
        ZT = at("ZT", S0 + 16, [16, P])
        EP = at("EP", S0 + 17, [P, 2, 129, 16])
        w1_dram = nc.dram_tensor("w1_dram", [P, 2, NP5, P], F32, kind="Internal").ap()
        ca_dram = nc.dram_tensor("ca_dram", [P, 2, NP5, P], F32, kind="Internal").ap()
        ep_dram = nc.dram_tensor("ep_dram", [P, 2, 129 * 16], F32, kind="Internal").ap()
        r8_dram = nc.dram_tensor("r8_dram", [P, 16], F32, kind="Internal").ap()
        kp_dram = nc.dram_tensor("kp_dram", [16, 32, 256], F32, kind="Internal").ap()
        x2_dram = nc.dram_tensor("x2_dram", [P, KD, T], F32, kind="Internal").ap()
        s5p_in, pr_chain, pr_dt, pr_angle, pr_act, pr_xb, pr_ca, pr_kl, pr_ep = (once(n) for n in (
            "s5p_in", "pr_chain", "pr_dt", "pr_angle", "pr_act", "pr_xb", "pr_ca", "pr_kl", "pr_ep"))
        pr_w1t, pr_w1, pr_kps, pr_ks, pr_zero, pr_out = (once(n) for n in (
            "pr_w1t", "pr_w1", "pr_kps", "pr_ks", "pr_zero", "pr_out"))
        HALF = [x[:, i * H:i * H + H] for x in BANKS for i in range(2)]
        are, aim, ldt = (S5P[:, 16 * i:16 * i + 16] for i in range(3))
        Bre, Bim, Cre, Cim = (S5P[:, 48 + 256 * i:48 + 256 * i + 256].rearrange("p (t c) -> p t c", c=16)
                              for i in range(4))

        def prep_sp(sp):
            sp.wait_ge(pr_w1, 8)
            sp.dma_start(w1_dram, W1[:, :, :, :]).then_inc(pr_out, 16)
            sp.wait_ge(pr_ca, 1)
            sp.dma_start(ca_dram, CA[:, :, :, :, :].rearrange("p r t j c -> p r t (j c)")).then_inc(pr_out, 16)
            sp.wait_ge(pr_ep, 1)
            sp.dma_start(ep_dram, EP[:, :, :, :].rearrange("p r c t -> p r (c t)")).then_inc(pr_out, 16)
            sp.dma_start(r8_dram, SM[:, 8, :]).then_inc(pr_out, 16)
            sp.wait_ge(pr_zero, 1)
            sp.dma_start(kp_dram[:, :, 0:P],
                         ZT[:, :].rearrange("p (a k) -> p a k", a=1).broadcast_to([16, 32, P])).then_inc(pr_out, 16)
            sp.wait_ge(pr_ks, 8)
            sp.dma_start(kp_dram[:, :, P:256], KS[:, :, :, :].rearrange("p t g n -> p (t g) n")).then_inc(pr_out, 16)

        def prep_act(act):
            act.wait_ge(s5p_in, 16)
            act.activation(SM[:, 0, :], ldt, ACT.Exp).then_inc(pr_dt, 1)
            act.wait_ge(pr_angle, 1)
            act.activation(SM[:, 7, :], SM[:, 1, :], ACT.Exp)
            act.activation(SM[:, 8, :], SM[:, 1, :], ACT.Exp, scale=8.0)
            act.activation(SM[:, 9, :], SM[:, 1, :], ACT.Tanh, scale=0.5)
            act.activation(SM[:, 10:12, :], SM[:, 4:6, :], ACT.Sin, scale=0.5)
            act.activation(SM[:, 12:14, :], SM[:, 4:6, :], ACT.Sin).then_inc(pr_act, 1)
            for n in range(8):
                act.wait_ge(pr_w1t, n + 1)
                act.activation(W1[:, n // 4, 4 * (n % 4):4 * (n % 4) + 4, :].rearrange("p t n -> p (t n)"), HALF[n],
                               ACT.Copy).then_inc(pr_w1, 1)
            for n in range(8):
                act.wait_ge(pr_kps, n + 1)
                act.activation(KS[:, 4 * (n // 2):4 * (n // 2) + 4, n % 2, :],
                               HALF[n][0:16, :].rearrange("p (t n) -> p t n", t=4), ACT.Copy).then_inc(pr_ks, 1)

        def prep_pe(pe):
            pe.wait_ge(pr_xb, 1)
            for n in range(8):
                for i in range(4):
                    t = 4 * (n % 4) + i
                    tr = pe.transpose(HALF[n][:, P * i:P * i + P], XB[:, n // 4, t].rearrange("p j c -> p (j c)"),
                                      IDENT)
                tr.then_inc(pr_w1t, 1)
            pe.wait_ge(pr_w1, 8)
            pe.wait_ge(pr_kl, 1)
            for n in range(8):
                g = n % 2
                r = slice(64 * g, 64 * g + 64)
                for i in range(4):
                    t = 4 * (n // 2) + i
                    for ri in range(2):
                        mm = pe.matmul(HALF[n][0:16, P * i:P * i + P], BZ[r, ri, t, :],
                                       KL[r, ri, t].rearrange("p j c -> p (j c)"), start=(ri == 0), stop=(ri == 1))
                mm.then_inc(pr_kps, 1)

        def prep_dve(dve):
            n = [0]

            def link(ins):
                n[0] += 1
                ins.then_inc(pr_chain, 1)
                dve.wait_ge(pr_chain, n[0])

            def tt(o, x, y, op):
                link(dve.tensor_tensor(o, x, y, op))

            dve.memset(ZT[:, :], 0.0).then_inc(pr_zero, 1)
            s = lambda i: SM[:, i, :]
            dve.wait_ge(s5p_in, 16)
            dve.wait_ge(pr_dt, 1)
            tt(s(1), are, s(0), ALU.mult)
            tt(s(2), aim, s(0), ALU.mult)
            link(dve.tensor_scalar(s(3), s(2), 8.0, None, ALU.mult))
            magic = 12582912.0
            c1, c2 = 6.28125, 2029.0 / 2 ** 20
            c3 = 2 * np.pi - c1 - c2
            k, ph = SM[:, 14:16, :], SM[:, 4:6, :]
            link(dve.tensor_scalar(k, SM[:, 2:4, :], 1 / (2 * np.pi), magic, ALU.mult, ALU.add))
            link(dve.tensor_scalar(k, k, magic, None, ALU.subtract))
            link(dve.scalar_tensor_tensor(out=ph, in0=k, scalar=-c1, in1=SM[:, 2:4, :], op0=ALU.mult, op1=ALU.add))
            link(dve.scalar_tensor_tensor(out=ph, in0=k, scalar=-c2, in1=ph, op0=ALU.mult, op1=ALU.add))
            link(dve.scalar_tensor_tensor(out=ph, in0=k, scalar=-c3, in1=ph, op0=ALU.mult, op1=ALU.add))
            link(dve.tensor_scalar(ph, ph, 3.1415925, -3.1415925, ALU.min, ALU.max))
            dve.sem_inc(pr_angle, 1)
            dve.wait_ge(pr_act, 1)
            link(dve.scalar_tensor_tensor(out=SM[:, 16:18, :], in0=SM[:, 10:12, :], scalar=-2.0,
                                          in1=SM[:, 10:12, :], op0=ALU.mult, op1=ALU.mult))
            link(dve.tensor_scalar(SM[:, 18:20, :], SM[:, 16:18, :], 1.0, None, ALU.add))
            link(dve.tensor_scalar(s(20), s(9), -1.0, 1.0, ALU.mult, ALU.add))
            link(dve.reciprocal(s(20), s(20)))
            link(dve.scalar_tensor_tensor(out=s(20), in0=s(9), scalar=2.0, in1=s(20), op0=ALU.mult, op1=ALU.mult))
            tt(s(21), s(7), s(18), ALU.mult)
            tt(s(22), s(7), s(12), ALU.mult)
            tt(s(23), s(20), s(18), ALU.mult)
            tt(s(23), s(23), s(16), ALU.add)
            tt(s(24), are, are, ALU.mult)
            tt(s(25), aim, aim, ALU.mult)
            tt(s(24), s(24), s(25), ALU.add)
            link(dve.reciprocal(s(24), s(24)))
            tt(s(25), s(23), are, ALU.mult)
            tt(s(26), s(22), aim, ALU.mult)
            tt(s(25), s(25), s(26), ALU.add)
            tt(s(25), s(25), s(24), ALU.mult)
            tt(s(26), s(22), are, ALU.mult)
            tt(s(27), s(23), aim, ALU.mult)
            tt(s(26), s(26), s(27), ALU.subtract)
            tt(s(26), s(26), s(24), ALU.mult)

            def cmul(ore, oim, xre, xim, yre, yim, t1, t2, sign=1):
                tt(ore, xre, yre, ALU.mult)
                tt(t1, xim, yim, ALU.mult)
                tt(ore, ore, t1, ALU.subtract)
                tt(oim, xre, yim, ALU.mult)
                tt(t2, xim, yre, ALU.mult)
                if sign > 0:
                    tt(oim, oim, t2, ALU.add)
                else:
                    link(dve.scalar_tensor_tensor(out=oim, in0=oim, scalar=-1.0, in1=t2, op0=ALU.mult,
                                                  op1=ALU.subtract))

            def over(v, m):
                return v.rearrange("p (t k) -> p t k", k=1).broadcast_to([P, 16, m])

            t1, t2 = T1[:, :, 0, :], T2[:, :, 0, :]
            cmul(BZ[:, 0], BZ[:, 1], over(s(25), 16), over(s(26), 16), Bre, Bim, t1, t2)
            link(dve.memset(PW[:, 0, 0, :], 1.0))
            link(dve.memset(PW[:, 1, 0, :], 0.0))
            link(dve.tensor_copy(PW[:, 0, 1, :], s(21)))
            link(dve.tensor_copy(PW[:, 1, 1, :], s(22)))
            for m in (1, 2, 4):
                y = [PW[:, ri, m:m + 1, :].broadcast_to([P, m, 16]) for ri in range(2)]
                cmul(PW[:, 0, m + 1:2 * m + 1, :], PW[:, 1, m + 1:2 * m + 1, :], PW[:, 0, 1:m + 1, :],
                     PW[:, 1, 1:m + 1, :], y[0], y[1], T1[:, 0, 0:m, :], T2[:, 0, 0:m, :])
            for ri in range(2):
                for m in range(9):
                    link(dve.tensor_copy(PD[:, ri, m, :], PW[:, ri, 8 - m, :]))

            def power(src, ri, lo):
                return src[:, ri, lo:lo + 8, :].rearrange("p (k a) t -> p t k a", a=1).broadcast_to([P, 16, 8, 16])

            def coef(v):
                return v.rearrange("p t (a c) -> p t a c", a=1).broadcast_to([P, 16, 8, 16])

            cmul(XB[:, 0], XB[:, 1], power(PD, 0, 1), power(PD, 1, 1), coef(BZ[:, 0]), coef(BZ[:, 1]), T1[:, :], T2[:, :])
            dve.sem_inc(pr_xb, 1)
            cmul(CA[:, 0], CA[:, 1], power(PW, 0, 1), power(PW, 1, 1), coef(Cre), coef(Cim), T1[:, :], T2[:, :], -1)
            dve.sem_inc(pr_ca, 1)
            cmul(KL[:, 0], KL[:, 1], power(PW, 0, 0), power(PW, 1, 0), coef(Cre), coef(Cim), T1[:, :], T2[:, :], -1)
            dve.sem_inc(pr_kl, 1)
            link(dve.memset(EP[:, 0, 0, :], 1.0))
            link(dve.memset(EP[:, 1, 0, :], 0.0))
            link(dve.tensor_copy(EP[:, 0, 1, :], s(19)))
            link(dve.tensor_copy(EP[:, 1, 1, :], s(13)))
            m = 1
            f1 = T1[:, :, :, :].rearrange("p t j c -> p (t j) c")
            f2 = T2[:, :, :, :].rearrange("p t j c -> p (t j) c")
            while m < P:
                y = [EP[:, ri, m:m + 1, :].broadcast_to([P, m, 16]) for ri in range(2)]
                cmul(EP[:, 0, m + 1:2 * m + 1, :], EP[:, 1, m + 1:2 * m + 1, :], EP[:, 0, 1:m + 1, :],
                     EP[:, 1, 1:m + 1, :], y[0], y[1], f1[:, 0:m, :], f2[:, 0:m, :])
                m *= 2
            dve.sem_inc(pr_ep, 1)


        c1 = NormCount()
        c2 = NormCount()
        c2.sq, c2.ss, c2.nt = KD + 2 * NG * NPAIR, 1 + 2 * NG * NPAIR, KD
        c3 = NormCount()
        c3.sq, c3.ss, c3.nt = c2.sq + KD, c2.ss + 1, c2.nt + KD
        c4 = NormCount()
        c4.sq, c4.ss, c4.nt = c3.sq + KD, c3.ss + 1, c3.nt + KD

        with nc.Block() as block:
            @block.sync
            def _(sp):
                sp.dma_start(COL[:, :], a["cols"]).then_inc(con_in, 16)
                sp.dma_start(CON[:, :], a["cst"]).then_inc(con_in, 16)
                sp.dma_start(S5P[:, :], a["s5p"]).then_inc(s5p_in, 16)
                sp.dma_start(XR[:, :, :], a["x"]).then_inc(x_in, 16)
                prep_sp(sp)
                sp.wait_ge(pr_out, 96)
                sp.dma_start(BIAS[:, :], a["bias"]).then_inc(bias_in, 16)
                sp.dma_start(SEL[:, :, :], a["sel"]).then_inc(sel_in, 16)
                with sp.Fori(0, NPAIR) as p:
                    for i in range(9):
                        load(sp, Block("attn", p, i), a["w_attn"])
                with sp.Fori(0, 8) as m:
                    load(sp, Block("mixb", m, 0), a["w_gateb"], m)
                    load(sp, Block("mixb", m, 1), a["w_attnout"], m)
                sp.wait_ge(mx_done, 8)
                sp.dma_start(LM[:, :, :, :], a["levels"]).then_inc(lm_in, 16)
                sp.dma_start(mx_dram, MX[:, :, :]).then_inc(mx_out, 16)
                load(sp, Block("dnab", 0, 0), a["w_ab"])
                with sp.Fori(0, NPAIR) as p:
                    for i in range(4):
                        load(sp, Block("dn", p, i), a["w_dn"])
                sp.wait_ge(mx_out, 16)
                sp.wait_ge(st_ready, NPAIR * 16)
                sp.wait_ge(o_read, NPAIR * 16)
                sp.dma_start(MX[:, :, :], mx_dram).then_inc(mx_in, 16)
                with sp.Fori(0, 8) as m:
                    load(sp, Block("mixa", m, 0), a["w_gatea"], m)
                    load(sp, Block("mixa", m, 1), a["w_dnout"], m)
                sp.wait_ge(mm_done, last_block("mixa"))
                sp.wait_ge(yl_ready, 8)
                sp.dma_start(XR[:, :, :], a["x"]).then_inc(x_in, 16)
                with sp.Fori(0, 4) as m:
                    for i in range(2):
                        load(sp, Block("wo", m, i), a["w_o"])
                for i in range(4):
                    load(sp, Block("ffn0", 0, i), a["w_up"], i)
                with sp.Fori(0, FT // 2 - 1) as it:
                    for i in range(2):
                        load(sp, Block("ffn", it, i), a["w_up"], it * 4 + (4 + i))
                    for i in range(2):
                        load(sp, Block("ffn", it, 2 + i), a["w_down"], it * 2 + i)
                    for i in range(2):
                        load(sp, Block("ffn", it, 4 + i), a["w_up"], it * 4 + (6 + i))
                for i in range(2):
                    load(sp, Block("ffn1", 0, i), a["w_down"], FT - 2 + i)

            @block.gpsimd
            def _(pool):
                pool.wait_ge(pr_out, 96)
                norm_pool(pool, c1)
                with pool.Fori(0, NPAIR) as p:
                    for i in range(9):
                        split(pool, Block("attn", p, i))
                comb_pool(pool)
                with pool.Fori(0, 8) as m:
                    split(pool, Block("mixb", m, 0))
                    split(pool, Block("mixb", m, 1))
                delta_pool(pool)
                oa_split(None, pool, 4)
                with pool.Fori(0, 8) as m:
                    split(pool, Block("mixa", m, 0))
                    split(pool, Block("mixa", m, 1))
                mx_split(None, pool, 0, MX, None)
                with pool.Fori(0, 4) as m:
                    for i in range(2):
                        split(pool, Block("wo", m, i))
                norm_pool(pool, c2)
                ffn_pool(pool)
                for i in range(2):
                    split(pool, Block("ffn1", 0, i))

            @block.scalar
            def _(act):
                act.wait_ge(con_in, 32)
                act.wait_ge(x_in, 16)
                prep_act(act)
                act.wait_ge(pr_out, 96)
                norm_act(act, c1, XR)
                attn_act(act)
                comb_act(act)
                act.wait_ge(st_w, NG)
                mix_act(act, "mixb", 0)
                delta_act(act)
                oa_split(act, None, 4)
                mix_act(act, "mixa", 8)
                act.wait_ge(mx_done, 16)
                mx_split(act, None, 0, MX, last_block("mixa"))
                freed(act, Block("wo", 3, 0))
                freed(act, Block("wo", 3, 1))
                norm_act(act, c2, XR)
                ffn_act(act)

            @block.vector
            def _(dve):
                dve.wait_ge(con_in, 32)
                dve.wait_ge(x_in, 16)
                prep_dve(dve)
                dve.wait_ge(pr_out, 96)
                norm_dve(dve, c1, XR, "norm1")
                attn_dve(dve)
                comb_dve(dve)
                dve.wait_ge(og_sum, 2 * NPAIR)
                mix_dve(dve, "mixb", 0, False, True)
                delta_dve(dve)
                dve.wait_ge(yh_ready, 8)
                dve.wait_ge(mx_in, 16)
                mix_dve(dve, "mixa", 8, True, False)
                dve.wait_ge(x_in, 32)
                add_blocks_dve(dve, "wo", XR)
                norm_dve(dve, c2, XR, "norm2")
                ffn_dve(dve)

            @block.tensor
            def _(pe):
                pe.wait_ge(con_in, 32)
                prep_pe(pe)
                pe.wait_ge(pr_ks, 8)
                norm_pe(pe, c1)
                pe.wait_ge(xh_ready, KD)
                pe.wait_ge(nt_used, KD)
                attn_pe(pe)
                comb_pe(pe)
                pe.wait_ge(wb_used, NPAIR * NG)
                pe.wait_ge(yl_ready, 4)
                mix_pe(pe, "mixb")
                delta_pe(pe)
                pe.wait_ge(oa_done, NPAIR)
                pe.wait_ge(yl_ready, 8)
                mix_pe(pe, "mixa")
                pe.wait_ge(ms_hi, KD)
                pe.wait_ge(ms_lo, KD)
                plain_pe(pe, "wo", XH, XL)
                norm_pe(pe, c2)
                pe.wait_ge(xh_ready, c2.nt + KD)
                pe.wait_ge(nt_used, c2.nt + KD)
                ffn_pe(pe)


        nc.clear_and_free_semaphores(first)
        nc.all_engine_barrier()
        X5 = at("X5", 96, [P, 32, 8, 16])
        U5 = at("U5", 112, [P, 32, P])
        E5 = at("E5", S0, [P, 2, 129, 16])
        QZ = at("QZ", S0 + 16.5, [P, 2, NP5, P])
        D0 = at("D0", S0 + 32.5, [P, NP5, P])
        SV = [at(f"SV{i}", S0 + 32.5 + 4 * i, [P, 2, 4, P]) for i in range(2)]
        MS = at("MS", S0 + 40.5, [P, 8, P])
        DROW = at("DROW", 64, [P, 32, 16])
        F1, F2 = at("F1", 66, [P, 4, P]), at("F2", 68, [P, 4, P])
        WS = [at(f"WS{i}", 70 + 4 * i, [P, 2, 4, P]) for i in range(2)]
        G5 = at("G5", 80, [P, NPAIR, T])
        R8 = at("R8", 153.25, [P, 16])
        YH5 = at("YH5", S0 + 20, [P, NPAIR, T], F32R)
        YL5 = at("YL5", 64, [P, NPAIR, T], F32R)
        s5_in, ws_in, ms_in, x2_out = [sem("s5_in"), [sem("ws_in0"), sem("ws_in1")], sem("ms_in"), sem("x2_out")]
        x5_ready, g5_ready, d0_ready, ut, u5_ready, u5_dve, x5_scaled, p_ps, q_ready, q_chain, z_done = (
            sem(n) for n in ("x5_ready", "g5_ready", "d0_ready", "ut", "u5_ready", "u5_dve", "x5_scaled", "p_ps",
                             "q_ready", "q_chain", "z_done"))
        sv_ready, y_ps, y_ready, ge_ready, yt, yh5_ready, yl5_ready = (sem(n) for n in (
            "sv_ready", "y_ps", "y_ready", "ge_ready", "yt", "yh5_ready", "yl5_ready"))
        ga_ready, g5_mul, g5_done = sem("ga_ready"), sem("g5_mul"), sem("g5_done")

        def s5_sp(sp):
            sp.dma_start(x2_dram, XR[:, :, :]).then_inc(x2_out, 16)
            sp.wait_ge(nt_used, c3.nt + KD)
            sp.wait_ge(xh_ready, c3.nt + KD)
            sp.dma_start(E5[:, :, :, :].rearrange("p r c t -> p r (c t)"), ep_dram).then_inc(s5_in, 16)
            sp.dma_start(R8[:, :], r8_dram).then_inc(s5_in, 16)
            sp.wait_ge(x2_out, 16)
            sp.dma_start(DROW[:, :, :].rearrange("p g c -> p (g c)"), a["s5d"].broadcast_to([P, 512])).then_inc(
                s5_in, 16)

        def s5_sp_stream(sp):
            for b in range(8):
                if b >= 2:
                    if b < 6:
                        sp.wait_ge(p_ps, b - 1)
                    else:
                        sp.wait_ge(y_ps, b - 5)
                src = (w1_dram, ca_dram)[b // 4]
                sp.dma_start(WS[b % 2][:, :, :, :], src[:, :, 4 * (b % 4):4 * (b % 4) + 4, :]).then_inc(
                    ws_in[b % 2], 16)
                if b >= 4:
                    m = b - 4
                    if m:
                        sp.wait_ge(y_ps, m)
                    for j in range(8):
                        sp.dma_start(MS[16 * j:16 * j + 16, :, :],
                                     kp_dram[:, 8 * m:8 * m + 8, P - 16 * j:256 - 16 * j]).then_inc(ms_in, 16)

        def s5_pe(pe):
            with pe.Fori(0, 2) as m:
                for i in range(2):
                    b = Block("s5x", m, i)
                    pe.wait_ge(w_split, b.n + 1)
                    pe.wait_ge(psum_free[b.slot], b.loads - 1)
                    for j in range(8):
                        for k in range(KD):
                            for x, w, one, end in ((XH, WH, k == 0, False), (XL, WH, False, False),
                                                   (XH, WL, False, k == KD - 1)):
                                mm = pe.matmul(DP[b.slot][:, P * j:P * j + P],
                                               x[:, k, :].rearrange("p (s j) -> p j s", j=8)[:, j, :],
                                               w[b.slot][:, k, :], start=one, stop=end)
                    mm.then_inc(mm_done, 1)
            with pe.Fori(0, 2) as m:
                for i in range(2):
                    product(pe, Block("s5g", m, i), XH, XL)
            freed(pe, Block("s5g", 1, 0))
            freed(pe, Block("s5g", 1, 1))
            pe.wait_ge(x5_ready, 4)
            for n in range(8):
                for i in range(4):
                    tr = pe.transpose(HALF[n][:, P * i:P * i + P], X5[:, 4 * n + i].rearrange("p j c -> p (j c)"),
                                      IDENT)
                tr.then_inc(ut, 1)
            pe.wait_ge(u5_ready, 4)
            pe.wait_ge(u5_dve, 4)
            for b in range(4):
                pe.wait_ge(ws_in[b % 2], 16 * (b // 2 + 1))
                for ri in range(2):
                    for i in range(4):
                        for g in range(2):
                            mm = pe.matmul(HALF[2 * b + ri][64 * g:64 * g + 64, P * i:P * i + P],
                                           WS[b % 2][:, ri, i, 64 * g:64 * g + 64], U5[:, 2 * (4 * b + i) + g, :],
                                           start=True, stop=True)
                mm.then_inc(p_ps, 1)
            for b in range(4):
                pe.wait_ge(ws_in[b % 2], 16 * (b // 2 + 3))
                pe.wait_ge(ms_in, 128 * (b + 1))
                pe.wait_ge(sv_ready, b + 1)
                for g in range(2):
                    r = slice(64 * g, 64 * g + 64)
                    for i in range(4):
                        o = HALF[2 * b + g][:, P * i:P * i + P]
                        pe.matmul(o, U5[:, 2 * (4 * b + i) + g, :], MS[:, 2 * i + g, :], start=True, stop=False)
                        pe.matmul(o, SV[b % 2][r, 0, i, :], WS[b % 2][r, 0, i, :], start=False, stop=False)
                        mm = pe.matmul(o, SV[b % 2][r, 1, i, :], WS[b % 2][r, 1, i, :], start=False, stop=True)
                mm.then_inc(y_ps, 1)
            for b in range(4):
                pe.wait_ge(ge_ready, b + 1)
                for j in range(8):
                    tr = pe.transpose(BANKS[b][:, P * j:P * j + P], U5[:, 8 * b + j, :], IDENT)
                tr.then_inc(yt, 1)
            pe.wait_ge(yh5_ready, 4)
            pe.wait_ge(yl5_ready, 4)
            with pe.Fori(0, 4) as m:
                for i in range(2):
                    product(pe, Block("glu", m, i), YH5, YL5)

        def s5_act(act):
            with act.Fori(0, 2) as m:
                for i in range(2):
                    b = Block("s5x", m, i)
                    act.wait_ge(mm_done, b.n + 1)
                    act.activation(X5[:, ds(m * 16 + 8 * i, 8)].rearrange("p g j c -> p j g c"),
                                   DP[b.slot][:, :].rearrange("p (j g c) -> p j g c", j=8, g=8), ACT.Copy).then_inc(
                        x5_ready, 1)
                    act.wait_ge(x5_ready, m * 2 + (i + 1))
                    act.sem_inc(psum_free[b.slot], 1)
            with act.Fori(0, 2) as m:
                for i in range(2):
                    b = Block("s5g", m, i)
                    act.wait_ge(mm_done, b.n + 1)
                    act.wait_ge(x2_out, 16)
                    act.activation(G5[:, ds(m * 2 + i, 1), :].rearrange("p a n -> p (a n)"), DP[b.slot][:, :],
                                   ACT.Silu).then_inc(psum_free[b.slot], 1)
            for n in range(0, 8, 2):
                act.wait_ge(ut, n + 1)
                act.activation(U5[:, 4 * n:4 * n + 4, :].rearrange("p t n -> p (t n)"), HALF[n], ACT.Copy).then_inc(
                    u5_ready, 1)
            for b in range(4):
                act.wait_ge(y_ready, 2 * b + 2)
                act.activation(U5[:, 8 * b:8 * b + 8, :].rearrange("p j (g c) -> p g j c", g=8),
                               X5[:, 8 * b:8 * b + 8], ACT.Gelu_apprx_tanh).then_inc(ge_ready, 1)
            act.wait_ge(z_done, 2)
            act.wait_ge(sv_ready, 4)
            for b in range(4):
                act.wait_ge(yt, b + 1)
                act.activation(YH5[:, b, :].rearrange("p (s j) -> p j s", j=8),
                               BANKS[b][:, :].rearrange("p (j s) -> p j s", j=8), ACT.Copy).then_inc(yh5_ready, 1)
            act.wait_ge(yh5_ready, 4)
            with act.Fori(0, 4) as m:
                b = Block("glu", m, 1)
                act.wait_ge(mm_done, b.n + 1)
                act.wait_ge(g5_mul, m)
                act.activation(SG[0][:, :], DP[b.slot][:, :], ACT.Sigmoid).then_inc(ga_ready, 1)
                act.wait_ge(ga_ready, m + 1)
                act.sem_inc(psum_free[b.slot], 1)
            act.wait_ge(g5_done, 4)
            act.wait_ge(mm_done, last_block("glu"))
            for p in range(NPAIR):
                act.activation(YH[:, p, :], G5[:, p, :], ACT.Copy).then_inc(yh_ready, 1)

        def s5_dve(dve):
            dve.wait_ge(s5_in, 48)
            dve.tensor_copy(D0[:, :, :], R8[:, :].rearrange("p (t k) -> p t k", k=1).broadcast_to([P, NP5, P])).then_inc(
                d0_ready, 1)
            dve.wait_ge(d0_ready, 1)
            dve.memset(D0[:, :, 0:1], 0.0).then_inc(d0_ready, 1)
            for n in range(1, 8, 2):
                dve.wait_ge(ut, n + 1)
                dve.tensor_copy(U5[:, 4 * n:4 * n + 4, :].rearrange("p t n -> p (t n)"), HALF[n]).then_inc(u5_dve, 1)
            c = [0]

            def link(ins):
                c[0] += 1
                ins.then_inc(q_chain, 1)
                dve.wait_ge(q_chain, c[0])

            def phase(ri, b, lo, hi):
                return E5[:, ri, lo:hi, 4 * b:4 * b + 4].rearrange("p c t -> p t c")

            for b in range(4):
                dve.wait_ge(p_ps, b + 1)
                pr, pi = (HALF[2 * b + ri].rearrange("p (t n) -> p t n", t=4) for ri in range(2))
                er, ei = phase(0, b, 1, 129), phase(1, b, 1, 129)
                qr, qi = QZ[:, 0, 4 * b:4 * b + 4, :], QZ[:, 1, 4 * b:4 * b + 4, :]
                dve.tensor_tensor(qr, pr, er, ALU.mult)
                dve.tensor_tensor(F1[:, :, :], pi, ei, ALU.mult)
                dve.tensor_tensor(qi, pi, er, ALU.mult)
                link(dve.tensor_tensor(F2[:, :, :], pr, ei, ALU.mult))
                dve.tensor_tensor(qr, qr, F1[:, :, :], ALU.add)
                link(dve.tensor_tensor(qi, qi, F2[:, :, :], ALU.subtract))
            dve.wait_ge(d0_ready, 2)
            for ri in range(2):
                z = QZ[:, ri].rearrange("p t n -> p (t n)")
                dve.tensor_tensor_scan(z, D0[:, :, :].rearrange("p t n -> p (t n)"), z, 0.0, ALU.mult,
                                       ALU.add).then_inc(z_done, 1)
            dve.wait_ge(z_done, 2)
            for b in range(4):
                if b >= 2:
                    dve.wait_ge(y_ps, b - 1)
                er, ei = phase(0, b, 1, P), phase(1, b, 1, P)
                zr, zi = QZ[:, 0, 4 * b:4 * b + 4, 0:P - 1], QZ[:, 1, 4 * b:4 * b + 4, 0:P - 1]
                sr, si = SV[b % 2][:, 0, :, 1:P], SV[b % 2][:, 1, :, 1:P]
                f1, f2 = F1[:, :, 0:P - 1], F2[:, :, 0:P - 1]
                dve.memset(SV[b % 2][:, :, :, 0:1], 0.0)
                dve.tensor_tensor(sr, zr, er, ALU.mult)
                dve.tensor_tensor(f1, zi, ei, ALU.mult)
                dve.tensor_tensor(si, zi, er, ALU.mult)
                link(dve.tensor_tensor(f2, zr, ei, ALU.mult))
                dve.tensor_tensor(sr, sr, f1, ALU.subtract)
                link(dve.tensor_tensor(si, si, f2, ALU.add))
                dve.sem_inc(sv_ready, 1)
            dve.wait_ge(x5_scaled, 1)
            for b in range(4):
                dve.wait_ge(y_ps, b + 1)
                for g in range(2):
                    x = X5[:, 8 * b + g:8 * b + 8:2].rearrange("p t j c -> p t (j c)")
                    dve.tensor_tensor(x, x, HALF[2 * b + g].rearrange("p (t n) -> p t n", t=4), ALU.add).then_inc(
                        y_ready, 1)
            dve.wait_ge(y_ps, 4)
            for b in range(4):
                dve.wait_ge(yh5_ready, b + 1)
                dve.tensor_tensor(YL5[:, b, :].rearrange("p (s j) -> p j s", j=8),
                                  BANKS[b][:, :].rearrange("p (j s) -> p j s", j=8),
                                  YH5[:, b, :].bitcast(F32).rearrange("p (s j) -> p j s", j=8),
                                  ALU.subtract).then_inc(yl5_ready, 1)
            dve.wait_ge(yl5_ready, 4)
            with dve.Fori(0, 4) as m:
                b = Block("glu", m, 0)
                dve.wait_ge(mm_done, b.n + 1)
                dve.wait_ge(ga_ready, m + 1)
                dve.wait_ge(g5_done, m)
                dve.tensor_tensor(SG[1][:, :], SG[0][:, :], DP[b.slot][:, :], ALU.mult).then_inc(g5_mul, 1)
                dve.wait_ge(g5_mul, m + 1)
                dve.sem_inc(psum_free[b.slot], 1)
                g = G5[:, ds(m, 1), :].rearrange("p a n -> p (a n)")
                dve.tensor_tensor(g, g, SG[1][:, :], ALU.mult).then_inc(g5_done, 1)

        def s5_pool(pool):
            for name in ("s5x", "s5g"):
                with pool.Fori(0, 2) as m:
                    for i in range(2):
                        split(pool, Block(name, m, i))
            pool.wait_ge(s5_in, 48)
            pool.wait_ge(ut, 8)
            pool.tensor_tensor(X5[:, :, :, :], X5[:, :, :, :],
                               DROW[:, :, :].rearrange("p g (a c) -> p g a c", a=1).broadcast_to([P, 32, 8, 16]),
                               ALU.mult).then_inc(x5_scaled, 1)
            with pool.Fori(0, 4) as m:
                for i in range(2):
                    split(pool, Block("glu", m, i))
            for p in range(NPAIR):
                pool.wait_ge(yh_ready, 8 + p + 1)
                pool.wait_ge(mm_done, last_block("glu"))
                pool.tensor_tensor(YL[:, p, :], G5[:, p, :], YH[:, p, :].bitcast(F32), ALU.subtract).then_inc(
                    yl_ready, 1)

        LC = at("LC", S0, [P, T])
        LCH, LCL = at("LCH", S0 + 4, [P, 1, T], F32R), at("LCL", S0 + 8, [P, 1, T], F32R)
        LR, LI, LA, LD, LG = (at(n, S0 + 12 + 4 * i, [P, T]) for i, n in enumerate(("LR", "LI", "LA", "LD", "LG")))
        LH, LL = at("LH", S0 + 32, [P, 2, T], F32R), at("LL", S0 + 40, [P, 2, T], F32R)
        ZL = at("ZL", 64, [P, KD, T])
        SP4, SPA, SPB = at("SP4", 153.5, [P, 10]), at("SPA", 153.625, [P, 10]), at("SPB", 153.75, [P, 10])
        sp_act, sp4_ready, zl_zero = sem("sp_act"), sem("sp4_ready"), sem("zl_zero")
        lc_mid, lc_conv, lc_ready, lch_ready, lcl_ready, lr_ready, li_ready, lt_ready, l_dve, lm2_ready, lroot = (
            sem(n) for n in ("lc_mid", "lc_conv", "lc_ready", "lch_ready", "lcl_ready", "lr_ready", "li_ready",
                             "lt_ready", "l_dve", "lm2_ready", "lroot"))
        lic_ready, lin_ready, lscan, lg_ready, lhb_ready, lh_ready, ll_ready = (sem(n) for n in (
            "lic_ready", "lin_ready", "lscan", "lg_ready", "lhb_ready", "lh_ready", "ll_ready"))

        LRU_AT = {"x0": 0, "gate0": 1, "down0": 2, "ai0": 3, "x1": 4, "down1": 5, "ai1": 6, "gate1": 7}
        LRU_AT0 = {"x0": 0, "gate0": 1, "ai0": 2, "x1": 3, "ai1": 4, "gate1": 5}
        GROUP0 = FT

        def lru_block(it, what):
            return Block("lru0", 0, LRU_AT0[what]) if it is None else Block("lru", it, LRU_AT[what])

        def head(it, h):
            return h if it is None else it * 2 + (2 + h)

        def after(e, s, n):
            if not (isinstance(n, int) and n <= 0):
                e.wait_ge(s, n)

        def lru_steps(e, step):
            step(None)
            with e.Fori(0, 4) as it:
                step(it)

        def lru_down(it, i):
            if it is None:
                return Block("lru1", 0, i), GROUP0 + 8 + i
            return Block("lru", it, LRU_AT[f"down{i}"]), it * 2 + (GROUP0 + i)

        def lru_load(sp, a):
            def step(it):
                for h in range(2):
                    n = head(it, h)
                    for what in (("x0", "gate0", "down0", "ai0") if h == 0 else ("x1", "down1", "ai1", "gate1")):
                        if what[:4] != "down":
                            load(sp, lru_block(it, what), a[{"x": "w_lrux", "g": "w_lrug", "a": "w_lruai"}[what[0]]], n)
                        elif it is not None:
                            load(sp, lru_block(it, what), a["w_bl"], it * 2 + h)

            lru_steps(sp, step)
            for i in range(2):
                load(sp, lru_down(None, i)[0], a["w_bl"], 8 + i)

        def lru_pe(pe):
            def down(it, i):
                b, group = lru_down(it, i)
                if i == 0:
                    pe.wait_ge(ll_ready, 10 if it is None else it * 2 + 2)
                pe.wait_ge(li_ready, 10 if it is None else head(it, 0) + i)
                product4(pe, b, group, LH, LL, False)

            def step(it):
                for h in range(2):
                    n = head(it, h)
                    product(pe, lru_block(it, f"x{h}"), XH, XL)
                    if h == 0:
                        product(pe, lru_block(it, "gate0"), XH, XL)
                    if it is not None:
                        down(it, h)
                    b = lru_block(it, f"ai{h}")
                    pe.wait_ge(lch_ready, n + 1)
                    pe.wait_ge(lcl_ready, n + 1)
                    pe.wait_ge(w_split, b.n + 1)
                    pe.wait_ge(psum_free[b.slot], b.loads - 1)
                    if it is not None:
                        pe.wait_ge(part_read, lru_down(it, h)[1] * 4 + 4)
                    after(pe, li_ready, n)
                    product_into(pe, b, DP[b.slot], 0, 1, LCH, LCL)
                    product_into(pe, b, B67, 1, 1, LCH, LCL).then_inc(mm_done, 1)
                product(pe, lru_block(it, "gate1"), XH, XL)

            lru_steps(pe, step)
            for i in range(2):
                down(None, i)

        def lru_act(act):
            lam = COL[:, COLS["lam"]:COLS["lam"] + 10]
            act.activation(SPA[:, :], lam, ACT.Abs).then_inc(sp_act, 1)
            act.wait_ge(sp_act, 1)
            act.activation(SPB[:, :], SPA[:, :], ACT.Exp, scale=-1.0).then_inc(sp_act, 1)
            act.wait_ge(sp_act, 2)
            act.activation(SPA[:, :], SPB[:, :], ACT.Ln, bias=1.0).then_inc(sp_act, 1)
            act.wait_ge(sp_act, 3)
            act.activation(SPB[:, :], lam, ACT.Relu, scale=-1.0).then_inc(sp_act, 1)
            act.wait_ge(sp4_ready, 1)
            act.wait_ge(mm_done, last_block("mixs"))
            act.wait_ge(mx_done, 24)

            def step(it):
                def column(name, h, i=0):
                    return COL[:, ds(head(it, h) + (COLS[name] + i), 1)]

                def x(h):
                    n, b = head(it, h), lru_block(it, f"x{h}")
                    act.wait_ge(mm_done, b.n + 1)
                    after(act, lcl_ready, n)
                    after(act, lic_ready, n)
                    act.activation(LC[:, :], DP[b.slot][:, :], ACT.Identity, scale=column("lruconv", h, 30),
                                   bias=column("convb", h)).then_inc(lc_mid, 1)

                def x_hi(h):
                    n = head(it, h)
                    act.wait_ge(lc_ready, n + 1)
                    if it is not None or h:
                        act.wait_ge(mm_done, ai_before(it, h).n + 1)
                    act.activation(LCH[:, 0, :], LC[:, :], ACT.Copy).then_inc(lch_ready, 1)

                def gate_(h):
                    n, b = head(it, h), lru_block(it, f"gate{h}")
                    act.wait_ge(mm_done, b.n + 1)
                    after(act, ll_ready, n)
                    act.activation(LG[:, :], DP[b.slot][:, :], ACT.Silu).then_inc(lg_ready, 1)
                    act.wait_ge(lg_ready, n + 1)
                    act.sem_inc(psum_free[b.slot], 1)

                def ai(h):
                    n, b = head(it, h), lru_block(it, f"ai{h}")
                    act.wait_ge(mm_done, b.n + 1)
                    after(act, lhb_ready, n)
                    act.activation(LR[:, :], DP[b.slot][:, :], ACT.Sigmoid, bias=column("ba", h)).then_inc(lr_ready, 1)
                    after(act, lscan, n)
                    act.activation(LI[:, :], B67[:, :], ACT.Sigmoid, bias=column("bx", h)).then_inc(li_ready, 1)
                    act.wait_ge(lr_ready, n + 1)
                    act.sem_inc(psum_free[b.slot], 1)
                    act.activation(LR[:, :], LR[:, :], ACT.Tanh, scale=SP4[:, ds(n, 1)]).then_inc(lt_ready, 1)

                def root(h):
                    act.wait_ge(lm2_ready, head(it, h) + 1)
                    act.activation(LR[:, :], LR[:, :], ACT.Sqrt).then_inc(lroot, 1)

                def hi(h):
                    act.wait_ge(lhb_ready, head(it, h) + 1)
                    if it is not None:
                        act.wait_ge(mm_done, lru_down(it, 1)[0].n + 1)
                    act.activation(LH[:, h, :], LG[:, :], ACT.Copy).then_inc(lh_ready, 1)

                x(0)
                x_hi(0)
                gate_(0)
                ai(0)
                x(1)
                root(0)
                x_hi(1)
                hi(0)
                ai(1)
                gate_(1)
                root(1)
                hi(1)

            lru_steps(act, step)

        def ai_before(it, h):
            if h == 1:
                return lru_block(it, "ai0")
            b = Block("lru", it, 0)
            b.n = it * 8 + (Block("lru", 0, 0).n - 2)
            return b

        def lru_dve(dve):
            dve.wait_ge(sp_act, 4)
            dve.tensor_tensor(SPA[:, :], SPA[:, :], SPB[:, :], ALU.add).then_inc(sp_act, 1)
            dve.wait_ge(sp_act, 5)
            dve.tensor_scalar(SP4[:, :], SPA[:, :], 4.0, None, ALU.mult).then_inc(sp4_ready, 1)
            dve.wait_ge(zl_zero, 1)

            def step(it):
                def conv(h):
                    n, b = head(it, h), lru_block(it, f"x{h}")
                    dve.wait_ge(lc_mid, n + 1)
                    for i, back in enumerate((1, 2, 3)):
                        dve.scalar_tensor_tensor(out=LC[:, back:T], in0=DP[b.slot][:, 0:T - back],
                                                 scalar=COL[:, ds(n + (COLS["lruconv"] + 10 * (3 - back)), 1)],
                                                 in1=LC[:, back:T], op0=ALU.mult, op1=ALU.add).then_inc(lc_conv, 1)
                        dve.wait_ge(lc_conv, n * 3 + (i + 1))
                    dve.sem_inc(psum_free[b.slot], 1)
                    dve.sem_inc(lc_ready, 1)

                def decay(h):
                    n = head(it, h)
                    dve.wait_ge(lt_ready, n + 1)
                    steps = [
                        lambda: dve.tensor_scalar(LD[:, :], LR[:, :], 1.0, None, ALU.add),
                        lambda: dve.reciprocal(LD[:, :], LD[:, :]),
                        lambda: dve.tensor_scalar(LA[:, :], LR[:, :], -1.0, 1.0, ALU.mult, ALU.add),
                        lambda: dve.tensor_tensor(LA[:, :], LA[:, :], LD[:, :], ALU.mult),
                        lambda: dve.scalar_tensor_tensor(out=LR[:, :], in0=LR[:, :], scalar=2.0, in1=LD[:, :],
                                                         op0=ALU.mult, op1=ALU.mult),
                    ]
                    for i, s in enumerate(steps):
                        s().then_inc(l_dve, 1)
                        dve.wait_ge(l_dve, n * 5 + (i + 1))
                    dve.scalar_tensor_tensor(out=LR[:, :], in0=LA[:, :], scalar=1.0, in1=LR[:, :], op0=ALU.add,
                                             op1=ALU.mult).then_inc(lm2_ready, 1)

                def scan(h):
                    n = head(it, h)
                    dve.wait_ge(lroot, n + 1)
                    dve.wait_ge(lic_ready, n + 1)
                    dve.tensor_tensor(LI[:, :], LI[:, :], LR[:, :], ALU.mult).then_inc(lin_ready, 1)
                    dve.wait_ge(lin_ready, n + 1)
                    dve.tensor_tensor_scan(LR[:, :], LA[:, :], LI[:, :], 0.0, ALU.mult, ALU.add).then_inc(lscan, 1)
                    dve.wait_ge(lscan, n + 1)
                    dve.wait_ge(lg_ready, n + 1)
                    dve.tensor_tensor(LG[:, :], LG[:, :], LR[:, :], ALU.mult).then_inc(lhb_ready, 1)

                def add(i, outputs):
                    if it is not None:
                        b, group = lru_down(it, i)
                        add4(dve, b, group, ZL, outputs, 4 * i)

                conv(0)
                add(0, range(4))
                decay(0)
                conv(1)
                add(1, (0, 1))
                scan(0)
                add(1, (2, 3))
                decay(1)
                scan(1)

            lru_steps(dve, step)
            for i in range(2):
                b, group = lru_down(None, i)
                add4(dve, b, group, ZL, m0=4 * i)

        def lru_pool(pool):
            pool.wait_ge(mm_done, last_block("mixs"))
            pool.memset(ZL[:, :, :], 0.0).then_inc(zl_zero, 1)

            def lo(n, h):
                pool.wait_ge(lh_ready, n + 1)
                pool.tensor_tensor(LL[:, h, :], LG[:, :], LH[:, h, :].bitcast(F32), ALU.subtract).then_inc(ll_ready, 1)

            def step(it):
                def x_lo(h):
                    pool.wait_ge(lch_ready, head(it, h) + 1)
                    pool.tensor_tensor(LCL[:, 0, :], LC[:, :], LCH[:, 0, :].bitcast(F32),
                                       ALU.subtract).then_inc(lcl_ready, 1)

                def gated(h):
                    pool.wait_ge(li_ready, head(it, h) + 1)
                    pool.tensor_tensor(LI[:, :], LI[:, :], LC[:, :], ALU.mult).then_inc(lic_ready, 1)

                def block(what):
                    if it is not None or what[:4] != "down":
                        split(pool, lru_block(it, what))

                block("x0")
                block("gate0")
                block("down0")
                if it is not None:
                    lo(it * 2 + 1, 1)
                x_lo(0)
                block("ai0")
                block("x1")
                gated(0)
                block("down1")
                block("ai1")
                x_lo(1)
                block("gate1")
                gated(1)
                lo(head(it, 0), 0)

            lru_steps(pool, step)
            lo(9, 1)
            for i in range(2):
                split(pool, lru_down(None, i)[0])

        TO = at("TO", 64, [P, KD, T])
        PR = at("PR", S0 + 20, [P, 2, T])
        PH, PL = at("PH", S0 + 28, [P, 2, T], F32R), at("PL", S0 + 36, [P, 2, T], F32R)
        gl_ready, gl_used, gl_done, to_ready, x3_in, x3_ready = (sem(n) for n in (
            "gl_ready", "gl_used", "gl_done", "to_ready", "x3_in", "x3_ready"))
        p_in, ph_ready, pl_ready, pg_ready, pg_used, out_ready, out_done = (sem(n) for n in (
            "p_in", "ph_ready", "pl_ready", "pg_ready", "pg_used", "out_ready", "out_done"))

        def end_pe(pe):
            plain_pe(pe, "gatel", XH, XL)
            pe.wait_ge(ms_hi, 2 * KD)
            pe.wait_ge(ms_lo, 2 * KD)
            plain_pe(pe, "wout", XH, XL)
            norm_pe(pe, c4)
            pe.wait_ge(xh_ready, c4.nt + KD)
            pe.wait_ge(nt_used, c4.nt + KD)
            pe.wait_ge(ph_ready, 1)
            pe.wait_ge(pl_ready, 1)
            with pe.Fori(0, 8) as m:
                product(pe, Block("ple", m, 0), PH, PL)
                product(pe, Block("ple", m, 1), XH, XL)

        def end_act(act):
            act.wait_ge(mm_done, last_block("lru"))
            act.wait_ge(part_read, 4 * (FT + 10))
            with act.Fori(0, 4) as m:
                for i in range(2):
                    b = Block("gatel", m, i)
                    act.wait_ge(mm_done, b.n + 1)
                    if i == 0:
                        act.wait_ge(gl_done, m * 2)
                    else:
                        act.wait_ge(gl_done, m * 2)
                    act.activation(SG[i][:, :], DP[b.slot][:, :], ACT.Sigmoid).then_inc(gl_ready, 1)
                    act.wait_ge(gl_ready, m * 2 + (i + 1))
                    act.sem_inc(psum_free[b.slot], 1)
            act.wait_ge(gl_done, 8)
            mx_split(act, None, KD, MX, last_block("gatel"))
            with act.Fori(0, 4) as m:
                for i in range(2):
                    b = Block("wout", m, i)
                    act.wait_ge(mm_done, b.n + 1)
                    act.activation(TO[:, ds(m * 2 + i, 1), :].rearrange("p a n -> p (a n)"), DP[b.slot][:, :],
                                   ACT.Copy).then_inc(to_ready, 1)
                    act.wait_ge(to_ready, m * 2 + (i + 1))
                    act.sem_inc(psum_free[b.slot], 1)
            for k in range(KD):
                act.wait_ge(sq_used, c4.sq + k - 1)
                act.activation(SQ[k % 2][:, :], TO[:, k, :], ACT.Square).then_inc(sq_ready, 1)
            act.wait_ge(sq_used, c4.sq + KD)
            act.activation(RS[:, :], B67[:, :], ACT.Sqrt, scale=1.0 / D, bias=EPS).then_inc(rs_sqrt, 1)
            act.wait_ge(p_in, 16)
            act.activation(PH[:, :, :], PR[:, :, :], ACT.Copy).then_inc(ph_ready, 1)
            for k in range(KD):
                act.wait_ge(x3_ready, k + 1)
                act.activation(XH[:, k, :], MX[:, k, :], ACT.Copy).then_inc(xh_ready, 1)
            with act.Fori(0, 8) as m:
                b = Block("ple", m, 1)
                act.wait_ge(mm_done, b.n + 1)
                act.wait_ge(pg_used, m)
                act.activation(SG[0][:, :], DP[b.slot][:, :], ACT.Sigmoid).then_inc(pg_ready, 1)
                act.wait_ge(pg_ready, m + 1)
                act.sem_inc(psum_free[b.slot], 1)

        def end_dve(dve):
            with dve.Fori(0, 4) as m:
                for i in range(2):
                    n = m * 2 + i
                    dve.wait_ge(gl_ready, m * 2 + (i + 1))
                    zl = ZL[:, ds(n, 1), :].rearrange("p a n -> p (a n)")
                    mx = MX[:, ds(n, 1), :].rearrange("p a n -> p (a n)")
                    dve.tensor_tensor(SG[i][:, :], SG[i][:, :], zl, ALU.mult).then_inc(gl_used, 1)
                    dve.wait_ge(gl_used, m * 2 + (i + 1))
                    dve.tensor_tensor(mx, mx, SG[i][:, :], ALU.add).then_inc(gl_done, 1)
            dve.wait_ge(rs_sqrt, c4.ss + 1)
            dve.reciprocal(RS[:, :], RS[:, :]).then_inc(rs_ready, 1)
            dve.wait_ge(rs_ready, c4.ss + 1)
            dve.wait_ge(x3_in, 16)
            for k in range(KD):
                if k >= 2:
                    dve.wait_ge(x3_ready, k - 1)
                dve.scalar_tensor_tensor(out=NTL[k % 2][:, :], in0=TO[:, k, :], scalar=col("gpost", k),
                                         in1=RS[:, :], op0=ALU.mult, op1=ALU.mult).then_inc(nt_ready, 1)
                dve.wait_ge(nt_ready, c4.nt + k + 1)
                dve.tensor_tensor(MX[:, k, :], MX[:, k, :], NTL[k % 2][:, :], ALU.add).then_inc(x3_ready, 1)
            dve.wait_ge(sq_used, c4.sq + KD)
            with dve.Fori(0, 8) as m:
                b = Block("ple", m, 0)
                dve.wait_ge(mm_done, b.n + 1)
                dve.wait_ge(pg_ready, m + 1)
                dve.wait_ge(out_ready, m)
                dve.wait_ge(nt_used, c4.nt + KD)
                dve.tensor_tensor(SG[1][:, :], SG[0][:, :], DP[b.slot][:, :], ALU.mult).then_inc(pg_used, 1)
                dve.wait_ge(pg_used, m + 1)
                dve.sem_inc(psum_free[b.slot], 1)
                o = MX[:, ds(m, 1), :].rearrange("p a n -> p (a n)")
                dve.tensor_tensor(o, o, SG[1][:, :], ALU.add).then_inc(out_ready, 1)

        def end_pool(pool):
            with pool.Fori(0, 4) as m:
                for i in range(2):
                    split(pool, Block("gatel", m, i))
            mx_split(None, pool, KD, MX, None)
            with pool.Fori(0, 4) as m:
                for i in range(2):
                    split(pool, Block("wout", m, i))
            pool.wait_ge(ph_ready, 1)
            pool.tensor_tensor(PL[:, :, :], PR[:, :, :], PH[:, :, :].bitcast(F32), ALU.subtract).then_inc(pl_ready, 1)
            for k in range(KD):
                pool.wait_ge(xh_ready, c4.nt + k + 1)
                pool.tensor_tensor(XL[:, k, :], MX[:, k, :], XH[:, k, :].bitcast(F32), ALU.subtract).then_inc(
                    nt_used, 1)
            with pool.Fori(0, 8) as m:
                split(pool, Block("ple", m, 0))
                split(pool, Block("ple", m, 1))

        with nc.Block() as block:
            @block.sync
            def _(sp):
                s5_sp(sp)
                for name, w in (("s5x", "w_s5x"), ("s5g", "w_s5g")):
                    with sp.Fori(0, 2) as m:
                        for i in range(2):
                            load(sp, Block(name, m, i), a[w])
                s5_sp_stream(sp)
                with sp.Fori(0, 4) as m:
                    load(sp, Block("glu", m, 0), a["w_glua"], m)
                    load(sp, Block("glu", m, 1), a["w_glub"], m)
                with sp.Fori(0, 8) as m:
                    load(sp, Block("mixs", m, 0), a["w_gates"], m)
                    load(sp, Block("mixs", m, 1), a["w_bs"], m)
                lru_load(sp, a)
                for name, w in (("gatel", "w_gatel"), ("wout", "w_out")):
                    with sp.Fori(0, 4) as m:
                        for i in range(2):
                            load(sp, Block(name, m, i), a[w])
                    if name == "gatel":
                        sp.wait_ge(gl_done, 8)
                sp.wait_ge(ms_lo, 2 * KD)
                sp.wait_ge(ms_hi, 2 * KD)
                sp.dma_start(MX[:, :, :], x2_dram).then_inc(x3_in, 16)
                sp.dma_start(PR[:, :, :], a["p"]).then_inc(p_in, 16)
                with sp.Fori(0, 8) as m:
                    load(sp, Block("ple", m, 0), a["w_ple"], m)
                    load(sp, Block("ple", m, 1), a["w_pleg"], m)
                sp.wait_ge(out_ready, 8)
                sp.dma_start(out, MX[:, :, :]).then_inc(out_done, 16)
                sp.wait_ge(out_done, 16)

            @block.gpsimd
            def _(pool):
                norm_pool(pool, c3)
                s5_pool(pool)
                with pool.Fori(0, 8) as m:
                    split(pool, Block("mixs", m, 0))
                    split(pool, Block("mixs", m, 1))
                lru_pool(pool)
                end_pool(pool)

            @block.scalar
            def _(act):
                norm_act(act, c3, XR)
                s5_act(act)
                mix_act(act, "mixs", 16)
                lru_act(act)
                end_act(act)

            @block.vector
            def _(dve):
                norm_dve(dve, c3, XR, "gpre")
                s5_dve(dve)
                dve.wait_ge(yh_ready, 12)
                mix_dve(dve, "mixs", 16, False, True)
                lru_dve(dve)
                end_dve(dve)

            @block.tensor
            def _(pe):
                norm_pe(pe, c3)
                pe.wait_ge(xh_ready, c3.nt + KD)
                pe.wait_ge(nt_used, c3.nt + KD)
                s5_pe(pe)
                pe.wait_ge(yh_ready, 12)
                pe.wait_ge(yl_ready, 12)
                mix_pe(pe, "mixs")
                lru_pe(pe)
                end_pe(pe)



def blocks(w, cols=None):
    k, n = w.shape
    return np.ascontiguousarray(w.reshape(k // P, P, n // P, P).transpose(2, 1, 0, 3)).reshape(n // P, P, k)


def columns(v):
    return np.ascontiguousarray(np.asarray(v).reshape(-1, P).T)


def pack(i):
    w_in = i["w_in"][0]
    arrays = {}
    cst, bias, levels, sel = constants()
    arrays.update(cst=cst, bias=bias, levels=levels, sel=sel)
    arrays["x"] = np.ascontiguousarray(i["x"][0].T.reshape(KD, P, T).transpose(1, 0, 2))
    qb, kb, vb = 2080, 2080 + 1536, 2080 + 3072
    ga, gb = 2080 + 4608, 2080 + 4608 + 1024
    arrays["w_attn"] = blocks(np.concatenate(
        [w_in[:, o + 512 * g + 128 * p:o + 512 * g + 128 * p + 128]
         for p in range(NPAIR) for g in range(NG) for o in (qb, kb, vb)], 1))
    arrays["w_gateb"], arrays["w_gatea"] = blocks(w_in[:, gb:gb + D]), blocks(w_in[:, ga:ga + D])
    arrays["w_attnout"], arrays["w_dnout"] = blocks(i["w_attn_out"][0]), blocks(i["w_dn_out"][0])
    arrays["w_o"] = blocks(i["w_o"][0])
    up, down, dff = i["w_ffn_up"][0], i["w_ffn_down"][0], FT * P
    arrays["w_up"] = blocks(np.concatenate(
        [up[:, dff * part + P * t:dff * part + P * t + P] for t in range(FT) for part in range(2)], 1))

    def fours(w):
        return np.ascontiguousarray(w.reshape(-1, 2, P, 2, 4, P).transpose(0, 3, 2, 4, 1, 5)).reshape(-1, P, 8 * P)

    arrays["w_down"] = fours(down)
    w2 = i["w_in_2"][0]
    for name, o, n in (("w_s5x", 0, 512), ("w_s5g", 512, 512), ("w_lrux", 1024, 1280), ("w_lrug", 2304, 1280),
                       ("w_gates", 3584, D), ("w_gatel", 4608, D)):
        arrays[name] = blocks(w2[:, o:o + n])
    arrays["w_glua"], arrays["w_glub"] = blocks(i["w_glu_2"][0][:, 0:512]), blocks(i["w_glu_2"][0][:, 512:])
    arrays["w_bs"], arrays["w_out"] = blocks(i["w_bs_2"][0]), blocks(i["w_out_2"][0])
    arrays["w_lruai"] = np.ascontiguousarray(np.concatenate([i["lru_w_a_2"][0], i["lru_w_x_2"][0]], 2))
    arrays["w_bl"] = fours(i["w_bl_2"][0])
    arrays["w_ple"], arrays["w_pleg"] = blocks(i["w_ple_2"][0]), blocks(i["w_ple_gate_2"][0])
    arrays["p"] = np.ascontiguousarray(i["p_2"][0, 0].T.reshape(2, P, T).transpose(1, 0, 2))
    arrays["s5d"] = i["s5_d_2"]

    def states(v):
        v = v.reshape((16, 2, 64) + v.shape[2:])
        return np.moveaxis(v, 0, 2).reshape(P, -1)

    arrays["s5p"] = np.ascontiguousarray(np.concatenate(
        [states(i["s5_a_re_2"][0]), states(i["s5_a_im_2"][0]), states(np.repeat(i["s5_log_dt_2"][0][:, None], 64, 1)),
         states(i["s5_b_re_2"][0]), states(i["s5_b_im_2"][0]),
         states(i["s5_c_re_2"][0].transpose(0, 2, 1)), states(i["s5_c_im_2"][0].transpose(0, 2, 1))], 1))
    ab = np.zeros((D, P), np.float32)
    ab[:, 0:16], ab[:, 32:48] = w_in[:, 2048:2064], w_in[:, 2064:2080]
    arrays["w_ab"] = blocks(ab)
    arrays["w_dn"] = blocks(np.concatenate(
        [w_in[:, 512 * o + 128 * p:512 * o + 128 * p + 128] for p in range(NPAIR) for o in range(4)], 1))
    c = np.zeros((P, NCOLS), np.float32)

    def put(name, v):
        c[:v.shape[0], COLS[name]:COLS[name] + v.shape[1]] = v

    put("norm1", columns(i["norm1_w"]))
    put("norm2", columns(i["norm2_w"]))
    put("gpre", columns(i["g_pre_2"]))
    put("gpost", columns(i["g_post_2"]))
    put("qn", columns(np.tile(i["attn_q_norm_w"][0], 2)))
    put("kn", columns(np.tile(i["attn_k_norm_w"][0], 2)))
    put("dnw", columns(np.tile(i["dn_out_norm_w"][0], 2)))
    put("dtb", i["dn_dt_bias"].reshape(16, 1))
    put("alog", i["dn_a_log"].reshape(16, 1))
    put("lruconv", columns(i["conv_w_2"]))
    for name, key in (("convb", "conv_b_2"), ("ba", "lru_b_a_2"), ("bx", "lru_b_x_2"), ("lam", "lru_lambda_2")):
        put(name, columns(i[key]))
    put("ffnconv", columns(i["ffn_conv_w"]))
    put("dnconv", columns(i["dn_conv_w"]))
    arrays["cols"] = c
    return arrays


def kernel(**inputs):
    import numpy as _np
    import concourse.bacc as _bacc
    from concourse import mybir as _mybir
    from concourse.bass_utils import run_bass_kernel_spmd as _run

    inputs = {k: _np.asarray(v) for k, v in inputs.items()}
    arrays = {f"in_{k}": _np.ascontiguousarray(v) for k, v in pack(inputs).items()}
    nc = _bacc.Bacc("TRN2", target_bir_lowering=False, num_devices=1)
    a = {k[3:]: nc.dram_tensor(k, list(v.shape), _mybir.dt.from_np(v.dtype), kind="ExternalInput").ap()
         for k, v in arrays.items()}
    out = nc.dram_tensor("out", [P, KD, T], _mybir.dt.float32, kind="ExternalOutput").ap()
    program(nc, a, out)
    result = _run(nc, [arrays], core_ids=[0])
    out_t = result.results[0]["out"]
    return _np.ascontiguousarray(out_t.transpose(2, 1, 0)).reshape(1, T, D)
```
